# Optimizing a Trainium2 kernel written in Bass

```python
import math
import jax, jax.numpy as jnp
from jax import lax
import numpy as np

D_MODEL = 1024
BATCH = 1
SEQ = 256
DEPTH = 2

N_MIXERS = 3
NORM_EPS = 1e-6
ROPE_THETA = 500000.0
NEG_INF = -1e30
POS_OFFSET_MAX = 4096
DILATED_PAIRS = ((128, 1), (512, 4), (2048, 16))
A_GROUPS = len(DILATED_PAIRS)
A_HEAD_DIM = 128
A_HEADS = D_MODEL // A_HEAD_DIM
ROT_DIM = A_HEAD_DIM // 4
B_HEAD_DIM = 64
B_HEADS = D_MODEL // B_HEAD_DIM
B_DECAY_LORA = 64
B_ICLR_LORA = 64
B_GATE_LORA = 128
B_N_MU = 8
B_DECAY_SCALE = math.exp(-0.5)
B_GN_EPS = 64e-5
C_HEADS = D_MODEL // 64
C_Q_LORA = 384
C_KV_LORA = 128
C_NOPE = 64
C_ROPE = ROT_DIM
C_V = 64
Q_BLOCK = 128
D_FF = 2816
N_EXPERTS = 8
TOP_K = 2
D_FF_EXPERT = 3584

kernel_name = "hybrid_dilated_rwkv7_mla_moe_encoder"

def _count_layers(m, period):
    return (DEPTH - m + period - 1) // period

def rms_norm(x, g, eps=NORM_EPS):
    xf = x.astype(jnp.float32)
    y = xf * lax.rsqrt(jnp.mean(xf * xf, axis=-1, keepdims=True) + eps)
    return (y * g.astype(jnp.float32)).astype(x.dtype)

def rope_tables(positions, rot):
    inv_freq = ROPE_THETA ** (-jnp.arange(0, rot, 2, dtype=jnp.float32) / rot)
    ang = positions.astype(jnp.float32)[..., None] * inv_freq
    return jnp.cos(ang), jnp.sin(ang)

def apply_rope(x, cos, sin):
    half = cos.shape[-1]
    bshape = cos.shape[:2] + (1,) * (x.ndim - 3) + (half,)
    c = cos.reshape(bshape)
    s = sin.reshape(bshape)
    xr = x[..., :2 * half].astype(jnp.float32)
    x1, x2 = xr[..., :half], xr[..., half:]
    rot = jnp.concatenate([x1 * c - x2 * s, x2 * c + x1 * s], axis=-1).astype(x.dtype)
    return jnp.concatenate([rot, x[..., 2 * half:]], axis=-1)

def swiglu(h, w13, w2):
    gate, up = jnp.split(h @ w13, 2, axis=-1)
    return (jax.nn.silu(gate) * up) @ w2

def banded_attention(q, k, v, half):
    lead = q.shape[:-2]
    L, hd = q.shape[-2:]
    blk = half
    nb = -(-L // blk)
    lp = nb * blk
    nl = len(lead)
    qb = jnp.pad(q.astype(jnp.float32), [(0, 0)] * nl + [(0, lp - L), (0, 0)]).reshape(lead + (nb, blk, hd))

    def windows(t):
        tb = jnp.pad(t.astype(jnp.float32), [(0, 0)] * nl + [(blk, lp - L + blk), (0, 0)])
        tb = tb.reshape(lead + (nb + 2, blk, hd))
        return jnp.concatenate([tb[..., 0:nb, :, :], tb[..., 1:nb + 1, :, :], tb[..., 2:nb + 2, :, :]], axis=-2)

    kw = windows(k)
    vw = windows(v)
    qi = np.arange(nb)[:, None, None] * blk + np.arange(blk)[None, :, None]
    kj = (np.arange(nb)[:, None, None] - 1) * blk + np.arange(3 * blk)[None, None, :]
    mask = (np.abs(qi - kj) <= half) & (kj >= 0) & (kj < L)
    s = jnp.einsum('...nqd,...nkd->...nqk', qb, kw) * (hd ** -0.5)
    s = jnp.where(mask, s, NEG_INF)
    m = jnp.max(s, axis=-1, keepdims=True)
    p = jnp.exp(s - m)
    l = jnp.sum(p, axis=-1, keepdims=True)
    o = jnp.einsum('...nqk,...nkd->...nqd', p, vw) / l
    lse = (m + jnp.log(l))[..., 0]
    o = o.reshape(lead + (lp, hd))[..., :L, :]
    lse = lse.reshape(lead + (lp,))[..., :L]
    return o, lse

def dilated_attention(h, wqkv, qk_norm, wo, cos, sin):
    B, S, _ = h.shape
    qkv = (h @ wqkv).reshape(B, S, 3, A_GROUPS, A_HEADS, A_HEAD_DIM)
    q = apply_rope(rms_norm(qkv[:, :, 0], qk_norm[0][:, None, :]), cos, sin)
    k = apply_rope(rms_norm(qkv[:, :, 1], qk_norm[1][:, None, :]), cos, sin)
    v = qkv[:, :, 2]
    outs, lses = [], []
    for g, (window, dil) in enumerate(DILATED_PAIRS):
        half = window // (2 * dil)
        L = S // dil

        def to_sub(t):
            return t[:, :, g].reshape(B, L, dil, A_HEADS, A_HEAD_DIM).transpose(0, 2, 3, 1, 4)

        o, lse = banded_attention(to_sub(q), to_sub(k), to_sub(v), half)
        outs.append(o.transpose(0, 3, 1, 2, 4).reshape(B, S, A_HEADS, A_HEAD_DIM))
        lses.append(lse.transpose(0, 3, 1, 2).reshape(B, S, A_HEADS))
    alpha = jax.nn.softmax(jnp.stack(lses), axis=0)
    o = jnp.einsum('gbsh,gbshd->bshd', alpha, jnp.stack(outs))
    return o.reshape(B, S, A_HEADS * A_HEAD_DIM).astype(h.dtype) @ wo

def wkv_scan(r, w, k, v, a, b, reverse):
    B, S, H, N = r.shape

    def step(state, inp):
        r_t, w_t, k_t, v_t, a_t, b_t = inp
        sa = jnp.einsum('bhvk,bhk->bhv', state, a_t)
        state = state * w_t[:, :, None, :] + sa[..., None] * b_t[:, :, None, :] + v_t[..., None] * k_t[:, :, None, :]
        return state, jnp.einsum('bhvk,bhk->bhv', state, r_t)

    xs = tuple(jnp.moveaxis(t, 1, 0) for t in (r, w, k, v, a, b))
    _, ys = lax.scan(step, jnp.zeros((B, H, N, N), jnp.float32), xs, reverse=reverse)
    return jnp.moveaxis(ys, 0, 1)

def _heads(t):
    return t.reshape(t.shape[:-1] + (B_HEADS, B_HEAD_DIM))

def rwkv7_bidirectional(h, mu, w_rkv, w0, w1, w2, a0, a1, a2, g1, g2, k_k, k_a, r_k, ln_x, wo):
    B, S, D = h.shape
    f32 = jnp.float32
    zero = jnp.zeros_like(h[:, :1])
    d_f = jnp.concatenate([zero, h[:, :-1]], axis=1) - h
    d_b = jnp.concatenate([h[:, 1:], zero], axis=1) - h
    d_c = 0.5 * (d_f + d_b)
    shared = h[None] + d_c[None] * mu[:4, None, None, :]
    r, k, v = jnp.einsum('nbsd,nde->nbse', shared[:3], w_rkv)
    g = jax.nn.sigmoid(shared[3] @ g1) @ g2
    dirs = jnp.stack([d_f, d_b])
    x_w = h[None] + dirs * mu[4:6, None, None, :]
    x_a = h[None] + dirs * mu[6:8, None, None, :]
    z = w0[:, None, None, :] + jnp.einsum('nbsr,nrd->nbsd', jnp.tanh(jnp.einsum('nbsd,ndr->nbsr', x_w, w1)), w2)
    decay = _heads(jnp.exp(-B_DECAY_SCALE * jax.nn.sigmoid(z.astype(f32))))
    a = _heads(jax.nn.sigmoid((a0[:, None, None, :] + jnp.einsum('nbsr,nrd->nbsd', jnp.einsum('nbsd,ndr->nbsr', x_a, a1), a2)).astype(f32)))
    rf = _heads(r.astype(f32))
    kf = _heads(k.astype(f32))
    vf = _heads(v.astype(f32))
    kk = kf * _heads(k_k.astype(f32))
    kk = kk / jnp.maximum(jnp.sqrt(jnp.sum(kk * kk, axis=-1, keepdims=True)), 1e-12)
    k_dir = kf[None] * (1.0 + (a - 1.0) * _heads(k_a.astype(f32)))
    y_f = wkv_scan(rf, decay[0], k_dir[0], vf, -kk, kk * a[0], reverse=False)
    y_b = wkv_scan(rf, decay[1], k_dir[1], vf, -kk, kk * a[1], reverse=True)
    y = y_f + y_b
    mean = jnp.mean(y, axis=-1, keepdims=True)
    var = jnp.mean(jnp.square(y - mean), axis=-1, keepdims=True)
    y = ((y - mean) * lax.rsqrt(var + B_GN_EPS)).reshape(B, S, D) * ln_x[0].astype(f32) + ln_x[1].astype(f32)
    bonus = jnp.sum(rf[None] * k_dir * _heads(r_k.astype(f32)), axis=(0, -1))[..., None] * vf
    out = (y + bonus.reshape(B, S, D)) * g.astype(f32)
    return out.astype(h.dtype) @ wo

def dense_attention(q, k, v):
    B, S, H, dk = q.shape
    nb = S // Q_BLOCK
    scale = dk ** -0.5
    qb = q.astype(jnp.float32).reshape(B, nb, Q_BLOCK, H, dk).transpose(1, 0, 3, 2, 4)
    kt = k.astype(jnp.float32).transpose(0, 2, 1, 3)
    vt = v.astype(jnp.float32).transpose(0, 2, 1, 3)

    def block(qblk):
        p = jax.nn.softmax(jnp.einsum('bhqd,bhkd->bhqk', qblk, kt) * scale, axis=-1)
        return jnp.einsum('bhqk,bhkd->bhqd', p, vt)

    o = lax.map(block, qb)
    return o.transpose(1, 0, 3, 2, 4).reshape(B, S, H, v.shape[-1])

def mla(h, wa, qa_norm, kva_norm, wq_b, wkv_b, qk_norm, wo, cos, sin):
    B, S, _ = h.shape
    lat = h @ wa
    q_lat, kv_lat, k_rope = jnp.split(lat, [C_Q_LORA, C_Q_LORA + C_KV_LORA], axis=-1)
    q = (rms_norm(q_lat, qa_norm) @ wq_b).reshape(B, S, C_HEADS, C_ROPE + C_NOPE)
    kv = (rms_norm(kv_lat, kva_norm) @ wkv_b).reshape(B, S, C_HEADS, C_NOPE + C_V)
    k_nope, v = kv[..., :C_NOPE], kv[..., C_NOPE:]
    k = jnp.concatenate([jnp.broadcast_to(k_rope[:, :, None, :], (B, S, C_HEADS, C_ROPE)), k_nope], axis=-1)
    q = apply_rope(rms_norm(q, qk_norm[0]), cos, sin)
    k = apply_rope(rms_norm(k, qk_norm[1]), cos, sin)
    o = dense_attention(q, k, v)
    return o.reshape(B, S, C_HEADS * C_V).astype(h.dtype) @ wo

def moe_swiglu(h, router, w13, w2):
    B, S, D = h.shape
    t = h.reshape(B * S, D)
    logits = (t @ router).astype(jnp.float32)
    top_val, top_idx = lax.top_k(logits, TOP_K)
    gate = jax.nn.softmax(top_val, axis=-1)
    combine = jnp.einsum('tk,tke->te', gate, jax.nn.one_hot(top_idx, N_EXPERTS, dtype=jnp.float32))
    out = jnp.zeros_like(t)
    for e in range(N_EXPERTS):
        out = out + combine[:, e:e + 1].astype(t.dtype) * swiglu(t, w13[e], w2[e])
    return out.reshape(B, S, D)

def setup_inputs(seed: int = 0) -> dict:
    key = jax.random.key(seed)
    keys = iter(jax.random.split(key, 64))
    f32 = jnp.float32
    D = D_MODEL

    def nrm(shape, scale):
        return jax.random.normal(next(keys), shape, f32) * scale

    def gain(shape):
        return 1.0 + nrm(shape, 0.02)

    n_a = _count_layers(0, N_MIXERS)
    n_b = _count_layers(1, N_MIXERS)
    n_c = _count_layers(2, N_MIXERS)
    n_dense = _count_layers(0, 2)
    n_moe = _count_layers(1, 2)
    a_width = A_GROUPS * A_HEADS * A_HEAD_DIM
    x = nrm((BATCH, SEQ, D), 1.0)
    positions = jnp.arange(SEQ, dtype=jnp.int32)[None, :] + jax.random.randint(next(keys), (BATCH, 1), 0, POS_OFFSET_MAX, dtype=jnp.int32)
    return {
        "x": x,
        "positions": positions,
        "ln_mix": gain((DEPTH, D)),
        "ln_ffn": gain((DEPTH, D)),
        "a_wqkv": nrm((n_a, D, 3 * a_width), D ** -0.5),
        "a_qk_norm": gain((n_a, 2, A_GROUPS, A_HEAD_DIM)),
        "a_wo": nrm((n_a, A_HEADS * A_HEAD_DIM, D), (A_HEADS * A_HEAD_DIM) ** -0.5),
        "b_mu": jax.random.uniform(next(keys), (n_b, B_N_MU, D), f32),
        "b_wrkv": nrm((n_b, 3, D, D), D ** -0.5),
        "b_w0": nrm((n_b, 2, D), 1.0),
        "b_w1": nrm((n_b, 2, D, B_DECAY_LORA), D ** -0.5),
        "b_w2": nrm((n_b, 2, B_DECAY_LORA, D), B_DECAY_LORA ** -0.5),
        "b_a0": nrm((n_b, 2, D), 0.5),
        "b_a1": nrm((n_b, 2, D, B_ICLR_LORA), D ** -0.5),
        "b_a2": nrm((n_b, 2, B_ICLR_LORA, D), 0.5 * B_ICLR_LORA ** -0.5),
        "b_g1": nrm((n_b, D, B_GATE_LORA), D ** -0.5),
        "b_g2": nrm((n_b, B_GATE_LORA, D), B_GATE_LORA ** -0.5),
        "b_kk": 0.85 + nrm((n_b, D), 0.05),
        "b_ka": 1.0 + nrm((n_b, D), 0.05),
        "b_rk": nrm((n_b, D), 0.1),
        "b_lnx": jnp.stack([gain((n_b, D)), nrm((n_b, D), 0.02)], axis=1),
        "b_wo": nrm((n_b, D, D), D ** -0.5),
        "c_wa": nrm((n_c, D, C_Q_LORA + C_KV_LORA + C_ROPE), D ** -0.5),
        "c_qa_norm": gain((n_c, C_Q_LORA)),
        "c_kva_norm": gain((n_c, C_KV_LORA)),
        "c_wq_b": nrm((n_c, C_Q_LORA, C_HEADS * (C_ROPE + C_NOPE)), C_Q_LORA ** -0.5),
        "c_wkv_b": nrm((n_c, C_KV_LORA, C_HEADS * (C_NOPE + C_V)), C_KV_LORA ** -0.5),
        "c_qk_norm": gain((n_c, 2, C_ROPE + C_NOPE)),
        "c_wo": nrm((n_c, C_HEADS * C_V, D), (C_HEADS * C_V) ** -0.5),
        "f_w13": nrm((n_dense, D, 2 * D_FF), D ** -0.5),
        "f_w2": nrm((n_dense, D_FF, D), D_FF ** -0.5),
        "m_router": nrm((n_moe, D, N_EXPERTS), D ** -0.5),
        "m_w13": nrm((n_moe, N_EXPERTS, D, 2 * D_FF_EXPERT), D ** -0.5),
        "m_w2": nrm((n_moe, N_EXPERTS, D_FF_EXPERT, D), D_FF_EXPERT ** -0.5),
    }

def reference(x, positions, ln_mix, ln_ffn, a_wqkv, a_qk_norm, a_wo, b_mu, b_wrkv, b_w0, b_w1, b_w2, b_a0, b_a1, b_a2, b_g1, b_g2, b_kk, b_ka, b_rk, b_lnx, b_wo, c_wa, c_qa_norm, c_kva_norm, c_wq_b, c_wkv_b, c_qk_norm, c_wo, f_w13, f_w2, m_router, m_w13, m_w2):
    cos, sin = rope_tables(positions, ROT_DIM)
    for i in range(DEPTH):
        j = i // N_MIXERS
        kind = i % N_MIXERS
        h = rms_norm(x, ln_mix[i])
        if kind == 0:
            y = dilated_attention(h, a_wqkv[j], a_qk_norm[j], a_wo[j], cos, sin)
        elif kind == 1:
            y = rwkv7_bidirectional(h, b_mu[j], b_wrkv[j], b_w0[j], b_w1[j], b_w2[j], b_a0[j], b_a1[j], b_a2[j], b_g1[j], b_g2[j], b_kk[j], b_ka[j], b_rk[j], b_lnx[j], b_wo[j])
        else:
            y = mla(h, c_wa[j], c_qa_norm[j], c_kva_norm[j], c_wq_b[j], c_wkv_b[j], c_qk_norm[j], c_wo[j], cos, sin)
        x = x + y
        h = rms_norm(x, ln_ffn[i])
        f = i // 2
        if i % 2 == 0:
            x = x + swiglu(h, f_w13[f], f_w2[f])
        else:
            x = x + moe_swiglu(h, m_router[f], m_w13[f], m_w2[f])
    return x


_drawn_inputs = setup_inputs


def setup_inputs(seed=0):
    import zlib

    import numpy as np

    out = dict(_drawn_inputs(seed))
    spreads = {}
    factors = {}
    for name, (base, spread) in spreads.items():
        noise = np.random.default_rng([zlib.crc32(name.encode()), seed]).standard_normal(out[name].shape)
        drawn = base * np.exp(spread * noise) if base else spread * noise
        out[name] = __import__('jax').numpy.asarray(drawn.astype(out[name].dtype))
    for name, factor in factors.items():
        out[name] = (out[name] * factor).astype(out[name].dtype)
    return out
```

```python
import math
from contextlib import ExitStack, contextmanager

import numpy as np

import concourse.bass as bass
from concourse import mybir

F32 = mybir.dt.float32
I32 = mybir.dt.int32
ALU = mybir.AluOpType
ACT = mybir.ActivationFunctionType
AX = mybir.AxisListType.X

P = 128
D = 1024
S = 256
T = S // P
KB = D // P
EPS = 1e-6
NEG = -1e30
GROUPS = 3
HEAD = 128
ROT = 32
HG = 2
FF = 2816
FFE = 3584
EXPERTS = 8
RH = 64
RQ = 256
NQ = D // RQ
RHD = D // RH
LORA = 64
GN_EPS = 64e-5
DECAY = math.exp(-0.5)
BLK = 16

SLOT = 4096
R = 6
U_QKV = 18
U_AWO = 2
U_FF = 17
U_RKV = 6
U_BWO = 2
U_DENSE = U_QKV + U_AWO + U_FF + U_RKV + U_BWO
U_EXPERT = 21

C_ID = 0
C_FREQ = C_ID + P
C_TRI = C_FREQ + 16
C_TIE = C_TRI + 8 * P
C_HALF = C_TIE + 64
C_CEN = C_HALF + 2
C_ALL = C_CEN + 4 * P
U16, UOFF, L16, LOFF, UI, US, LI, LS = range(8)


def constants():
    c = np.zeros((P, C_ALL), np.float32)
    mask = np.zeros((P, T * 512), np.float32)
    c[:, C_ID:C_ID + P] = np.eye(P)
    where = np.arange(S)
    token = (where % 16) * 16 + where // 64 + 4 * ((where // 16) % 4)
    for t in range(T):
        own = token[t * P:(t + 1) * P]
        near = np.abs(own[:, None] - token[None, :]) <= 64
        four = (own[:, None] - own[None, :]) % 4 == 0
        sixteen = (own[:, None] - own[None, :]) % 16 == 0
        mask[:, t * 512:(t + 1) * 512] = np.where(np.concatenate([near, four, sixteen], 1), 0.0, NEG)
    c[:, C_FREQ:C_FREQ + 16] = (np.float32(500000.0) ** (-np.arange(0, ROT, 2, dtype=np.float32) / np.float32(ROT)))[None]
    i = np.arange(P)
    r, q = i[:, None], i[None, :]
    same = r // BLK == q // BLK
    for n, m in enumerate([(r < q) & same, (r < q) & ~same, (r > q) & same, (r > q) & ~same, r <= q, r < q, r >= q, r > q]):
        c[:, C_TRI + n * P:C_TRI + (n + 1) * P] = m
    e = np.arange(8)
    c[:, C_TIE:C_TIE + 64] = (e[None, :] < e[:, None]).reshape(1, 64)
    c[:, C_HALF] = i < P // 2
    c[:, C_HALF + 1] = i >= P // 2
    first, last = (i < P // 2)[:, None].astype(np.float32), (i >= P // 2)[:, None].astype(np.float32)
    for n, m in enumerate([(r <= q) - first, (r < q) - first, (r >= q) - last, (r > q) - last]):
        c[:, C_CEN + n * P:C_CEN + (n + 1) * P] = m
    return c, mask


class Steps:

    def __init__(self, eng, sem):
        self.eng, self.sem, self.n, self.off = eng, sem, 0, 0

    def link(self, ins):
        self.n += 1
        ins.then_inc(self.sem, 1)
        self.eng.wait_ge(self.sem, self.off + self.n)

    @contextmanager
    def repeated(self, i, times, each):
        start, self.off = self.n, i * each
        yield
        assert self.n - start == each, f"links in a turn: {self.n - start}"
        self.n, self.off = start + each * times, 0


def ff_plan(groups, first):
    order, u = [], first
    pairs = -(-groups // 2)
    for p in range(pairs):
        for g in range(2 * p, min(2 * p + 2, groups)):
            order.append(("up", g, u)); u += 1
        if p:
            order.append(("down", p - 1, u)); u += 1
    order.append(("down", pairs - 1, u))
    return order


def build(nc, x_in, pos_in, const_in, mask_in, vec_in, rows_in, qk_rows, qk_cols, wqkv, awo, wrkv, w0, w1, w2, a0, a1, a2,
          g1, g2, bwo, fw13, fw2, router, mw13, mw2, out):
    ctx = ExitStack()
    with ctx:
        arena = ctx.enter_context(nc.sbuf_tensor("arena", [P, 53200], F32))
        ps = ctx.enter_context(nc.psum_tensor("ps", [P, 8, 512], F32))

        def sem(name):
            return ctx.enter_context(nc.semaphore(name))

        class Region:

            def __init__(self, at, end):
                self.at, self.end = at, end

            def take(self, *shape, parts=P):
                n = math.prod(shape)
                v = arena[0:parts, self.at:self.at + n]
                self.at += n
                assert self.at <= self.end, (self.at, self.end)
                if len(shape) > 1:
                    names = "abcd"[:len(shape)]
                    v = v.rearrange(f"p ({' '.join(names)}) -> p {' '.join(names)}",
                                    **{n: s for n, s in zip(names, shape)})
                return v

        fixed = Region(0, 53200)
        ring = [fixed.take(SLOT) for _ in range(R)]
        x = fixed.take(T, D)
        const = fixed.take(C_ALL)
        vec = fixed.take(96)
        qkc = fixed.take(6)
        qkr = fixed.take(6, ROT)
        pos_i = fixed.take(T).bitcast(I32)
        stat = fixed.take(64)
        union = fixed.at

        ident = const[:, C_ID:C_ID + P]

        def tri(n):
            return const[:, C_TRI + n * P:C_TRI + (n + 1) * P]

        m = Region(union, 53200)
        hT = m.take(KB, S)
        qT = m.take(GROUPS, 4, S)
        kT = m.take(GROUPS, 4, S)
        v = m.take(T, GROUPS, 512)
        attn = m.take(T, D)
        oT = m.take(KB, S)
        qn = m.take(2, 4, HEAD)
        sq = m.take(2, 512)
        rope_tmp = m.take(3, 4, ROT)
        probs = m.take(2, 512)
        pT = m.take(2, 4, P)
        cs = m.take(2, T, ROT)
        ang = m.take(4, T, 16)
        amask = m.take(T, 512)
        m = Region(union, 53200)
        assert m.take(KB, S).offset == hT.offset
        hid = m.take(2, 4, S)
        sg = m.take(2, S)
        rw = m.take(KB, EXPERTS)
        logits = m.take(T, EXPERTS)
        comb = m.take(T, EXPERTS)
        cmp_a = m.take(T, EXPERTS, EXPERTS)
        cmp_b = m.take(T, EXPERTS, EXPERTS)
        m = Region(union, 53200)
        rkv = m.take(3, T, D)
        loraT = [m.take(S, parts=LORA + 1) for _ in range(4)]
        sgT = m.take(S)
        after_pre = m.at
        hR = m.take(KB, S)
        d_f = m.take(KB, S)
        d_b = m.take(KB, S)
        d_c = m.take(KB, S)
        mx = m.take(2, KB, S)
        lw1 = m.take(4, KB, LORA)
        lg1 = m.take(KB, P)
        m = Region(after_pre, 53200)
        par_l = m.take(4, RQ, parts=LORA + 1)
        par_g = m.take(RQ)
        rows = m.take(5, RQ)
        mixo = m.take(T, D)
        kkn = m.take(T, RQ)
        y_sum = m.take(T, RQ)
        small = m.take(64)
        lent = Region(3 * SLOT, R * SLOT)

        def stream(m, lent):
            o = {}
            o["E"] = lent.take(T, 2, RQ)
            o["six"] = lent.take(2, 4, P)
            o["gm"] = lent.take(4, 4, P)
            o["sig"] = m.take(T, RQ)
            o["a"] = m.take(T, RQ)
            o["inv"] = lent.take(T, RQ)
            o["kt"] = lent.take(T, RQ)
            o["kd"] = lent.take(T, RQ)
            o["be"] = m.take(RQ)
            o["ke"] = m.take(RQ)
            o["AR"] = m.take(2, 2, P)
            o["BK"] = m.take(4, 2, P)
            o["z"] = [o["sig"][:, 0, :], o["sig"][:, 1, :], o["a"][:, 0, :]]
            o["DT"] = lent.take(4, P)
            for n in ("Mo", "G", "D2T"):
                o[n] = m.take(4, P)
            o["D"], o["D2"] = o["six"][:, 0], o["six"][:, 1]
            o["S0"] = m.take(4, RH)
            o["pm"] = m.take(2)
            return o

        st = [stream(m, lent), stream(m, lent)]
        w_ = st[0]["G"].rearrange("p a b -> p (a b)").rearrange("p (t n) -> p t n", t=T)
        b_ = st[0]["AR"].rearrange("p a b c -> p (a b c)").rearrange("p (t n) -> p t n", t=T)
        m = Region(after_pre + 4 * RQ + RQ + 5 * RQ + T * D, 53200)
        moT = m.take(KB, S)

        slot_full = [sem(f"slot_full{i}") for i in range(R)]
        in_x, in_const, in_small, out_done = sem("in_x"), sem("in_const"), sem("in_small"), sem("out_done")
        dve_step, act_step, pool_step = sem("dve_step"), sem("act_step"), sem("pool_step")
        rms_ss, rms_ms, rms_rt, rms_xn, rms_tp, rms_h = (sem("rms_" + n) for n in ("ss", "ms", "rt", "xn", "tp", "h"))
        tables, qkgain = sem("tables"), sem("qkgain")
        proj_ready, proj_taken = sem("proj_ready"), sem("proj_taken")
        sq_ready, ms_ready, rt_ready, qn_ready, rope_ready = (sem(n) for n in ("sq_ready", "ms_ready", "rt_ready", "qn_ready", "rope_ready"))
        qkT_ps, qkT_sb = sem("qkT_ps"), sem("qkT_sb")
        sc_ps, masked, maxed, prob_rdy, pT_ps, pT_sb, o_ps, o_sb = (sem(n) for n in ("sc_ps", "masked", "maxed", "prob_rdy", "pT_ps", "pT_sb", "o_ps", "o_sb"))
        oT_ps, oT_sb = sem("oT_ps"), sem("oT_sb")
        wo_ps, x_done = sem("wo_ps"), sem("x_done")
        gu_ps, sg_sb, hid_sb, dn_ps, dn_taken = (sem(n) for n in ("gu_ps", "sg_sb", "hid_sb", "dn_ps", "dn_taken"))
        lg_ps, lg_sb, lg_ex, comb_ok = (sem(n) for n in ("lg_ps", "lg_sb", "lg_ex", "comb_ok"))
        in_lora, in_par, d_ready, mix_ready, mix_ps, mix_sb, ones_ok = (sem(n) for n in ("in_lora", "in_par", "d_ready", "mix_ready", "mix_ps", "mix_sb", "ones_ok"))
        rkv_ps, rkv_sb = sem("rkv_ps"), sem("rkv_sb")
        head_done = sem("head_done")
        kk_sq, kk_ss, kk_rt, kk_ok = (sem(n) for n in ("kk_sq", "kk_ss", "kk_rt", "kk_ok"))
        gate_ps, gn_ss, gn_rt = (sem(n) for n in ("gate_ps", "gn_ss", "gn_rt"))

        class Pair:

            def __init__(self, name):
                self.ps, self.sb = sem(name + "_ps"), sem(name + "_sb")

        def turn(c, d, each=1):
            return c * (2 * each) + (d - 1) * each

        STAGES = ["za", "cum", "end", "tA", "tB", "X", "gm", "D2", "D2T", "D4", "D4T", "G2", "D8", "G3", "G4",
                  "E", "ET", "E2", "E2T", "E4T", "z0", "z1", "z2", "z3", "u", "y", "st"]
        stage = {n: Pair(n) for n in STAGES}
        ops_ok = [sem(f"ops_ok{d}") for d in range(2)]
        ke_ok = [sem(f"ke_ok{d}") for d in range(2)]
        g1_ok = [sem(f"g1_ok{d}") for d in range(2)]
        ex_ok = [sem(f"ex_ok{d}") for d in range(2)]
        kd_ok = [sem(f"kd_ok{d}") for d in range(2)]
        in_router = sem("in_router")
        vq_ok, pad_ok = sem("vq_ok"), sem("pad_ok")
        block = ctx.enter_context(nc.Block())

        free = {}
        for u in range(U_QKV):
            free[u] = (proj_ready, 2 * u + 2)
        u0 = U_QKV
        for n in range(U_AWO):
            free[u0 + n] = (wo_ps, 2 * n + 2)
        u0 += U_AWO
        FF0 = u0
        plan0 = ff_plan(FF // 256, FF0)
        for kind, n, u in plan0:
            free[u] = (gu_ps, 2 * n + 2) if kind == "up" else (dn_ps, n + 1)
        u0 += U_FF
        RKV0 = u0
        for n in range(U_RKV):
            free[u0 + n] = (rkv_ps, 2 * n + 2)
        u0 += U_RKV
        BWO0 = u0
        for n in range(U_BWO):
            free[u0 + n] = (wo_ps, 2 * (U_AWO + n) + 2)
        MOE0 = U_DENSE
        GU0, DN0 = 2 * (FF // 256), -(-FF // 512)
        GUE, DNE = 2 * (FFE // 256), FFE // 512

        def arrived(eng, u, rounds=0):
            eng.wait_ge(slot_full[u % R], rounds * 32 + (u // R + 1) * 32)

        def unit(u):
            return ring[u % R]

        free_e = {}
        for e in range(2):
            for kind, n, u in ff_plan(FFE // 256, MOE0 + e * U_EXPERT):
                free_e[u] = (gu_ps, GU0 + e * GUE + 2 * n + 2) if kind == "up" else (dn_ps, DN0 + e * DNE + n + 1)

        def wait_free_e(sp, u, i):
            w = u - R
            if w < MOE0 and isinstance(i, int):
                s, n = free[w]
                sp.wait_ge(s, n)
                return
            back = 0
            if w < MOE0:
                w, back = w + 2 * U_EXPERT, 1
            s, n = free_e[w]
            per = 2 * GUE if s is gu_ps else 2 * DNE
            sp.wait_ge(s, i * per + (n - back * per))

        @block.sync
        def _(sp):
            def halves(u, dst, src):
                for a, b in zip(dst, src):
                    sp.dma_start(a, b).then_inc(slot_full[u % R], 16)

            def square(u, w):
                s = unit(u).rearrange("p (k n) -> p k n", n=512)
                w = w.rearrange("(k p) n -> p k n", p=P)
                halves(u, (s[:, 0:4], s[:, 4:8]), (w[:, 0:4], w[:, 4:8]))

            def ff_unit(kind, u, w13, wd, ff, rows=512):
                if kind == "up":
                    s = unit(u).rearrange("p (k n) -> p k n", n=512)
                    halves(u, (s[:, :, 0:256], s[:, :, 256:512]), w13)
                else:
                    n = rows // P
                    s = unit(u)[:, 0:n * D].rearrange("p (k n) -> p k n", n=D)
                    halves(u, (s[:, 0:n // 2], s[:, n // 2:n]), (wd[:, 0:n // 2], wd[:, n // 2:n]))

            def wait_free(u):
                if u >= R:
                    s, n = free[u - R]
                    sp.wait_ge(s, n)

            sp.dma_start(x, x_in.rearrange("(t p) n -> p t n", p=P)).then_inc(in_x, 16)
            sp.dma_start(const, const_in).then_inc(in_const, 16)
            sp.dma_start(amask.rearrange("p t n -> p (t n)"), mask_in).then_inc(in_small, 16)
            sp.dma_start(vec, vec_in).then_inc(in_small, 16)
            sp.dma_start(qkc, qk_cols).then_inc(in_small, 16)
            sp.dma_start(qkr, qk_rows.partition_broadcast(P)).then_inc(in_small, 16)
            sp.dma_start(pos_i, pos_in).then_inc(in_small, 16)
            for u in range(U_QKV):
                hg, g, kind = u // 9, u % 9 // 3, u % 3
                col = (kind * GROUPS + g) * D + hg * 512
                wait_free(u)
                square(u, wqkv[:, col:col + 512])
            for n in range(U_AWO):
                wait_free(U_QKV + n)
                square(U_QKV + n, awo[:, n * 512:(n + 1) * 512])
            f13 = fw13.rearrange("(k p) n -> p k n", p=P)
            for kind, n, u in plan0:
                wait_free(u)
                c = n * 256
                r0, r1 = n * 512, min(n * 512 + 512, FF)
                if kind == "up":
                    ff_unit(kind, u, (f13[:, :, c:c + 256], f13[:, :, FF + c:FF + c + 256]), None, FF)
                else:
                    ff_unit(kind, u, None, fw2[r0:r1, :].rearrange("(k p) n -> p k n", p=P), FF, r1 - r0)
            sp.wait_ge(x_done, 4)
            for j, w in enumerate((w1[0], w1[1], a1[0], a1[1])):
                sp.dma_start(lw1[:, j], w.rearrange("(k p) n -> p k n", p=P)).then_inc(in_lora, 16)
            sp.dma_start(lg1, g1.rearrange("(k p) n -> p k n", p=P)).then_inc(in_lora, 16)
            for n in range(U_RKV):
                wait_free(RKV0 + n)
                square(RKV0 + n, wrkv[n // 2, :, (n % 2) * 512:(n % 2 + 1) * 512])
            def rest_unit(u):
                if u < MOE0:
                    square(u, bwo[:, (u - BWO0) * 512:(u - BWO0 + 1) * 512])
                else:
                    expert_unit(plan_e[u - MOE0], 0)

            plan_e = []
            for e in range(2):
                plan_e += [(e, *a) for a in ff_plan(FFE // 256, MOE0 + e * U_EXPERT)]

            def expert_unit(item, i):
                e, kind, n, u = item
                w13 = mw13[bass.ds(i * 2 + e, 1)].rearrange("e (k p) n -> p (e k) n", p=P)
                wd = mw2[bass.ds(i * 2 + e, 1)].rearrange("e (k p) n -> p (e k) n", p=P)
                c = n * 256
                if kind == "up":
                    ff_unit(kind, u, (w13[:, :, c:c + 256], w13[:, :, FFE + c:FFE + c + 256]), None, FFE)
                else:
                    ff_unit(kind, u, None, wd[:, 4 * n:4 * n + 4, :], FFE)

            for q in range(NQ):
                if q == 0:
                    sp.wait_ge(rkv_sb, 12)
                else:
                    sp.wait_ge(head_done, q + 1)
                c = q * RQ
                for j, (w, b) in enumerate(((w2[0], w0[0]), (w2[1], w0[1]), (a2[0], a0[0]), (a2[1], a0[1]))):
                    sp.dma_start(par_l[0:LORA, j], w[:, c:c + RQ]).then_inc(in_par, 16)
                    sp.dma_start(par_l[LORA:LORA + 1, j], b[c:c + RQ].unsqueeze(0)).then_inc(in_par, 16)
                sp.dma_start(par_g, g2[:, c:c + RQ]).then_inc(in_par, 16)
                sp.dma_start(rows, rows_in[:, c:c + RQ].partition_broadcast(P)).then_inc(in_par, 16)
            for u in range(BWO0, BWO0 + R):
                if u % R >= 3:
                    sp.wait_ge(head_done, NQ + 1)
                wait_free(u)
                rest_unit(u)
            first = BWO0 + R - MOE0
            for item in plan_e[first:]:
                wait_free_e(sp, item[3], 0)
                expert_unit(item, 0)
            with sp.Fori(1, EXPERTS // 2) as i:
                for item in plan_e:
                    wait_free_e(sp, item[3], i)
                    expert_unit(item, i)
            sp.wait_ge(dn_taken, 4 * EXPERTS + 4)
            sp.dma_start(out.rearrange("(t p) n -> p t n", p=P), x).then_inc(out_done, 16)
            sp.wait_ge(out_done, 16)

        @block.tensor
        def _(pe):
            mm = pe.matmul

            def run(o, pairs, **kw):
                for n, (a, b) in enumerate(pairs):
                    last = mm(o, a, b, start=(n == 0), stop=(n == len(pairs) - 1))
                return last

            def rms_transposes(n, src):
                pe.wait_ge(rms_xn, n * T + T)
                for b in range(4):
                    for f in range(2):
                        for t in range(T):
                            c = (2 * b + f) * P
                            last = pe.transpose(ps[:, b, f * S + t * P:f * S + (t + 1) * P], src[:, t, c:c + P], ident)
                    last.then_inc(rms_tp, 1)

            def back_transposes(src, bank0, done, wait):
                pe.wait_ge(*wait)
                for b in range(4):
                    for f in range(2):
                        for t in range(T):
                            c = (2 * b + f) * P
                            last = pe.transpose(ps[:, bank0 + b, f * S + t * P:f * S + (t + 1) * P], src[:, t, c:c + P], ident)
                    last.then_inc(done, 1)

            def out_projection(n0, u0, srcT, ready):
                pe.wait_ge(*ready)
                for n in range(2):
                    arrived(pe, u0 + n)
                    w = unit(u0 + n).rearrange("p (k n) -> p k n", n=512)
                    for t in range(T):
                        run(ps[:, 2 * n + t, :], [(srcT[:, k, t * P:(t + 1) * P], w[:, k, :]) for k in range(KB)]).then_inc(wo_ps, 1)

            def ff_units(plan, src, gu0, dn0, rounds, off_gu, off_dn, taken, last_rows):
                for kind, n, u in plan:
                    arrived(pe, u, rounds)
                    if kind == "up":
                        w = unit(u).rearrange("p (k n) -> p k n", n=512)
                        for f in range(2):
                            c = gu0 + 2 * n + f
                            if isinstance(off_gu, int) and c < 4:
                                pass
                            else:
                                pe.wait_ge(hid_sb, off_gu + (c - 3))
                            for side in range(2):
                                last = run(ps[:, c % 4, side * S:(side + 1) * S],
                                           [(w[:, k, side * S + f * P:side * S + (f + 1) * P], src[:, k, :]) for k in range(KB)])
                            last.then_inc(gu_ps, 1)
                    else:
                        rows = last_rows if (kind, n) == plan[-1][:2] else 512
                        w = unit(u)[:, 0:rows * D // P].rearrange("p (k n) -> p k n", n=D)
                        blocks = rows // P
                        pe.wait_ge(hid_sb, off_gu + (gu0 + 4 * n + blocks))
                        if n == 0:
                            pe.wait_ge(*taken)
                        for t in range(T):
                            for h in range(2):
                                for k in range(blocks):
                                    last = mm(ps[:, 4 + 2 * t + h, :], hid[:, n % 2, k, t * P:(t + 1) * P],
                                              w[:, k, h * 512:(h + 1) * 512], start=(n == 0 and k == 0),
                                              stop=((kind, n) == plan[-1][:2] and k == blocks - 1), skip_group_check=True)
                        last.then_inc(dn_ps, 1)

            pe.wait_ge(in_const, 16)
            rms_transposes(0, attn)
            pe.wait_ge(rms_h, 8)
            for hg in range(HG):
                def qk_transposes(j):
                    kind = j // 2 % 3
                    if kind < 2:
                        c = hg * 12 + (j // 6) * 4 + j % 6
                        pe.wait_ge(rope_ready, c + 1)
                        if c >= 2:
                            pe.wait_ge(qkT_sb, c - 1)
                        for h in range(4):
                            last = pe.transpose(ps[:, 2 + c % 2, h * P:(h + 1) * P], qn[:, c % 2, h, :], ident)
                        last.then_inc(qkT_ps, 1)

                for j in range(18):
                    u = hg * 9 + j // 2
                    c = hg * 18 + j
                    t = j % 2
                    if t == 0:
                        arrived(pe, u)
                    if c >= 2:
                        pe.wait_ge(proj_taken, c - 1)
                    w = unit(u).rearrange("p (k n) -> p k n", n=512)
                    run(ps[:, c % 2, :], [(hT[:, k, t * P:(t + 1) * P], w[:, k, :]) for k in range(KB)]).then_inc(proj_ready, 1)
                    if j:
                        qk_transposes(j - 1)

                pe.wait_ge(qkT_sb, hg * 12 + 12)
                pe.wait_ge(proj_taken, hg * 18 + 18)

                def scores(j):
                    h, t, c = j // 2, j % 2, hg * 8 + j
                    if c >= 2:
                        pe.wait_ge(masked, c - 1)
                    q = slice(t * P, (t + 1) * P)
                    run(ps[:, 4 + c % 2, 0:S], [(qT[:, 0, h, q], kT[:, 0, h, :])])
                    run(ps[:, 4 + c % 2, S:S + P], [(qT[:, 1, h, q], kT[:, 1, h, q])])
                    run(ps[:, 4 + c % 2, S + P:512], [(qT[:, 2, h, q], kT[:, 2, h, q])]).then_inc(sc_ps, 1)

                scores(0)
                for j in range(8):
                    h, t, c = j // 2, j % 2, hg * 8 + j
                    if j < 7:
                        scores(j + 1)
                    pe.wait_ge(prob_rdy, c + 1)
                    if c:
                        pe.wait_ge(pT_sb, c)
                    for b in range(4):
                        last = pe.transpose(ps[:, 6, b * P:(b + 1) * P], probs[:, c % 2, b * P:(b + 1) * P], ident)
                    last.then_inc(pT_ps, 1)
                    pe.wait_ge(pT_sb, c + 1)
                    if c:
                        pe.wait_ge(o_sb, c)
                    hc = slice(h * HEAD, (h + 1) * HEAD)
                    run(ps[:, 7, 0:HEAD], [(pT[:, c % 2, 0], v[:, 0, 0, hc]), (pT[:, c % 2, 1], v[:, 1, 0, hc]),
                                           (pT[:, c % 2, 2], v[:, t, 1, hc]), (pT[:, c % 2, 3], v[:, t, 2, hc])]).then_inc(o_ps, 1)
            back_transposes(attn, 0, oT_ps, (o_sb, 16))
            out_projection(0, U_QKV, oT, (oT_sb, 4))
            rms_transposes(1, attn)
            pe.wait_ge(rms_h, 16)
            ff_units(plan0, hT, 0, 0, 0, 0, 0, (rms_h, 16), FF % 512)
            rms_transposes(2, mx.rearrange("p a k s -> p a (k s)")[:, :, 0:D])
            pe.wait_ge(in_lora, 80)
            for j in range(8):
                pe.wait_ge(mix_ready, (j + 1) * KB)
                if j < 5:
                    m_rows = LORA if j < 4 else P
                    w = lw1[:, j] if j < 4 else lg1
                    if j >= 2:
                        pe.wait_ge(mix_sb, j - 1)
                    run(ps[0:m_rows, j % 2, 0:S], [(w[:, k, :], mx[:, j % 2, k, :]) for k in range(KB)]).then_inc(mix_ps, 1)
                else:
                    for n in range(2):
                        u = RKV0 + 2 * (j - 5) + n
                        arrived(pe, u)
                        w = unit(u).rearrange("p (k n) -> p k n", n=512)
                        for t in range(T):
                            c = 4 * (j - 5) + 2 * n + t
                            if c >= 2:
                                pe.wait_ge(rkv_sb, c - 1)
                            run(ps[:, 2 + c % 2, :], [(mx[:, j % 2, k, t * P:(t + 1) * P], w[:, k, :]) for k in range(KB)]).then_inc(rkv_ps, 1)

            pe.wait_ge(mix_sb, 5)
            pe.wait_ge(rkv_sb, 12)
            with pe.Fori(0, NQ) as q:
                pe.wait_ge(in_par, q * 160 + 160)
                for d in range(2):
                    b = 4 * d
                    pe.wait_ge(head_done, q + 1)
                    for n in range(2):
                        for t in range(T):
                            last = run(ps[:, b + n, t * RQ:(t + 1) * RQ], [(loraT[2 * n + d][:, t * P:(t + 1) * P], par_l[:, 2 * n + d, :])])
                    last.then_inc(stage["za"].ps, 1)
                for d in range(2):
                    b = 4 * d
                    o = st[d]
                    pe.wait_ge(stage["za"].sb, turn(q + 1, d, 2))
                    cen = [const[:, C_CEN + (2 * d + n) * P:C_CEN + (2 * d + n + 1) * P] for n in range(2)]
                    for t in range(T):
                        for n in range(2):
                            last = run(ps[:, b + 2 + t, n * RQ:(n + 1) * RQ], [(cen[n], o["sig"][:, t, :])])
                    last.then_inc(stage["cum"].ps, 1)
                    run(ps[:, b, 0:RQ], [(tri(LS if d == 0 else US), o["sig"][:, d, :])])
                    for pr in range(2):
                        last = run(ps[:, b, RQ + pr:RQ + pr + 1], [(o["sig"][:, 1 - d, pr * P:(pr + 1) * P], const[:, C_HALF + d:C_HALF + d + 1])])
                    last.then_inc(stage["end"].ps, 1)
                for s in range(2):
                    k = q * 2 + (s + 1)

                    def need(d, name):
                        pe.wait_ge(stage[name].sb, turn(k, d))

                    def four(d, name, bank, of, by, width=P):
                        for h in range(4):
                            last = run(ps[:, 4 * d + bank, h * width:(h + 1) * width], [(of[:, h, :], by(h))])
                        last.then_inc(stage[name].ps, 1)

                    def tile(d):
                        return s if d == 0 else 1 - s

                    for d in range(2):
                        o, t, b = st[d], tile(d), 4 * d
                        pe.wait_ge(ops_ok[d], q * 4 + 4)
                        if s:
                            pe.wait_ge(stage["st"].sb, turn(q + 1, d, 4))
                        for pr in range(2):
                            c = slice(pr * P, (pr + 1) * P)
                            pe.transpose(ps[:, b, (2 * pr) * P:(2 * pr + 1) * P], o["E"][:, t, 1, c], ident)
                            last = pe.transpose(ps[:, b, (2 * pr + 1) * P:(2 * pr + 2) * P], o["E"][:, t, 0, c], ident)
                        last.then_inc(stage["tA"].ps, 1)
                        for pr in range(2):
                            c = slice(pr * P, (pr + 1) * P)
                            pe.transpose(ps[:, b + 1, (2 * pr) * P:(2 * pr + 1) * P], o["inv"][:, t, c], ident)
                            last = pe.transpose(ps[:, b + 1, (2 * pr + 1) * P:(2 * pr + 2) * P], o["kt"][:, t, c], ident)
                        last.then_inc(stage["tB"].ps, 1)
                    for d in range(2):
                        o, b = st[d], 4 * d
                        need(d, "tA")
                        pe.wait_ge(stage["tB"].sb, turn(k, d, 2))
                        for h in range(4):
                            last = run(ps[:, b + 2, h * P:(h + 1) * P], [(o["AR"][:, h // 2, 0, :], o["BK"][:, h, 0, :])])
                        last.then_inc(stage["X"].ps, 1)
                    for h in range(4):
                        for d in range(2):
                            o, b = st[d], 4 * d
                            bank = b + (3, 0, 1, 3)[h]
                            if h == 0 and s:
                                pe.wait_ge(stage["y"].sb, turn(k - 1, d))
                            if h == 3:
                                pe.wait_ge(stage["gm"].sb, q * 16 + (8 * s + d + 1))
                            ar = o["AR"][:, h // 2].rearrange("p a b -> p (a b)")
                            run(ps[:, bank, 0:2 * P], [(o["BK"][:, h, 0, :], ar)])
                            run(ps[:, bank, 2 * P:4 * P], [(o["BK"][:, h, 1, :], ar)]).then_inc(stage["gm"].ps, 1)
                    for d in range(2):
                        o = st[d]
                        pe.wait_ge(stage["X"].sb, turn(k, d, 2))
                        pe.wait_ge(stage["gm"].sb, q * 16 + (8 * s + d + 7))
                        four(d, "D2", 0, o["DT"], lambda h: o["D"][:, h, :])
                        four(d, "D2T", 1, o["D"], lambda h: o["DT"][:, h, :])
                    for d in range(2):
                        o = st[d]
                        need(d, "D2"); need(d, "D2T")
                        pe.wait_ge(g1_ok[d], k)
                        four(d, "D4", 2, o["D2T"], lambda h: o["D2"][:, h, :])
                        four(d, "D4T", 3, o["D2"], lambda h: o["D2T"][:, h, :])
                        four(d, "G2", 0, o["D2"], lambda h: o["G"][:, h, :])
                    for d in range(2):
                        o = st[d]
                        need(d, "D4"); need(d, "D4T")
                        four(d, "D8", 1, o["DT"], lambda h: o["D"][:, h, :])
                        need(d, "G2")
                        four(d, "G3", 2, o["D"], lambda h: o["G"][:, h, :])
                    for d in range(2):
                        o = st[d]
                        need(d, "D8"); need(d, "G3")
                        four(d, "G4", 3, o["D2"], lambda h: o["G"][:, h, :])
                    for d in range(2):
                        o = st[d]
                        need(d, "G4")
                        four(d, "E", 0, o["G"], lambda h: o["Mo"][:, h, :])
                        four(d, "ET", 1, o["Mo"], lambda h: o["G"][:, h, :])
                    for d in range(2):
                        o = st[d]
                        need(d, "E"); need(d, "ET")
                        four(d, "E2", 2, o["D"], lambda h: o["D2T"][:, h, :])
                        four(d, "E2T", 3, o["D2T"], lambda h: o["D"][:, h, :])
                    for d in range(2):
                        o = st[d]
                        need(d, "E2"); need(d, "E2T")
                        four(d, "E4T", 0, o["DT"], lambda h: o["Mo"][:, h, :])

                    def value(t, h):
                        return kkn[:, t, h * RH:(h + 1) * RH]

                    pe.wait_ge(vq_ok, q + 1)
                    for d in range(2):
                        o, t = st[d], tile(d)
                        for h in range(4):
                            pairs = [(o["gm"][:, h, 2, :], value(t, h))]
                            if s:
                                pairs.append((o["AR"][:, h // 2, 0, :], o["S0"][:, h, :]))
                            last = run(ps[:, 4 * d + 1, h * RH:(h + 1) * RH], pairs)
                        last.then_inc(stage["z0"].ps, 1)
                    for name, bank, of, src, before in (("z1", 2, "G", 0, "z0"), ("z2", 3, "D", 1, "z1"),
                                                        ("z3", 1, "Mo", 2, "z2"), ("u", 2, "D2", 0, "z3")):
                        for d in range(2):
                            o = st[d]
                            need(d, before)
                            if name == "u":
                                need(d, "E4T")
                            four(d, name, bank, o[of], lambda h: o["z"][src][:, h * RH:(h + 1) * RH], RH)
                    for d in range(2):
                        o, t = st[d], tile(d)
                        need(d, "u")
                        for h in range(4):
                            u = o["z"][1][:, h * RH:(h + 1) * RH]
                            pairs = [(o["gm"][:, h, 3, :], value(t, h)), (o["gm"][:, h, 1, :], u)]
                            if s:
                                pairs.append((o["AR"][:, h // 2, 1, :], o["S0"][:, h, :]))
                            last = run(ps[:, 4 * d + 3, h * RH:(h + 1) * RH], pairs)
                        last.then_inc(stage["y"].ps, 1)
                        if not s:
                            pe.wait_ge(ke_ok[d], q * 2 + 2)
                            for h in range(4):
                                pr, r = h // 2, slice(h % 2 * RH, h % 2 * RH + RH)
                                c = slice(h * RH, (h + 1) * RH)
                                last = run(ps[r, 4 * d, pr * RH:(pr + 1) * RH],
                                           [(o["ke"][:, c], value(t, h)), (o["be"][:, c], o["z"][1][:, c])])
                            last.then_inc(stage["st"].ps, 1)
                for t in range(T):
                    last = run(ps[:, 1, t * RQ:(t + 1) * RQ], [(sgT[:, t * P:(t + 1) * P], par_g)])
                last.then_inc(gate_ps, 1)
            back_transposes(mixo, 0, oT_ps, (head_done, NQ + 1))
            out_projection(1, BWO0, moT, (oT_sb, 8))
            rms_transposes(3, mixo)
            pe.wait_ge(rms_h, 32)
            pe.wait_ge(in_router, 16)
            for t in range(T):
                last = run(ps[:, 4, t * EXPERTS:(t + 1) * EXPERTS], [(hT[:, k, t * P:(t + 1) * P], rw[:, k, :]) for k in range(KB)])
            last.then_inc(lg_ps, 1)

            with pe.Fori(0, EXPERTS // 2) as i:
                for e in range(2):
                    ff_units(ff_plan(FFE // 256, MOE0 + e * U_EXPERT), hT, GU0 + e * GUE, 0, i * 7, i * 2 * GUE, 0,
                             (dn_taken, i * 8 + (4 * e + 4)), 512)

        @block.scalar
        def _(act):
            steps = Steps(act, act_step)

            def rms_squares(n, junk):
                for t in range(T):
                    if t:
                        act.wait_ge(rms_ss, n * T + t)
                    act.activation(junk, x[:, t, :], ACT.Square, accum_out=stat[:, 4 * n + t:4 * n + t + 1]).then_inc(rms_ss, 1)
                act.wait_ge(rms_ms, n + 1)
                act.activation(stat[:, 4 * n + 2:4 * n + 4], stat[:, 4 * n:4 * n + 2], ACT.Sqrt).then_inc(rms_rt, 1)

            def ff_gates(groups, gu0, off):
                for c in range(gu0, gu0 + 2 * groups):
                    act.wait_ge(gu_ps, off + (c + 1))
                    if not (isinstance(off, int) and c < 2):
                        act.wait_ge(hid_sb, off + (c - 1))
                    act.activation(sg[:, c % 2, :], ps[:, c % 4, 0:S], ACT.Silu).then_inc(sg_sb, 1)

            act.wait_ge(in_x, 16)
            rms_squares(0, probs.rearrange("p a b -> p (a b)"))
            act.wait_ge(tables, 1)
            act.activation(cs[:, 1, :, 16:32], ang[:, 1], ACT.Sin).then_inc(tables, 1)
            act.activation(cs[:, 0, :, 0:16], ang[:, 2], ACT.Sin).then_inc(tables, 1)
            act.wait_ge(qkgain, 1)
            for hg in range(HG):
                def move(j):
                    kind, g, t = j // 2 % 3, j // 6, j % 2
                    if kind < 2:
                        c = hg * 12 + g * 4 + j % 6
                        act.wait_ge(qkT_ps, c + 1)
                        act.activation((qT, kT)[kind][:, g, :, t * P:(t + 1) * P],
                                       ps[:, 2 + c % 2, :].rearrange("p (h n) -> p h n", h=4), ACT.Copy,
                                       scale=qkc[:, kind * 3 + g:kind * 3 + g + 1]).then_inc(qkT_sb, 1)

                for j in range(18):
                    c = hg * 18 + j
                    if j // 2 % 3 < 2:
                        n = hg * 12 + (j // 6) * 4 + j % 6
                        act.wait_ge(proj_ready, c + 1)
                        if n >= 2:
                            act.wait_ge(ms_ready, n - 1)
                        act.activation(sq[:, n % 2, :], ps[:, c % 2, :], ACT.Square).then_inc(sq_ready, 1)
                        act.wait_ge(ms_ready, n + 1)
                        b = 16 + 8 * (n % 2)
                        act.activation(stat[:, b + 4:b + 8], stat[:, b:b + 4], ACT.Sqrt).then_inc(rt_ready, 1)
                    if j:
                        move(j - 1)
                for j in range(8):
                    c = hg * 8 + j
                    act.wait_ge(maxed, c + 1)
                    b = 32 + 2 * (c % 2)
                    act.activation(probs[:, c % 2, :], probs[:, c % 2, :], ACT.Exp, bias=stat[:, b:b + 1],
                                   accum_out=stat[:, b + 1:b + 2]).then_inc(prob_rdy, 1)
                    act.wait_ge(pT_ps, c + 1)
                    act.activation(pT[:, c % 2].rearrange("p a b -> p (a b)"), ps[:, 6, :], ACT.Copy).then_inc(pT_sb, 1)
            for b in range(4):
                act.wait_ge(oT_ps, b + 1)
                for f in range(2):
                    last = act.activation(oT[:, 2 * b + f, :].rearrange("p (l q r) -> p r q l", q=4, r=4),
                                          ps[:, b, f * S:(f + 1) * S].rearrange("p (r q l) -> p r q l", r=4, q=4), ACT.Copy)
                last.then_inc(oT_sb, 1)
            act.wait_ge(x_done, 4)
            rms_squares(1, probs.rearrange("p a b -> p (a b)"))
            ff_gates(FF // 256, 0, 0)
            act.wait_ge(dn_taken, 4)
            rms_squares(2, d_f.rearrange("p k s -> p (k s)")[:, 0:D])
            for j in range(5):
                act.wait_ge(mix_ps, j + 1)
                m_rows = LORA if j < 4 else P
                dst = loraT[j][0:LORA, :] if j < 4 else sgT
                f = (ACT.Tanh, ACT.Tanh, ACT.Copy, ACT.Copy, ACT.Sigmoid)[j]
                act.activation(dst, ps[0:m_rows, j % 2, 0:S], f).then_inc(mix_sb, 1)
            for c in range(12):
                act.wait_ge(rkv_ps, c + 1)
                act.activation(rkv[:, c // 4, c % 2, (c // 2 % 2) * 512:(c // 2 % 2 + 1) * 512], ps[:, 2 + c % 2, :], ACT.Copy).then_inc(rkv_sb, 1)
            act.wait_ge(pad_ok, 4)
            with act.Fori(0, NQ) as q:
                act.wait_ge(kk_ss, q + 1)
                act.activation(small[:, 8:16], small[:, 0:8], ACT.Sqrt).then_inc(kk_rt, 1)
                for d in range(2):
                    o, b = st[d], 4 * d
                    act.wait_ge(stage["za"].ps, turn(q + 1, d))
                    for n, name in enumerate(("sig", "a")):
                        act.activation(o[name].rearrange("p t n -> p (t n)"), ps[:, b + n, :], ACT.Sigmoid).then_inc(stage["za"].sb, 1)
                for d in range(2):
                    o, b = st[d], 4 * d
                    act.wait_ge(stage["cum"].ps, turn(q + 1, d))
                    for t in range(T):
                        act.activation(o["E"][:, t].rearrange("p a n -> p (a n)"), ps[:, b + 2 + t, :], ACT.Exp, scale=-DECAY).then_inc(ex_ok[d], 1)
                        act.activation(o["inv"][:, t, :], ps[:, b + 2 + t, 0:RQ], ACT.Exp, scale=DECAY).then_inc(ex_ok[d], 1)
                    act.wait_ge(stage["end"].ps, turn(q + 1, d))
                    act.activation(o["be"], ps[:, b, 0:RQ], ACT.Exp, scale=-DECAY).then_inc(ex_ok[d], 1)
                    act.activation(o["pm"], ps[:, b, RQ:RQ + 2], ACT.Exp, scale=-DECAY).then_inc(ex_ok[d], 1)
                for s in range(2):
                    k = q * 2 + (s + 1)

                    def out_of(d, name, bank, dst, width=512):
                        act.wait_ge(stage[name].ps, turn(k, d))
                        act.activation(dst, ps[:, 4 * d + bank, 0:width], ACT.Copy).then_inc(stage[name].sb, 1)

                    for d in range(2):
                        out_of(d, "tA", 0, st[d]["AR"].rearrange("p a b c -> p (a b c)"))
                        act.wait_ge(stage["tB"].ps, turn(k, d))
                        for f in range(2):
                            r = slice(f * RH, f * RH + RH)
                            act.activation(st[d]["BK"][r, f::2].rearrange("p a b c -> p a (b c)"),
                                           ps[r, 4 * d + 1, :].rearrange("p (a n) -> p a n", a=2), ACT.Copy).then_inc(stage["tB"].sb, 1)
                    for names in ((("D2", 0, "D2"), ("D2T", 1, "D2T")), (("D4", 2, "D"), ("D4T", 3, "DT")), (("D8", 1, "D2"),),
                                  (("E", 0, "D2T"), ("ET", 1, "D")), (("E2", 2, "DT"), ("E2T", 3, "Mo")), (("E4T", 0, "D2"),)):
                        for d in range(2):
                            for name, bank, dst in names:
                                out_of(d, name, bank, st[d][dst].rearrange("p a b -> p (a b)"))
                    for name, bank, n in (("z0", 1, 0), ("z1", 2, 1)):
                        for d in range(2):
                            out_of(d, name, bank, st[d]["z"][n], RQ)
                act.wait_ge(gn_ss, q + 1)
                act.activation(small[:, 32:40], small[:, 24:32], ACT.Sqrt).then_inc(gn_rt, 1)
            for b in range(4):
                act.wait_ge(oT_ps, 5 + b)
                act.activation(moT[:, 2 * b:2 * b + 2, :].rearrange("p a s -> p (a s)"), ps[:, b, :], ACT.Copy).then_inc(oT_sb, 1)
            act.wait_ge(x_done, 8)
            rms_squares(3, moT.rearrange("p k s -> p (k s)")[:, 0:D])
            act.wait_ge(lg_sb, 1)
            act.activation(logits.rearrange("p a b -> p (a b)"), logits.rearrange("p a b -> p (a b)"), ACT.Exp).then_inc(lg_ex, 1)
            with act.Fori(0, EXPERTS // 2) as i:
                for e in range(2):
                    ff_gates(FFE // 256, GU0 + e * GUE, i * 2 * GUE)

        @block.vector
        def _(dve):
            steps = Steps(dve, dve_step)
            link = steps.link

            def attend(hg, j, c):
                h, t = j // 2, j % 2
                b = 32 + 2 * (c % 2)
                dve.wait_ge(prob_rdy, c + 1)
                link(dve.reciprocal(stat[:, b + 1:b + 2], stat[:, b + 1:b + 2]))
                dve.wait_ge(o_ps, c + 1)
                col = hg * 512 + h * HEAD
                dve.tensor_scalar(attn[:, t, col:col + HEAD], ps[:, 7, 0:HEAD], stat[:, b + 1:b + 2], None, ALU.mult).then_inc(o_sb, 1)

            def rms_rest(n, xn, gain, dst, permuted=False):
                dve.wait_ge(rms_ss, n * T + T)
                dve.tensor_scalar(stat[:, 4 * n:4 * n + 2], stat[:, 4 * n:4 * n + 2], 1.0 / D, EPS, ALU.mult, ALU.add).then_inc(rms_ms, 1)
                dve.wait_ge(rms_rt, n + 1)
                link(dve.reciprocal(stat[:, 4 * n + 2:4 * n + 4], stat[:, 4 * n + 2:4 * n + 4]))
                for t in range(T):
                    dve.tensor_scalar(xn[:, t, :], x[:, t, :], stat[:, 4 * n + 2 + t:4 * n + 3 + t], None, ALU.mult).then_inc(rms_xn, 1)
                for b in range(4):
                    dve.wait_ge(rms_tp, 4 * n + b + 1)
                    for f in range(2):
                        k = 2 * b + f
                        o, src = dst[:, k, :], ps[:, b, f * S:(f + 1) * S]
                        if permuted:
                            o = o.rearrange("p (r q l) -> p l q r", r=4, q=4)
                            src = src.rearrange("p (l q r) -> p l q r", q=4, r=4)
                        dve.tensor_scalar(o, src, vec[:, gain * KB + k:gain * KB + k + 1], None, ALU.mult).then_inc(rms_h, 1)

            def ff_products(groups, gu0, off, hid_of):
                for c in range(gu0, gu0 + 2 * groups):
                    dve.wait_ge(sg_sb, off + (c + 1))
                    n = c - gu0
                    w = hid_of + n // 4 - 1
                    if n % 4 == 0 and not (isinstance(off, int) and w < 1):
                        dve.wait_ge(dn_ps, off_dn(off, w))
                    dve.tensor_tensor(hid[:, n // 4 % 2, n % 4, :], sg[:, c % 2, :], ps[:, c % 4, S:2 * S], ALU.mult).then_inc(hid_sb, 1)

            def off_dn(off, w):
                return w if isinstance(off, int) else off[1] + w

            dve.wait_ge(in_x, 16)
            dve.wait_ge(in_small, 80)
            dve.wait_ge(in_const, 16)
            dve.memset(qkc[0:ROT, :], 1.0).then_inc(qkgain, 1)
            posf, turns = ang[:, 3, :, 0], ang[:, 0]
            link(dve.tensor_copy(posf, pos_i))
            link(dve.tensor_tensor(ang[:, 1], const[:, C_FREQ:C_FREQ + 16].unsqueeze(1).broadcast_to([P, T, 16]),
                                   posf.unsqueeze(2).broadcast_to([P, T, 16]), ALU.mult))
            whole = 1.5 * 2.0 ** 23
            link(dve.tensor_scalar(turns, ang[:, 1], 1.0 / (2.0 * math.pi), whole, ALU.mult, ALU.add))
            link(dve.tensor_scalar(turns, turns, whole, None, ALU.subtract))
            t1 = 6.28125
            t2 = float(np.float32(round((2.0 * math.pi - t1) * 2 ** 20) / 2 ** 20))
            t3 = 2.0 * math.pi - t1 - t2
            for part in (t1, t2, t3):
                link(dve.scalar_tensor_tensor(ang[:, 1], turns, -part, ang[:, 1], ALU.mult, ALU.add))
            link(dve.tensor_scalar(ang[:, 2], ang[:, 1], math.pi / 2, None, ALU.add))
            link(dve.tensor_scalar(turns, ang[:, 2], math.pi, -2.0 * math.pi, ALU.is_gt, ALU.mult))
            link(dve.tensor_tensor(ang[:, 2], ang[:, 2], turns, ALU.add))
            PI = 3.1415925
            dve.tensor_scalar(ang[:, 2], ang[:, 2], -PI, PI, ALU.max, ALU.min)
            link(dve.tensor_scalar(ang[:, 1], ang[:, 1], -PI, PI, ALU.max, ALU.min))
            dve.wait_ge(dve_step, steps.n)
            dve.memset(stat[:, 60:61], 0.0).then_inc(tables, 1)
            rms_rest(0, attn, 0, hT, permuted=True)
            dve.wait_ge(tables, 3)
            dve.tensor_copy(cs[:, 0, :, 16:32], cs[:, 0, :, 0:16]).then_inc(tables, 1)
            dve.tensor_scalar(cs[:, 1, :, 0:16], cs[:, 1, :, 16:32], -1.0, None, ALU.mult).then_inc(tables, 1)

            for hg in range(HG):
                for j in range(18):
                    c, kind, g, t = hg * 18 + j, j // 2 % 3, j // 6, j % 2
                    if kind < 2:
                        n = hg * 12 + g * 4 + j % 6
                        b = 16 + 8 * (n % 2)
                        dve.wait_ge(sq_ready, n + 1)
                        link(dve.tensor_reduce(stat[:, b:b + 4], sq[:, n % 2].rearrange("p (h d) -> p h d", h=4), AX, ALU.add))
                        dve.tensor_scalar(stat[:, b:b + 4], stat[:, b:b + 4], 1.0 / HEAD, EPS, ALU.mult, ALU.add).then_inc(ms_ready, 1)
                        dve.wait_ge(rt_ready, n + 1)
                        link(dve.reciprocal(stat[:, b + 4:b + 8], stat[:, b + 4:b + 8]))
                        if n >= 2:
                            dve.wait_ge(qkT_ps, n - 1)
                        dve.tensor_tensor(qn[:, n % 2], ps[:, c % 2, :].rearrange("p (h d) -> p h d", h=4),
                                          stat[:, b + 4:b + 8].unsqueeze(2).broadcast_to([P, 4, HEAD]), ALU.mult).then_inc(proj_taken, 1)
                    else:
                        dve.wait_ge(proj_ready, c + 1)
                        dve.tensor_copy(v[:, t, g, :], ps[:, c % 2, :]).then_inc(proj_taken, 1)

                for j in range(8):
                    h, t, c = j // 2, j % 2, hg * 8 + j
                    b = 32 + 2 * (c % 2)
                    dve.wait_ge(sc_ps, c + 1)
                    if c >= 2:
                        dve.wait_ge(pT_ps, c - 1)
                    dve.scalar_tensor_tensor(probs[:, c % 2, :], ps[:, 4 + c % 2, :], HEAD ** -0.5,
                                             amask[:, t, :], ALU.mult, ALU.add).then_inc(masked, 1)
                    dve.wait_ge(masked, c + 1)
                    link(dve.reduce_max(stat[:, b:b + 1], probs[:, c % 2, :], AX))
                    dve.tensor_scalar(stat[:, b:b + 1], stat[:, b:b + 1], -1.0, None, ALU.mult).then_inc(maxed, 1)
                    if j:
                        attend(hg, j - 1, c - 1)
                attend(hg, 7, hg * 8 + 7)

            def add_to_x(n0):
                for n in range(4):
                    h, t = n // 2, n % 2
                    dve.wait_ge(wo_ps, n0 + n + 1)
                    dve.tensor_tensor(x[:, t, h * 512:(h + 1) * 512], x[:, t, h * 512:(h + 1) * 512], ps[:, n, :], ALU.add).then_inc(x_done, 1)

            add_to_x(0)
            dve.wait_ge(x_done, 4)
            rms_rest(1, attn, 2, hT)
            ff_products(FF // 256, 0, 0, 0)
            dve.wait_ge(dn_ps, DN0)
            for t in range(T):
                for h in range(2):
                    c = slice(h * 512, (h + 1) * 512)
                    dve.tensor_tensor(x[:, t, c], x[:, t, c], ps[:, 4 + 2 * t + h, :], ALU.add).then_inc(dn_taken, 1)
            dve.wait_ge(dn_taken, 4)
            rms_rest(2, mx.rearrange("p a k s -> p a (k s)")[:, :, 0:D], 1, hR)
            dve.wait_ge(rms_h, 24)
            dve.tensor_tensor(d_f[:, :, 1:S], hR[:, :, 0:S - 1], hR[:, :, 1:S], ALU.subtract).then_inc(d_ready, 1)
            dve.tensor_scalar(d_f[:, :, 0:1], hR[:, :, 0:1], -1.0, None, ALU.mult).then_inc(d_ready, 1)
            dve.tensor_tensor(d_b[:, :, 0:S - 1], hR[:, :, 1:S], hR[:, :, 0:S - 1], ALU.subtract).then_inc(d_ready, 1)
            dve.tensor_scalar(d_b[:, :, S - 1:S], hR[:, :, S - 1:S], -1.0, None, ALU.mult).then_inc(d_ready, 1)
            dve.wait_ge(d_ready, 4)
            dve.tensor_tensor(d_c, d_f, d_b, ALU.add).then_inc(d_ready, 1)
            dve.wait_ge(d_ready, 5)
            dve.tensor_scalar(d_c, d_c, 0.5, None, ALU.mult).then_inc(d_ready, 1)
            for j in range(4):
                dve.memset(loraT[j][LORA:LORA + 1, :], 1.0).then_inc(ones_ok, 1)
            dve.wait_ge(d_ready, 6)
            for j, (mu, src) in enumerate(((4, d_f), (5, d_b), (6, d_f), (7, d_b), (3, d_c), (0, d_c), (1, d_c), (2, d_c))):
                if j == 2 or j == 3 or j == 4 or j == 5 or j == 6:
                    dve.wait_ge(mix_ps, j - 1)
                elif j == 7:
                    dve.wait_ge(rkv_ps, 4)
                for k in range(KB):
                    dve.scalar_tensor_tensor(mx[:, j % 2, k, :], src[:, k, :], vec[:, 32 + mu * KB + k:33 + mu * KB + k], hR[:, k, :],
                                             ALU.mult, ALU.add).then_inc(mix_ready, 1)
            dve.wait_ge(rkv_sb, 12)
            dve.wait_ge(rkv_ps, 12)

            dve.wait_ge(pad_ok, 4)
            dve.memset(small, 0.0).then_inc(head_done, 1)
            with dve.Fori(0, NQ) as q:
                with steps.repeated(q, NQ, LINKS):
                    qs = bass.ds(q * RQ, RQ)
                    dve.wait_ge(in_par, q * 160 + 160)
                    row = [rows[:, n, :].unsqueeze(1).broadcast_to([P, T, RQ]) for n in range(5)]
                    r_, k_, v_ = (rkv[:, n, :, qs] for n in range(3))

                    def heads(a):
                        return a.rearrange("p t (h n) -> p t h n", n=RH)

                    def per_head(n):
                        return small[:, n:n + 8].rearrange("p (t h) -> p t h", t=T)

                    def spread(n):
                        return per_head(n).unsqueeze(3).broadcast_to([P, T, 4, RH])

                    link(dve.tensor_tensor(kkn, k_, row[0], ALU.mult))
                    link(dve.tensor_tensor(w_, kkn, kkn, ALU.mult))
                    dve.tensor_reduce(per_head(0), heads(w_), AX, ALU.add).then_inc(kk_ss, 1)
                    dve.wait_ge(kk_rt, q + 1)
                    link(dve.tensor_scalar(small[:, 8:16], small[:, 8:16], 1e-12, None, ALU.max))
                    link(dve.reciprocal(small[:, 8:16], small[:, 8:16]))
                    link(dve.tensor_tensor(heads(kkn), heads(kkn), spread(8), ALU.mult))
                    for d in range(2):
                        o = st[d]
                        dve.wait_ge(stage["za"].sb, turn(q + 1, d, 2))
                        link(dve.scalar_tensor_tensor(o["kd"], o["a"], -1.0, row[1], ALU.add, ALU.mult))
                        link(dve.scalar_tensor_tensor(o["kd"], o["kd"], 1.0, k_, ALU.add, ALU.mult))
                        link(dve.tensor_tensor(o["a"], kkn, o["a"], ALU.mult))
                        dve.wait_ge(ex_ok[d], q * 6 + 6)
                        dve.tensor_tensor(o["E"][:, :, 0, :], o["E"][:, :, 0, :], r_, ALU.mult).then_inc(ops_ok[d], 1)
                        dve.scalar_tensor_tensor(o["E"][:, :, 1, :], kkn, -1.0, o["E"][:, :, 1, :], ALU.mult, ALU.mult).then_inc(ops_ok[d], 1)
                        dve.tensor_tensor(o["kt"], o["kd"], o["inv"], ALU.mult).then_inc(ops_ok[d], 1)
                        dve.tensor_tensor(o["inv"], o["a"], o["inv"], ALU.mult).then_inc(ops_ok[d], 1)
                        dve.tensor_tensor(o["ke"], o["kd"][:, d, :], o["be"], ALU.mult).then_inc(ke_ok[d], 1)
                        dve.tensor_tensor(o["be"], o["a"][:, d, :], o["be"], ALU.mult).then_inc(ke_ok[d], 1)
                    dve.wait_ge(ke_ok[0], q * 2 + 2)
                    dve.wait_ge(ke_ok[1], q * 2 + 2)
                    dve.wait_ge(ops_ok[0], q * 4 + 4)
                    dve.wait_ge(ops_ok[1], q * 4 + 4)
                    dve.tensor_copy(kkn, v_).then_inc(vq_ok, 1)
                    for s in range(2):
                        k = q * 2 + (s + 1)

                        def bank(d, n, width=512):
                            return ps[:, 4 * d + n, 0:width]

                        def ready(d, name):
                            dve.wait_ge(stage[name].ps, turn(k, d))

                        def four(a):
                            return a.rearrange("p (h n) -> p h n", h=4)

                        def over(mask):
                            return tri(mask).unsqueeze(1).broadcast_to([P, 4, P])

                        for d in range(2):
                            o = st[d]
                            ready(d, "X")
                            dve.tensor_tensor(o["D"], four(bank(d, 2)), over((L16, U16)[d]), ALU.mult).then_inc(stage["X"].sb, 1)
                            dve.tensor_tensor(o["Mo"], four(bank(d, 2)), over((LOFF, UOFF)[d]), ALU.mult).then_inc(stage["X"].sb, 1)
                        for h in range(4):
                            for d in range(2):
                                o = st[d]
                                b = ps[:, 4 * d + (3, 0, 1, 3)[h], :].rearrange("p (a n) -> p a n", a=4)
                                dve.wait_ge(stage["gm"].ps, q * 16 + (8 * s + 2 * h + d + 1))
                                incl = tri((UI, LI)[d])
                                strict = tri((US, LS)[d])
                                dve.tensor_tensor(o["DT"][:, h, :], b[:, 0], tri((U16, L16)[d]), ALU.mult)
                                dve.tensor_tensor(o["gm"][:, h, 2, :], b[:, 2], strict, ALU.mult)
                                dve.tensor_tensor(o["gm"][:, h, 1::2, :], b[:, 1::2], incl.unsqueeze(1).broadcast_to([P, 2, P]), ALU.mult).then_inc(stage["gm"].sb, 1)
                        for d in range(2):
                            o = st[d]
                            dve.wait_ge(stage["gm"].sb, q * 16 + (8 * s + d + 7))
                            dve.tensor_tensor(o["G"], o["DT"], ident.unsqueeze(1).broadcast_to([P, 4, P]), ALU.add).then_inc(g1_ok[d], 1)
                        before = g1_ok
                        for name, b in (("G2", 0), ("G3", 2), ("G4", 3)):
                            for d in range(2):
                                o = st[d]
                                ready(d, name)
                                if before is g1_ok:
                                    dve.wait_ge(g1_ok[d], k)
                                else:
                                    dve.wait_ge(stage[before].sb, turn(k, d))
                                dve.tensor_tensor(o["G"], four(bank(d, b)), o["G"], ALU.add).then_inc(stage[name].sb, 1)
                            before = name
                        for name, b, src, dst, before in (("z2", 3, 1, 2, "z1"), ("z3", 1, 2, 0, "z2"), ("u", 2, 0, 1, "z3")):
                            for d in range(2):
                                o = st[d]
                                ready(d, name)
                                dve.wait_ge(stage[before].sb, turn(k, d))
                                dve.tensor_tensor(o["z"][dst], bank(d, b, RQ), o["z"][src], ALU.add).then_inc(stage[name].sb, 1)
                        for d in range(2):
                            o = st[d]
                            t = s if d == 0 else 1 - s
                            ready(d, "y")
                            if s:
                                dve.wait_ge(stage["y"].sb, turn(q * 2 + 1, 1 - d))
                                dve.tensor_tensor(y_sum[:, t, :], bank(d, 3, RQ), y_sum[:, t, :], ALU.add).then_inc(stage["y"].sb, 1)
                            else:
                                dve.tensor_copy(y_sum[:, t, :], bank(d, 3, RQ)).then_inc(stage["y"].sb, 1)
                                dve.wait_ge(stage["st"].ps, turn(q + 1, d))
                                for h in range(4):
                                    pr, r = h // 2, slice(h % 2 * RH, h % 2 * RH + RH)
                                    dve.tensor_scalar(o["S0"][r, h, :], ps[r, 4 * d, pr * RH:(pr + 1) * RH], o["pm"][r, pr:pr + 1], None, ALU.mult).then_inc(stage["st"].sb, 1)
                    for d in range(2):
                        dve.wait_ge(stage["y"].sb, turn(q * 2 + 2, d))
                    y = y_sum
                    link(dve.tensor_reduce(per_head(16), heads(y), AX, ALU.add))
                    link(dve.tensor_scalar(small[:, 16:24], small[:, 16:24], 1.0 / RH, None, ALU.mult))
                    link(dve.tensor_tensor(heads(y), heads(y), spread(16), ALU.subtract))
                    link(dve.tensor_tensor(w_, y, y, ALU.mult))
                    link(dve.tensor_reduce(per_head(24), heads(w_), AX, ALU.add))
                    dve.tensor_scalar(small[:, 24:32], small[:, 24:32], 1.0 / RH, GN_EPS, ALU.mult, ALU.add).then_inc(gn_ss, 1)
                    link(dve.tensor_tensor(b_, st[0]["kd"], st[1]["kd"], ALU.add))
                    link(dve.tensor_tensor(b_, b_, r_, ALU.mult))
                    link(dve.tensor_tensor(b_, b_, row[2], ALU.mult))
                    link(dve.tensor_reduce(per_head(40), heads(b_), AX, ALU.add))
                    link(dve.tensor_tensor(heads(b_), heads(v_), spread(40), ALU.mult))
                    dve.wait_ge(gn_rt, q + 1)
                    link(dve.reciprocal(small[:, 32:40], small[:, 32:40]))
                    link(dve.tensor_tensor(heads(y), heads(y), spread(32), ALU.mult))
                    link(dve.tensor_tensor(y, y, row[3], ALU.mult))
                    link(dve.tensor_tensor(y, y, row[4], ALU.add))
                    link(dve.tensor_tensor(y, y, b_, ALU.add))
                    dve.wait_ge(gate_ps, q + 1)
                    dve.tensor_tensor(mixo[:, :, qs], y, ps[:, 1, :].rearrange("p (t n) -> p t n", t=T), ALU.mult).then_inc(head_done, 1)
            add_to_x(4)
            dve.wait_ge(x_done, 8)
            rms_rest(3, mixo, 3, hT)
            dve.wait_ge(lg_ps, 1)
            link(dve.tensor_copy(logits, ps[:, 4, 0:2 * EXPERTS].rearrange("p (t e) -> p t e", t=T)))
            other = logits.unsqueeze(2).broadcast_to([P, T, EXPERTS, EXPERTS])
            own = logits.unsqueeze(3).broadcast_to([P, T, EXPERTS, EXPERTS])
            tie = const[:, C_TIE:C_TIE + 64].rearrange("p (a b) -> p a b", a=8)
            link(dve.tensor_tensor(cmp_a, other, own, ALU.is_gt))
            link(dve.tensor_tensor(cmp_b, other, own, ALU.is_equal))
            for t in range(T):
                link(dve.tensor_tensor(cmp_b[:, t], cmp_b[:, t], tie, ALU.mult))
            link(dve.tensor_tensor(cmp_a, cmp_a, cmp_b, ALU.add))
            link(dve.tensor_reduce(comb, cmp_a, AX, ALU.add))
            link(dve.tensor_scalar(comb, comb, 1.5, None, ALU.is_lt))
            top = stat[:, 40:42]
            link(dve.tensor_reduce(top, logits, AX, ALU.max))
            dve.tensor_tensor(logits, logits, top.unsqueeze(2).broadcast_to([P, T, EXPERTS]), ALU.subtract).then_inc(lg_sb, 1)
            dve.wait_ge(lg_ex, 1)
            link(dve.tensor_tensor(comb, comb, logits, ALU.mult))
            link(dve.tensor_reduce(top, comb, AX, ALU.add))
            link(dve.reciprocal(top, top))
            link(dve.tensor_tensor(comb, comb, top.unsqueeze(2).broadcast_to([P, T, EXPERTS]), ALU.mult))
            with dve.Fori(0, EXPERTS // 2) as i:
                for e in range(2):
                    for c in range(GUE):
                        g = GU0 + e * GUE + c
                        dve.wait_ge(sg_sb, i * 2 * GUE + (g + 1))
                        if c % 4 == 0:
                            dve.wait_ge(dn_ps, i * 2 * DNE + (DN0 + e * DNE + c // 4 - 1))
                        dve.tensor_tensor(hid[:, c // 4 % 2, c % 4, :], sg[:, g % 2, :], ps[:, g % 4, S:2 * S], ALU.mult).then_inc(hid_sb, 1)
                    dve.wait_ge(dn_ps, i * 2 * DNE + (DN0 + (e + 1) * DNE))
                    dve.wait_ge(dn_taken, i * 8 + (4 * e + 4))
                    for t in range(T):
                        for h in range(2):
                            c = slice(h * 512, (h + 1) * 512)
                            dve.scalar_tensor_tensor(x[:, t, c], ps[:, 4 + 2 * t + h, :], comb[:, t, bass.ds(i * 2 + e, 1)],
                                                     x[:, t, c], ALU.mult, ALU.add).then_inc(dn_taken, 1)

        @block.gpsimd
        def _(pool):
            pool.wait_ge(tables, 5)
            pool.wait_ge(in_small, 80)
            n_step = 0

            def link(ins):
                nonlocal n_step
                n_step += 1
                ins.then_inc(pool_step, 1)
                pool.wait_ge(pool_step, n_step)

            for hg in range(HG):
                for j in range(18):
                    c, kind, g, t = hg * 18 + j, j // 2 % 3, j // 6, j % 2
                    if kind == 2:
                        continue
                    n = hg * 12 + g * 4 + j % 6
                    pool.wait_ge(proj_taken, c + 1)
                    q = qn[:, n % 2, :, 0:ROT]
                    a, b1, b2 = rope_tmp[:, 0], rope_tmp[:, 1], rope_tmp[:, 2]

                    def along(r):
                        return r.unsqueeze(1).broadcast_to([P, 4, r.shape[-1]])

                    link(pool.tensor_tensor(a, q, along(qkr[:, kind * 3 + g, :]), ALU.mult))
                    pool.tensor_tensor(b1, a, along(cs[:, 0, t, :]), ALU.mult)
                    pool.tensor_tensor(b2[:, :, 0:16], a[:, :, 16:32], along(cs[:, 1, t, 0:16]), ALU.mult)
                    link(pool.tensor_tensor(b2[:, :, 16:32], a[:, :, 0:16], along(cs[:, 1, t, 16:32]), ALU.mult))
                    pool.tensor_tensor(q, b1, b2, ALU.add).then_inc(rope_ready, 1)
            pool.wait_ge(rkv_ps, 12)
            for d in range(2):
                pool.memset(st[d]["BK"], 0.0).then_inc(pad_ok, 1)
                pool.memset(st[d]["S0"], 0.0).then_inc(pad_ok, 1)
            pool.wait_ge(head_done, NQ + 1)
            pool.dma_start(rw, router.rearrange("(k p) n -> p k n", p=P)).then_inc(in_router, 16)


LINKS = 26


def kernel(**inputs):
    import concourse.bacc as bacc
    from concourse.bass_utils import run_bass_kernel_spmd

    a = {n: np.asarray(v) for n, v in inputs.items()}

    def by_feature(v):
        return v.reshape(-1, KB, P).transpose(2, 0, 1).reshape(P, -1)

    qk = a["a_qk_norm"][0]
    given = {
        "x": a["x"][0],
        "pos": a["positions"][0].reshape(16, 4, 4).transpose(2, 1, 0).reshape(T, P).T,
        "const": constants()[0],
        "mask": constants()[1],
        "vec": by_feature(np.concatenate([a["ln_mix"], a["ln_ffn"], a["b_mu"][0]])),
        "rows": np.concatenate([a["b_kk"], a["b_ka"], a["b_rk"], a["b_lnx"][0]]),
        "qk_rows": qk[:, :, :ROT].reshape(6, ROT),
        "qk_cols": qk.reshape(6, HEAD).T,
        "wqkv": a["a_wqkv"][0], "awo": a["a_wo"][0], "wrkv": a["b_wrkv"][0], "w0": a["b_w0"][0], "w1": a["b_w1"][0],
        "w2": a["b_w2"][0], "a0": a["b_a0"][0], "a1": a["b_a1"][0], "a2": a["b_a2"][0], "g1": a["b_g1"][0],
        "g2": a["b_g2"][0], "bwo": a["b_wo"][0], "fw13": a["f_w13"][0], "fw2": a["f_w2"][0],
        "router": a["m_router"][0], "mw13": a["m_w13"][0], "mw2": a["m_w2"][0],
    }
    given = {n: np.ascontiguousarray(v) for n, v in given.items()}
    nc = bacc.Bacc("TRN2", target_bir_lowering=False, num_devices=1)
    args = [nc.dram_tensor(n, v.shape, mybir.dt.from_np(v.dtype), kind="ExternalInput").ap() for n, v in given.items()]
    out = nc.dram_tensor("out", (S, D), F32, kind="ExternalOutput").ap()
    build(nc, *args, out)
    r = run_bass_kernel_spmd(nc, [given], core_ids=[0])
    return r.results[0]["out"].reshape(1, S, D)
```

```python
import math
from contextlib import ExitStack, contextmanager

import numpy as np

import concourse.bass as bass
from concourse import mybir

F32 = mybir.dt.float32
I32 = mybir.dt.int32
ALU = mybir.AluOpType
ACT = mybir.ActivationFunctionType
AX = mybir.AxisListType.X

P = 128
D = 1024
S = 256
T = S // P
KB = D // P
EPS = 1e-6
NEG = -1e30
GROUPS = 3
HEAD = 128
ROT = 32
HG = 2
FF = 2816
FFE = 3584
EXPERTS = 8
RH = 64
RQ = 256
NQ = D // RQ
RHD = D // RH
LORA = 64
GN_EPS = 64e-5
DECAY = math.exp(-0.5)
BLK = 16

SLOT = 4096
R = 6
U_QKV = 18
U_AWO = 2
U_FF = 17
U_RKV = 6
U_BWO = 2
U_DENSE = U_QKV + U_AWO + U_FF + U_RKV + U_BWO
U_EXPERT = 21
GE = FFE // 256
OVER = 3

C_ID = 0
C_FREQ = C_ID + P
C_TRI = C_FREQ + 16
C_TIE = C_TRI + 8 * P
C_HALF = C_TIE + 64
C_ROW = C_HALF + 2
C_CEN = C_ROW + P
C_ALL = C_CEN + 4 * P
U16, UOFF, L16, LOFF, UI, US, LI, LS = range(8)


def constants():
    c = np.zeros((P, C_ALL), np.float32)
    mask = np.zeros((P, T * 512), np.float32)
    c[:, C_ID:C_ID + P] = np.eye(P)
    where = np.arange(S)
    token = (where % 16) * 16 + where // 64 + 4 * ((where // 16) % 4)
    for t in range(T):
        own = token[t * P:(t + 1) * P]
        near = np.abs(own[:, None] - token[None, :]) <= 64
        four = (own[:, None] - own[None, :]) % 4 == 0
        sixteen = (own[:, None] - own[None, :]) % 16 == 0
        mask[:, t * 512:(t + 1) * 512] = np.where(np.concatenate([near, four, sixteen], 1), 0.0, NEG)
    c[:, C_FREQ:C_FREQ + 16] = (np.float32(500000.0) ** (-np.arange(0, ROT, 2, dtype=np.float32) / np.float32(ROT)))[None]
    i = np.arange(P)
    r, q = i[:, None], i[None, :]
    same = r // BLK == q // BLK
    for n, m in enumerate([(r < q) & same, (r < q) & ~same, (r > q) & same, (r > q) & ~same, r <= q, r < q, r >= q, r > q]):
        c[:, C_TRI + n * P:C_TRI + (n + 1) * P] = m
    e = np.arange(8)
    c[:, C_TIE:C_TIE + 64] = (e[None, :] < e[:, None]).reshape(1, 64)
    c[:, C_HALF] = i < P // 2
    c[:, C_HALF + 1] = i >= P // 2
    c[:, C_ROW:C_ROW + P] = i[None, :]
    first, last = (i < P // 2)[:, None].astype(np.float32), (i >= P // 2)[:, None].astype(np.float32)
    for n, m in enumerate([(r <= q) - first, (r < q) - first, (r >= q) - last, (r > q) - last]):
        c[:, C_CEN + n * P:C_CEN + (n + 1) * P] = m
    return c, mask


class Steps:

    def __init__(self, eng, sem):
        self.eng, self.sem, self.n, self.off = eng, sem, 0, 0

    def link(self, ins):
        self.n += 1
        ins.then_inc(self.sem, 1)
        self.eng.wait_ge(self.sem, self.off + self.n)

    @contextmanager
    def repeated(self, i, times, each):
        start, self.off = self.n, i * each
        yield
        assert self.n - start == each, f"links in a turn: {self.n - start}"
        self.n, self.off = start + each * times, 0


def expert_plan(first):
    order, u = [], first
    for g in range(GE):
        order.append(("up", g, u)); u += 1
        if g >= 2 and g % 2 == 0:
            order.append(("down", g // 2 - 1, u)); u += 1
    order.append(("down", GE // 2 - 1, u))
    return order


def ff_plan(groups, first):
    order, u = [], first
    pairs = -(-groups // 2)
    for p in range(pairs):
        for g in range(2 * p, min(2 * p + 2, groups)):
            order.append(("up", g, u)); u += 1
        if p:
            order.append(("down", p - 1, u)); u += 1
    order.append(("down", pairs - 1, u))
    return order


def build(nc, x_in, pos_in, const_in, mask_in, vec_in, rows_in, qk_rows, qk_cols, wqkv, awo, wrkv, w0, w1, w2, a0, a1, a2,
          g1, g2, bwo, fw13, fw2, router, mw13, mw2, out):
    ctx = ExitStack()
    with ctx:
        arena = ctx.enter_context(nc.sbuf_tensor("arena", [P, 53200], F32))
        ps = ctx.enter_context(nc.psum_tensor("ps", [P, 8, 512], F32))

        def sem(name):
            return ctx.enter_context(nc.semaphore(name))

        class Region:

            def __init__(self, at, end):
                self.at, self.end = at, end

            def take(self, *shape, parts=P):
                n = math.prod(shape)
                v = arena[0:parts, self.at:self.at + n]
                self.at += n
                assert self.at <= self.end, (self.at, self.end)
                if len(shape) > 1:
                    names = "abcd"[:len(shape)]
                    v = v.rearrange(f"p ({' '.join(names)}) -> p {' '.join(names)}",
                                    **{n: s for n, s in zip(names, shape)})
                return v

        fixed = Region(0, 53200)
        ring = [fixed.take(SLOT) for _ in range(R)]
        x = fixed.take(T, D)
        const = fixed.take(C_ALL)
        vec = fixed.take(96)
        qkc = fixed.take(6)
        qkr = fixed.take(6, ROT)
        pos_i = fixed.take(T).bitcast(I32)
        stat = fixed.take(64)
        union = fixed.at

        ident = const[:, C_ID:C_ID + P]

        def tri(n):
            return const[:, C_TRI + n * P:C_TRI + (n + 1) * P]

        m = Region(union, 53200)
        hT = m.take(KB, S)
        qT = m.take(GROUPS, 4, S)
        kT = m.take(GROUPS, 4, S)
        v = m.take(T, GROUPS, 512)
        attn = m.take(T, D)
        oT = m.take(KB, S)
        qn = m.take(2, 4, HEAD)
        sq = m.take(2, 512)
        rope_tmp = m.take(3, 4, ROT)
        probs = m.take(2, 512)
        pT = m.take(2, 4, P)
        cs = m.take(2, T, ROT)
        ang = m.take(4, T, 16)
        amask = m.take(T, 512)
        m = Region(union, 53200)
        assert m.take(KB, S).offset == hT.offset
        hid = m.take(2, 4, S)
        sg = m.take(2, S)
        xn = m.take(T, D)
        rw = m.take(KB, EXPERTS)
        logits = m.take(T, EXPERTS)
        chosen = m.take(T, EXPERTS)
        comb = m.take(T, EXPERTS + 1)
        place = m.take(T, EXPERTS + 1)
        place2 = m.take(T, EXPERTS)
        cmp_a = m.take(T, EXPERTS, EXPERTS)
        cmp_b = m.take(T, EXPERTS, EXPERTS)
        ones = m.take(P)
        full_e = m.take(4, EXPERTS)
        over_f = m.take(4)
        over_i = m.take(4).bitcast(I32)
        pick = m.take(2, T, P)
        pickT = m.take(2, T, P)
        picked = m.take(2, KB, P)
        hid_e = m.take(2, 256)
        sg_e = m.take(2, 256)
        hidT = m.take(2, 4, P)
        yb = m.take(D)
        m = Region(union, 53200)
        rkv = m.take(3, T, D)
        loraT = [m.take(S, parts=LORA + 1) for _ in range(4)]
        sgT = m.take(S)
        after_pre = m.at
        hR = m.take(KB, S)
        d_f = m.take(KB, S)
        d_b = m.take(KB, S)
        d_c = m.take(KB, S)
        mx = m.take(2, KB, S)
        lw1 = m.take(4, KB, LORA)
        lg1 = m.take(KB, P)
        m = Region(after_pre, 53200)
        par_l = m.take(4, RQ, parts=LORA + 1)
        par_g = m.take(RQ)
        rows = m.take(5, RQ)
        mixo = m.take(T, D)
        kkn = m.take(T, RQ)
        y_sum = m.take(T, RQ)
        small = m.take(64)
        lent = Region(3 * SLOT, R * SLOT)

        def stream(m, lent):
            o = {}
            o["E"] = lent.take(T, 2, RQ)
            o["six"] = lent.take(2, 4, P)
            o["gm"] = lent.take(4, 4, P)
            o["sig"] = m.take(T, RQ)
            o["a"] = m.take(T, RQ)
            o["inv"] = lent.take(T, RQ)
            o["kt"] = lent.take(T, RQ)
            o["kd"] = lent.take(T, RQ)
            o["be"] = m.take(RQ)
            o["ke"] = m.take(RQ)
            o["AR"] = m.take(2, 2, P)
            o["BK"] = m.take(4, 2, P)
            o["z"] = [o["sig"][:, 0, :], o["sig"][:, 1, :], o["a"][:, 0, :]]
            o["DT"] = lent.take(4, P)
            for n in ("Mo", "G", "D2T"):
                o[n] = m.take(4, P)
            o["D"], o["D2"] = o["six"][:, 0], o["six"][:, 1]
            o["S0"] = m.take(4, RH)
            o["pm"] = m.take(2)
            return o

        st = [stream(m, lent), stream(m, lent)]
        w_ = st[0]["G"].rearrange("p a b -> p (a b)").rearrange("p (t n) -> p t n", t=T)
        b_ = st[0]["AR"].rearrange("p a b c -> p (a b c)").rearrange("p (t n) -> p t n", t=T)
        m = Region(after_pre + 4 * RQ + RQ + 5 * RQ + T * D, 53200)
        moT = m.take(KB, S)

        slot_full = [sem(f"slot_full{i}") for i in range(R)]
        in_x, in_const, in_small, out_done = sem("in_x"), sem("in_const"), sem("in_small"), sem("out_done")
        dve_step, act_step, pool_step = sem("dve_step"), sem("act_step"), sem("pool_step")
        rms_ss, rms_ms, rms_rt, rms_xn, rms_tp, rms_h = (sem("rms_" + n) for n in ("ss", "ms", "rt", "xn", "tp", "h"))
        tables, qkgain = sem("tables"), sem("qkgain")
        proj_ready, proj_taken = sem("proj_ready"), sem("proj_taken")
        sq_ready, ms_ready, rt_ready, qn_ready, rope_ready = (sem(n) for n in ("sq_ready", "ms_ready", "rt_ready", "qn_ready", "rope_ready"))
        qkT_ps, qkT_sb = sem("qkT_ps"), sem("qkT_sb")
        sc_ps, masked, maxed, prob_rdy, pT_ps, pT_sb, o_ps, o_sb = (sem(n) for n in ("sc_ps", "masked", "maxed", "prob_rdy", "pT_ps", "pT_sb", "o_ps", "o_sb"))
        oT_ps, oT_sb = sem("oT_ps"), sem("oT_sb")
        wo_ps, x_done = sem("wo_ps"), sem("x_done")
        gu_ps, sg_sb, hid_sb, dn_ps, dn_taken = (sem(n) for n in ("gu_ps", "sg_sb", "hid_sb", "dn_ps", "dn_taken"))
        lg_ps, lg_sb, lg_ex = (sem(n) for n in ("lg_ps", "lg_sb", "lg_ex"))
        chosen_ok, place_ps, over_ok, zero_ok = (sem(n) for n in ("chosen_ok", "place_ps", "over_ok", "zero_ok"))
        pick_ok, pickT_ps, pickT_sb, picked_ps, picked_sb = (sem(n) for n in ("pick_ok", "pickT_ps", "pickT_sb", "picked_ps", "picked_sb"))
        up_ps, sge_sb, hide_sb, hidT_ps, hidT_sb, down_ps, y_sb, back_ps, back_sb = (
            sem(n) for n in ("up_ps", "sge_sb", "hide_sb", "hidT_ps", "hidT_sb", "down_ps", "result_sb", "back_ps", "back_sb"))
        experts_done = sem("experts_done")
        in_lora, in_par, d_ready, mix_ready, mix_ps, mix_sb, ones_ok = (sem(n) for n in ("in_lora", "in_par", "d_ready", "mix_ready", "mix_ps", "mix_sb", "ones_ok"))
        rkv_ps, rkv_sb = sem("rkv_ps"), sem("rkv_sb")
        head_done = sem("head_done")
        kk_sq, kk_ss, kk_rt, kk_ok = (sem(n) for n in ("kk_sq", "kk_ss", "kk_rt", "kk_ok"))
        gate_ps, gn_ss, gn_rt = (sem(n) for n in ("gate_ps", "gn_ss", "gn_rt"))

        class Pair:

            def __init__(self, name):
                self.ps, self.sb = sem(name + "_ps"), sem(name + "_sb")

        def turn(c, d, each=1):
            return c * (2 * each) + (d - 1) * each

        STAGES = ["za", "cum", "end", "tA", "tB", "X", "gm", "D2", "D2T", "D4", "D4T", "G2", "D8", "G3", "G4",
                  "E", "ET", "E2", "E2T", "E4T", "z0", "z1", "z2", "z3", "u", "y", "st"]
        stage = {n: Pair(n) for n in STAGES}
        ops_ok = [sem(f"ops_ok{d}") for d in range(2)]
        ke_ok = [sem(f"ke_ok{d}") for d in range(2)]
        g1_ok = [sem(f"g1_ok{d}") for d in range(2)]
        ex_ok = [sem(f"ex_ok{d}") for d in range(2)]
        kd_ok = [sem(f"kd_ok{d}") for d in range(2)]
        in_router = sem("in_router")
        vq_ok, pad_ok = sem("vq_ok"), sem("pad_ok")
        block = ctx.enter_context(nc.Block())

        free = {}
        for u in range(U_QKV):
            free[u] = (proj_ready, 2 * u + 2)
        u0 = U_QKV
        for n in range(U_AWO):
            free[u0 + n] = (wo_ps, 2 * n + 2)
        u0 += U_AWO
        FF0 = u0
        plan0 = ff_plan(FF // 256, FF0)
        for kind, n, u in plan0:
            free[u] = (gu_ps, 2 * n + 2) if kind == "up" else (dn_ps, n + 1)
        u0 += U_FF
        RKV0 = u0
        for n in range(U_RKV):
            free[u0 + n] = (rkv_ps, 2 * n + 2)
        u0 += U_RKV
        BWO0 = u0
        for n in range(U_BWO):
            free[u0 + n] = (wo_ps, 2 * (U_AWO + n) + 2)
        MOE0 = U_DENSE
        GU0, DN0 = 2 * (FF // 256), -(-FF // 512)
        plans = [expert_plan(MOE0), expert_plan(MOE0 + U_EXPERT)]

        def arrived(eng, u, rounds=0):
            eng.wait_ge(slot_full[u % R], rounds * 32 + (u // R + 1) * 32)

        def unit(u):
            return ring[u % R]

        free_e = {}
        for e in range(2):
            for kind, n, u in plans[e]:
                free_e[u] = (up_ps, e * GE + n + 1) if kind == "up" else (down_ps, e * GE // 2 + n + 1)
        per_turn = {up_ps: 2 * GE, down_ps: GE}

        def wait_free_e(sp, u, i):
            w = u - R
            if w < MOE0 and isinstance(i, int):
                s, n = free[w]
                sp.wait_ge(s, n)
                return
            back = 0
            if w < MOE0:
                w, back = w + 2 * U_EXPERT, 1
            s, n = free_e[w]
            for t, per in per_turn.items():
                if s is t:
                    sp.wait_ge(s, i * per + (n - back * per))

        over_plan = expert_plan(0)
        over_uses = [len([v for v in range(U_EXPERT) if v % R == r]) for r in range(R)]
        uses = [len([u for u in range(MOE0 + EXPERTS * U_EXPERT) if u % R == r]) for r in range(R)]

        @block.sync
        def _(sp):
            def halves(u, dst, src):
                for a, b in zip(dst, src):
                    sp.dma_start(a, b).then_inc(slot_full[u % R], 16)

            def square(u, w):
                s = unit(u).rearrange("p (k n) -> p k n", n=512)
                w = w.rearrange("(k p) n -> p k n", p=P)
                halves(u, (s[:, 0:4], s[:, 4:8]), (w[:, 0:4], w[:, 4:8]))

            def ff_unit(kind, u, w13, wd, ff, rows=512):
                if kind == "up":
                    s = unit(u).rearrange("p (k n) -> p k n", n=512)
                    halves(u, (s[:, :, 0:256], s[:, :, 256:512]), w13)
                else:
                    n = rows // P
                    s = unit(u)[:, 0:n * D].rearrange("p (k n) -> p k n", n=D)
                    halves(u, (s[:, 0:n // 2], s[:, n // 2:n]), (wd[:, 0:n // 2], wd[:, n // 2:n]))

            def wait_free(u):
                if u >= R:
                    s, n = free[u - R]
                    sp.wait_ge(s, n)

            sp.dma_start(x, x_in.rearrange("(t p) n -> p t n", p=P)).then_inc(in_x, 16)
            sp.dma_start(const, const_in).then_inc(in_const, 16)
            sp.dma_start(amask.rearrange("p t n -> p (t n)"), mask_in).then_inc(in_small, 16)
            sp.dma_start(vec, vec_in).then_inc(in_small, 16)
            sp.dma_start(qkc, qk_cols).then_inc(in_small, 16)
            sp.dma_start(qkr, qk_rows.partition_broadcast(P)).then_inc(in_small, 16)
            sp.dma_start(pos_i, pos_in).then_inc(in_small, 16)
            for u in range(U_QKV):
                hg, g, kind = u // 9, u % 9 // 3, u % 3
                col = (kind * GROUPS + g) * D + hg * 512
                wait_free(u)
                square(u, wqkv[:, col:col + 512])
            for n in range(U_AWO):
                wait_free(U_QKV + n)
                square(U_QKV + n, awo[:, n * 512:(n + 1) * 512])
            f13 = fw13.rearrange("(k p) n -> p k n", p=P)
            for kind, n, u in plan0:
                wait_free(u)
                c = n * 256
                r0, r1 = n * 512, min(n * 512 + 512, FF)
                if kind == "up":
                    ff_unit(kind, u, (f13[:, :, c:c + 256], f13[:, :, FF + c:FF + c + 256]), None, FF)
                else:
                    ff_unit(kind, u, None, fw2[r0:r1, :].rearrange("(k p) n -> p k n", p=P), FF, r1 - r0)
            sp.wait_ge(x_done, 4)
            for j, w in enumerate((w1[0], w1[1], a1[0], a1[1])):
                sp.dma_start(lw1[:, j], w.rearrange("(k p) n -> p k n", p=P)).then_inc(in_lora, 16)
            sp.dma_start(lg1, g1.rearrange("(k p) n -> p k n", p=P)).then_inc(in_lora, 16)
            for n in range(U_RKV):
                wait_free(RKV0 + n)
                square(RKV0 + n, wrkv[n // 2, :, (n % 2) * 512:(n % 2 + 1) * 512])
            def rest_unit(u):
                if u < MOE0:
                    square(u, bwo[:, (u - BWO0) * 512:(u - BWO0 + 1) * 512])
                else:
                    expert_unit(plan_e[u - MOE0], 0)

            plan_e = [(e, *a) for e in range(2) for a in plans[e]]

            def expert_unit(item, i):
                e, kind, n, u = item
                w13 = mw13[bass.ds(i * 2 + e, 1)].rearrange("e (k p) n -> p (e k) n", p=P)
                wd = mw2[bass.ds(i * 2 + e, 1)].rearrange("e (k p) n -> p (e k) n", p=P)
                c = n * 256
                if kind == "up":
                    ff_unit(kind, u, (w13[:, :, c:c + 256], w13[:, :, FFE + c:FFE + c + 256]), None, FFE)
                else:
                    ff_unit(kind, u, None, wd[:, 4 * n:4 * n + 4, :], FFE)

            for q in range(NQ):
                if q == 0:
                    sp.wait_ge(rkv_sb, 12)
                else:
                    sp.wait_ge(head_done, q + 1)
                c = q * RQ
                for j, (w, b) in enumerate(((w2[0], w0[0]), (w2[1], w0[1]), (a2[0], a0[0]), (a2[1], a0[1]))):
                    sp.dma_start(par_l[0:LORA, j], w[:, c:c + RQ]).then_inc(in_par, 16)
                    sp.dma_start(par_l[LORA:LORA + 1, j], b[c:c + RQ].unsqueeze(0)).then_inc(in_par, 16)
                sp.dma_start(par_g, g2[:, c:c + RQ]).then_inc(in_par, 16)
                sp.dma_start(rows, rows_in[:, c:c + RQ].partition_broadcast(P)).then_inc(in_par, 16)
            for u in range(BWO0, BWO0 + R):
                if u % R >= 3:
                    sp.wait_ge(head_done, NQ + 1)
                wait_free(u)
                rest_unit(u)
            first = BWO0 + R - MOE0
            for item in plan_e[first:]:
                wait_free_e(sp, item[3], 0)
                expert_unit(item, 0)
            with sp.Fori(1, EXPERTS // 2) as i:
                for item in plan_e:
                    wait_free_e(sp, item[3], i)
                    expert_unit(item, i)
            sp.wait_ge(over_ok, 1)
            many = sp.value_load(over_i[0:1, 0:1], min_val=0, max_val=OVER)
            with sp.Fori(0, OVER) as j:
                with sp.If(j < many):
                    e = sp.value_load(over_i[0:1, bass.ds(j + 1, 1)], min_val=0, max_val=EXPERTS - 1)
                    w13 = mw13[bass.ds(e, 1)].rearrange("e (k p) n -> p (e k) n", p=P)
                    wd = mw2[bass.ds(e, 1)].rearrange("e (k p) n -> p (e k) n", p=P)
                    sp.wait_ge(down_ps, j * (GE // 2) + EXPERTS * GE // 2)
                    freed = [(up_ps, n + 1) if kind == "up" else (down_ps, n + 1) for kind, n, _ in over_plan]
                    for kind, n, u in over_plan:
                        if u >= R:
                            s, c = freed[u - R]
                            per = GE if s is up_ps else GE // 2
                            sp.wait_ge(s, j * per + (EXPERTS * per + c))
                        c = n * 256
                        if kind == "up":
                            ff_unit(kind, u, (w13[:, :, c:c + 256], w13[:, :, FFE + c:FFE + c + 256]), None, FFE)
                        else:
                            ff_unit(kind, u, None, wd[:, 4 * n:4 * n + 4, :], FFE)
            sp.wait_ge(experts_done, 1)
            sp.dma_start(out.rearrange("(t p) n -> p t n", p=P), x).then_inc(out_done, 16)
            sp.wait_ge(out_done, 16)

        @block.tensor
        def _(pe):
            mm = pe.matmul

            def run(o, pairs, **kw):
                for n, (a, b) in enumerate(pairs):
                    last = mm(o, a, b, start=(n == 0), stop=(n == len(pairs) - 1))
                return last

            def rms_transposes(n, src):
                pe.wait_ge(rms_xn, n * T + T)
                for b in range(4):
                    for f in range(2):
                        for t in range(T):
                            c = (2 * b + f) * P
                            last = pe.transpose(ps[:, b, f * S + t * P:f * S + (t + 1) * P], src[:, t, c:c + P], ident)
                    last.then_inc(rms_tp, 1)

            def back_transposes(src, bank0, done, wait):
                pe.wait_ge(*wait)
                for b in range(4):
                    for f in range(2):
                        for t in range(T):
                            c = (2 * b + f) * P
                            last = pe.transpose(ps[:, bank0 + b, f * S + t * P:f * S + (t + 1) * P], src[:, t, c:c + P], ident)
                    last.then_inc(done, 1)

            def out_projection(n0, u0, srcT, ready):
                pe.wait_ge(*ready)
                for n in range(2):
                    arrived(pe, u0 + n)
                    w = unit(u0 + n).rearrange("p (k n) -> p k n", n=512)
                    for t in range(T):
                        run(ps[:, 2 * n + t, :], [(srcT[:, k, t * P:(t + 1) * P], w[:, k, :]) for k in range(KB)]).then_inc(wo_ps, 1)

            def ff_units(plan, src, gu0, dn0, rounds, off_gu, off_dn, taken, last_rows):
                for kind, n, u in plan:
                    arrived(pe, u, rounds)
                    if kind == "up":
                        w = unit(u).rearrange("p (k n) -> p k n", n=512)
                        for f in range(2):
                            c = gu0 + 2 * n + f
                            if isinstance(off_gu, int) and c < 4:
                                pass
                            else:
                                pe.wait_ge(hid_sb, off_gu + (c - 3))
                            for side in range(2):
                                last = run(ps[:, c % 4, side * S:(side + 1) * S],
                                           [(w[:, k, side * S + f * P:side * S + (f + 1) * P], src[:, k, :]) for k in range(KB)])
                            last.then_inc(gu_ps, 1)
                    else:
                        rows = last_rows if (kind, n) == plan[-1][:2] else 512
                        w = unit(u)[:, 0:rows * D // P].rearrange("p (k n) -> p k n", n=D)
                        blocks = rows // P
                        pe.wait_ge(hid_sb, off_gu + (gu0 + 4 * n + blocks))
                        if n == 0:
                            pe.wait_ge(*taken)
                        for t in range(T):
                            for h in range(2):
                                for k in range(blocks):
                                    last = mm(ps[:, 4 + 2 * t + h, :], hid[:, n % 2, k, t * P:(t + 1) * P],
                                              w[:, k, h * 512:(h + 1) * 512], start=(n == 0 and k == 0),
                                              stop=((kind, n) == plan[-1][:2] and k == blocks - 1), skip_group_check=True)
                        last.then_inc(dn_ps, 1)

            pe.wait_ge(in_const, 16)
            rms_transposes(0, attn)
            pe.wait_ge(rms_h, 8)
            for hg in range(HG):
                def qk_transposes(j):
                    kind = j // 2 % 3
                    if kind < 2:
                        c = hg * 12 + (j // 6) * 4 + j % 6
                        pe.wait_ge(rope_ready, c + 1)
                        if c >= 2:
                            pe.wait_ge(qkT_sb, c - 1)
                        for h in range(4):
                            last = pe.transpose(ps[:, 2 + c % 2, h * P:(h + 1) * P], qn[:, c % 2, h, :], ident)
                        last.then_inc(qkT_ps, 1)

                for j in range(18):
                    u = hg * 9 + j // 2
                    c = hg * 18 + j
                    t = j % 2
                    if t == 0:
                        arrived(pe, u)
                    if c >= 2:
                        pe.wait_ge(proj_taken, c - 1)
                    w = unit(u).rearrange("p (k n) -> p k n", n=512)
                    run(ps[:, c % 2, :], [(hT[:, k, t * P:(t + 1) * P], w[:, k, :]) for k in range(KB)]).then_inc(proj_ready, 1)
                    if j:
                        qk_transposes(j - 1)

                pe.wait_ge(qkT_sb, hg * 12 + 12)
                pe.wait_ge(proj_taken, hg * 18 + 18)

                def scores(j):
                    h, t, c = j // 2, j % 2, hg * 8 + j
                    if c >= 2:
                        pe.wait_ge(masked, c - 1)
                    q = slice(t * P, (t + 1) * P)
                    run(ps[:, 4 + c % 2, 0:S], [(qT[:, 0, h, q], kT[:, 0, h, :])])
                    run(ps[:, 4 + c % 2, S:S + P], [(qT[:, 1, h, q], kT[:, 1, h, q])])
                    run(ps[:, 4 + c % 2, S + P:512], [(qT[:, 2, h, q], kT[:, 2, h, q])]).then_inc(sc_ps, 1)

                scores(0)
                for j in range(8):
                    h, t, c = j // 2, j % 2, hg * 8 + j
                    if j < 7:
                        scores(j + 1)
                    pe.wait_ge(prob_rdy, c + 1)
                    if c:
                        pe.wait_ge(pT_sb, c)
                    for b in range(4):
                        last = pe.transpose(ps[:, 6, b * P:(b + 1) * P], probs[:, c % 2, b * P:(b + 1) * P], ident)
                    last.then_inc(pT_ps, 1)
                    pe.wait_ge(pT_sb, c + 1)
                    if c:
                        pe.wait_ge(o_sb, c)
                    hc = slice(h * HEAD, (h + 1) * HEAD)
                    run(ps[:, 7, 0:HEAD], [(pT[:, c % 2, 0], v[:, 0, 0, hc]), (pT[:, c % 2, 1], v[:, 1, 0, hc]),
                                           (pT[:, c % 2, 2], v[:, t, 1, hc]), (pT[:, c % 2, 3], v[:, t, 2, hc])]).then_inc(o_ps, 1)
            back_transposes(attn, 0, oT_ps, (o_sb, 16))
            out_projection(0, U_QKV, oT, (oT_sb, 4))
            rms_transposes(1, attn)
            pe.wait_ge(rms_h, 16)
            ff_units(plan0, hT, 0, 0, 0, 0, 0, (rms_h, 16), FF % 512)
            rms_transposes(2, mx.rearrange("p a k s -> p a (k s)")[:, :, 0:D])
            pe.wait_ge(in_lora, 80)
            for j in range(8):
                pe.wait_ge(mix_ready, (j + 1) * KB)
                if j < 5:
                    m_rows = LORA if j < 4 else P
                    w = lw1[:, j] if j < 4 else lg1
                    if j >= 2:
                        pe.wait_ge(mix_sb, j - 1)
                    run(ps[0:m_rows, j % 2, 0:S], [(w[:, k, :], mx[:, j % 2, k, :]) for k in range(KB)]).then_inc(mix_ps, 1)
                else:
                    for n in range(2):
                        u = RKV0 + 2 * (j - 5) + n
                        arrived(pe, u)
                        w = unit(u).rearrange("p (k n) -> p k n", n=512)
                        for t in range(T):
                            c = 4 * (j - 5) + 2 * n + t
                            if c >= 2:
                                pe.wait_ge(rkv_sb, c - 1)
                            run(ps[:, 2 + c % 2, :], [(mx[:, j % 2, k, t * P:(t + 1) * P], w[:, k, :]) for k in range(KB)]).then_inc(rkv_ps, 1)

            pe.wait_ge(mix_sb, 5)
            pe.wait_ge(rkv_sb, 12)
            with pe.Fori(0, NQ) as q:
                pe.wait_ge(in_par, q * 160 + 160)
                for d in range(2):
                    b = 4 * d
                    pe.wait_ge(head_done, q + 1)
                    for n in range(2):
                        for t in range(T):
                            last = run(ps[:, b + n, t * RQ:(t + 1) * RQ], [(loraT[2 * n + d][:, t * P:(t + 1) * P], par_l[:, 2 * n + d, :])])
                    last.then_inc(stage["za"].ps, 1)
                for d in range(2):
                    b = 4 * d
                    o = st[d]
                    pe.wait_ge(stage["za"].sb, turn(q + 1, d, 2))
                    cen = [const[:, C_CEN + (2 * d + n) * P:C_CEN + (2 * d + n + 1) * P] for n in range(2)]
                    for t in range(T):
                        for n in range(2):
                            last = run(ps[:, b + 2 + t, n * RQ:(n + 1) * RQ], [(cen[n], o["sig"][:, t, :])])
                    last.then_inc(stage["cum"].ps, 1)
                    run(ps[:, b, 0:RQ], [(tri(LS if d == 0 else US), o["sig"][:, d, :])])
                    for pr in range(2):
                        last = run(ps[:, b, RQ + pr:RQ + pr + 1], [(o["sig"][:, 1 - d, pr * P:(pr + 1) * P], const[:, C_HALF + d:C_HALF + d + 1])])
                    last.then_inc(stage["end"].ps, 1)
                for s in range(2):
                    k = q * 2 + (s + 1)

                    def need(d, name):
                        pe.wait_ge(stage[name].sb, turn(k, d))

                    def four(d, name, bank, of, by, width=P):
                        for h in range(4):
                            last = run(ps[:, 4 * d + bank, h * width:(h + 1) * width], [(of[:, h, :], by(h))])
                        last.then_inc(stage[name].ps, 1)

                    def tile(d):
                        return s if d == 0 else 1 - s

                    for d in range(2):
                        o, t, b = st[d], tile(d), 4 * d
                        pe.wait_ge(ops_ok[d], q * 4 + 4)
                        if s:
                            pe.wait_ge(stage["st"].sb, turn(q + 1, d, 4))
                        for pr in range(2):
                            c = slice(pr * P, (pr + 1) * P)
                            pe.transpose(ps[:, b, (2 * pr) * P:(2 * pr + 1) * P], o["E"][:, t, 1, c], ident)
                            last = pe.transpose(ps[:, b, (2 * pr + 1) * P:(2 * pr + 2) * P], o["E"][:, t, 0, c], ident)
                        last.then_inc(stage["tA"].ps, 1)
                        for pr in range(2):
                            c = slice(pr * P, (pr + 1) * P)
                            pe.transpose(ps[:, b + 1, (2 * pr) * P:(2 * pr + 1) * P], o["inv"][:, t, c], ident)
                            last = pe.transpose(ps[:, b + 1, (2 * pr + 1) * P:(2 * pr + 2) * P], o["kt"][:, t, c], ident)
                        last.then_inc(stage["tB"].ps, 1)
                    for d in range(2):
                        o, b = st[d], 4 * d
                        need(d, "tA")
                        pe.wait_ge(stage["tB"].sb, turn(k, d, 2))
                        for h in range(4):
                            last = run(ps[:, b + 2, h * P:(h + 1) * P], [(o["AR"][:, h // 2, 0, :], o["BK"][:, h, 0, :])])
                        last.then_inc(stage["X"].ps, 1)
                    for h in range(4):
                        for d in range(2):
                            o, b = st[d], 4 * d
                            bank = b + (3, 0, 1, 3)[h]
                            if h == 0 and s:
                                pe.wait_ge(stage["y"].sb, turn(k - 1, d))
                            if h == 3:
                                pe.wait_ge(stage["gm"].sb, q * 16 + (8 * s + d + 1))
                            ar = o["AR"][:, h // 2].rearrange("p a b -> p (a b)")
                            run(ps[:, bank, 0:2 * P], [(o["BK"][:, h, 0, :], ar)])
                            run(ps[:, bank, 2 * P:4 * P], [(o["BK"][:, h, 1, :], ar)]).then_inc(stage["gm"].ps, 1)
                    for d in range(2):
                        o = st[d]
                        pe.wait_ge(stage["X"].sb, turn(k, d, 2))
                        pe.wait_ge(stage["gm"].sb, q * 16 + (8 * s + d + 7))
                        four(d, "D2", 0, o["DT"], lambda h: o["D"][:, h, :])
                        four(d, "D2T", 1, o["D"], lambda h: o["DT"][:, h, :])
                    for d in range(2):
                        o = st[d]
                        need(d, "D2"); need(d, "D2T")
                        pe.wait_ge(g1_ok[d], k)
                        four(d, "D4", 2, o["D2T"], lambda h: o["D2"][:, h, :])
                        four(d, "D4T", 3, o["D2"], lambda h: o["D2T"][:, h, :])
                        four(d, "G2", 0, o["D2"], lambda h: o["G"][:, h, :])
                    for d in range(2):
                        o = st[d]
                        need(d, "D4"); need(d, "D4T")
                        four(d, "D8", 1, o["DT"], lambda h: o["D"][:, h, :])
                        need(d, "G2")
                        four(d, "G3", 2, o["D"], lambda h: o["G"][:, h, :])
                    for d in range(2):
                        o = st[d]
                        need(d, "D8"); need(d, "G3")
                        four(d, "G4", 3, o["D2"], lambda h: o["G"][:, h, :])
                    for d in range(2):
                        o = st[d]
                        need(d, "G4")
                        four(d, "E", 0, o["G"], lambda h: o["Mo"][:, h, :])
                        four(d, "ET", 1, o["Mo"], lambda h: o["G"][:, h, :])
                    for d in range(2):
                        o = st[d]
                        need(d, "E"); need(d, "ET")
                        four(d, "E2", 2, o["D"], lambda h: o["D2T"][:, h, :])
                        four(d, "E2T", 3, o["D2T"], lambda h: o["D"][:, h, :])
                    for d in range(2):
                        o = st[d]
                        need(d, "E2"); need(d, "E2T")
                        four(d, "E4T", 0, o["DT"], lambda h: o["Mo"][:, h, :])

                    def value(t, h):
                        return kkn[:, t, h * RH:(h + 1) * RH]

                    pe.wait_ge(vq_ok, q + 1)
                    for d in range(2):
                        o, t = st[d], tile(d)
                        for h in range(4):
                            pairs = [(o["gm"][:, h, 2, :], value(t, h))]
                            if s:
                                pairs.append((o["AR"][:, h // 2, 0, :], o["S0"][:, h, :]))
                            last = run(ps[:, 4 * d + 1, h * RH:(h + 1) * RH], pairs)
                        last.then_inc(stage["z0"].ps, 1)
                    for name, bank, of, src, before in (("z1", 2, "G", 0, "z0"), ("z2", 3, "D", 1, "z1"),
                                                        ("z3", 1, "Mo", 2, "z2"), ("u", 2, "D2", 0, "z3")):
                        for d in range(2):
                            o = st[d]
                            need(d, before)
                            if name == "u":
                                need(d, "E4T")
                            four(d, name, bank, o[of], lambda h: o["z"][src][:, h * RH:(h + 1) * RH], RH)
                    for d in range(2):
                        o, t = st[d], tile(d)
                        need(d, "u")
                        for h in range(4):
                            u = o["z"][1][:, h * RH:(h + 1) * RH]
                            pairs = [(o["gm"][:, h, 3, :], value(t, h)), (o["gm"][:, h, 1, :], u)]
                            if s:
                                pairs.append((o["AR"][:, h // 2, 1, :], o["S0"][:, h, :]))
                            last = run(ps[:, 4 * d + 3, h * RH:(h + 1) * RH], pairs)
                        last.then_inc(stage["y"].ps, 1)
                        if not s:
                            pe.wait_ge(ke_ok[d], q * 2 + 2)
                            for h in range(4):
                                pr, r = h // 2, slice(h % 2 * RH, h % 2 * RH + RH)
                                c = slice(h * RH, (h + 1) * RH)
                                last = run(ps[r, 4 * d, pr * RH:(pr + 1) * RH],
                                           [(o["ke"][:, c], value(t, h)), (o["be"][:, c], o["z"][1][:, c])])
                            last.then_inc(stage["st"].ps, 1)
                for t in range(T):
                    last = run(ps[:, 1, t * RQ:(t + 1) * RQ], [(sgT[:, t * P:(t + 1) * P], par_g)])
                last.then_inc(gate_ps, 1)
            back_transposes(mixo, 0, oT_ps, (head_done, NQ + 1))
            out_projection(1, BWO0, moT, (oT_sb, 8))
            rms_transposes(3, xn)
            pe.wait_ge(rms_h, 32)
            pe.wait_ge(in_router, 16)
            for t in range(T):
                last = run(ps[:, 4, t * EXPERTS:(t + 1) * EXPERTS], [(hT[:, k, t * P:(t + 1) * P], rw[:, k, :]) for k in range(KB)])
            last.then_inc(lg_ps, 1)
            pe.wait_ge(chosen_ok, 1)
            run(ps[:, 5, 0:EXPERTS], [(tri(US), chosen[:, 0, :])])
            run(ps[:, 5, EXPERTS:2 * EXPERTS], [(tri(US), chosen[:, 1, :]), (ones, chosen[:, 0, :])])
            run(ps[:, 5, 2 * EXPERTS:3 * EXPERTS], [(ones, chosen[:, 0, :]), (ones, chosen[:, 1, :])]).then_inc(place_ps, 1)
            pe.wait_ge(zero_ok, 1)

            def gather(c, b):
                pe.wait_ge(pick_ok, c * 2)
                if not isinstance(c, int):
                    pe.wait_ge(back_sb, c * 4 - 4)
                for t in range(T):
                    last = pe.transpose(ps[:, 4, t * P:(t + 1) * P], pick[:, b, t, :], ident)
                last.then_inc(pickT_ps, 1)
                for half, bank in ((0, 7), (1, 4)):
                    if half:
                        pe.wait_ge(pickT_sb, c)
                    for k in range(4):
                        f = (4 * half + k) * P
                        last = run(ps[:, bank, k * P:(k + 1) * P], [(xn[:, t, f:f + P], pick[:, b, t, :]) for t in range(T)])
                    last.then_inc(picked_ps, 1)

            def scatter(c, b):
                pe.wait_ge(y_sb, c * 2)
                pe.wait_ge(picked_sb, c * 2)
                for n in range(4):
                    t, h = n // 2, n % 2
                    if n >= 2:
                        pe.wait_ge(back_sb, c * 4 + (n - 5))
                    run(ps[:, (4, 7)[n % 2], :], [(pickT[:, b, t, :], yb[:, h * 512:(h + 1) * 512])]).then_inc(back_ps, 1)

            def expert(n, c, b, plan, landed, at_second=None, before_last=None):
                pe.wait_ge(picked_sb, c * 2)

                def hidden(g):
                    pe.wait_ge(hide_sb, n * GE + (g + 1))
                    if g:
                        pe.wait_ge(hidT_sb, n * GE + g)
                    for f in range(2):
                        at = g % 2 * 256 + f * P
                        last = pe.transpose(ps[:, 3, at:at + P], hid_e[:, g % 2, f * P:(f + 1) * P], ident)
                    last.then_inc(hidT_ps, 1)

                for kind, g, u in plan:
                    if kind == "down" and g == GE // 2 - 1:
                        if before_last:
                            before_last()
                        hidden(GE - 1)
                    landed(u)
                    if kind == "up":
                        w = unit(u).rearrange("p (k n) -> p k n", n=512)
                        if g >= 3:
                            pe.wait_ge(hide_sb, n * GE + (g - 2))
                        run(ps[:, g % 3, :], [(picked[:, b, k, :], w[:, k, :]) for k in range(KB)]).then_inc(up_ps, 1)
                        if g:
                            hidden(g - 1)
                        if g == 1 and at_second:
                            at_second()
                    else:
                        w = unit(u).rearrange("p (k n) -> p k n", n=D)
                        pe.wait_ge(hidT_sb, n * GE + (2 * g + 2))
                        if g == 0:
                            pe.wait_ge(y_sb, n * 2 + 2)
                        for h in range(2):
                            for k in range(4):
                                last = mm(ps[:, 5 + h, :], hidT[:, g % 2, k, :], w[:, k, h * 512:(h + 1) * 512],
                                          start=(g == 0 and k == 0), stop=(g == GE // 2 - 1 and k == 3), skip_group_check=True)
                        last.then_inc(down_ps, 1)

            gather(1, 0)
            with pe.Fori(0, EXPERTS // 2) as i:
                for e in range(2):
                    n = i * 2 + e
                    expert(n, n + 1, e, plans[e], lambda u: arrived(pe, u, i * (2 * U_EXPERT // R)),
                           lambda: scatter(n + 1, 1 - e), lambda: gather(n + 2, 1 - e))
            scatter(EXPERTS + 1, 1)
            pe.wait_ge(over_ok, 1)
            many = pe.value_load(over_i[0:1, 0:1], min_val=0, max_val=OVER)

            with pe.Fori(0, OVER) as j:
                with pe.If(j < many):
                    def landed(u):
                        pe.wait_ge(slot_full[u % R], j * (32 * over_uses[u % R]) + 32 * (uses[u % R] + u // R + 1))

                    n = j + EXPERTS
                    gather(n + 2, 0)
                    expert(n, n + 2, 0, over_plan, landed)
                    scatter(n + 2, 0)

        @block.scalar
        def _(act):
            steps = Steps(act, act_step)

            def rms_squares(n, junk):
                for t in range(T):
                    if t:
                        act.wait_ge(rms_ss, n * T + t)
                    act.activation(junk, x[:, t, :], ACT.Square, accum_out=stat[:, 4 * n + t:4 * n + t + 1]).then_inc(rms_ss, 1)
                act.wait_ge(rms_ms, n + 1)
                act.activation(stat[:, 4 * n + 2:4 * n + 4], stat[:, 4 * n:4 * n + 2], ACT.Sqrt).then_inc(rms_rt, 1)

            def ff_gates(groups, gu0, off):
                for c in range(gu0, gu0 + 2 * groups):
                    act.wait_ge(gu_ps, off + (c + 1))
                    if not (isinstance(off, int) and c < 2):
                        act.wait_ge(hid_sb, off + (c - 1))
                    act.activation(sg[:, c % 2, :], ps[:, c % 4, 0:S], ACT.Silu).then_inc(sg_sb, 1)

            act.wait_ge(in_x, 16)
            rms_squares(0, probs.rearrange("p a b -> p (a b)"))
            act.wait_ge(tables, 1)
            act.activation(cs[:, 1, :, 16:32], ang[:, 1], ACT.Sin).then_inc(tables, 1)
            act.activation(cs[:, 0, :, 0:16], ang[:, 2], ACT.Sin).then_inc(tables, 1)
            act.wait_ge(qkgain, 1)
            for hg in range(HG):
                def move(j):
                    kind, g, t = j // 2 % 3, j // 6, j % 2
                    if kind < 2:
                        c = hg * 12 + g * 4 + j % 6
                        act.wait_ge(qkT_ps, c + 1)
                        act.activation((qT, kT)[kind][:, g, :, t * P:(t + 1) * P],
                                       ps[:, 2 + c % 2, :].rearrange("p (h n) -> p h n", h=4), ACT.Copy,
                                       scale=qkc[:, kind * 3 + g:kind * 3 + g + 1]).then_inc(qkT_sb, 1)

                for j in range(18):
                    c = hg * 18 + j
                    if j // 2 % 3 < 2:
                        n = hg * 12 + (j // 6) * 4 + j % 6
                        act.wait_ge(proj_ready, c + 1)
                        if n >= 2:
                            act.wait_ge(ms_ready, n - 1)
                        act.activation(sq[:, n % 2, :], ps[:, c % 2, :], ACT.Square).then_inc(sq_ready, 1)
                        act.wait_ge(ms_ready, n + 1)
                        b = 16 + 8 * (n % 2)
                        act.activation(stat[:, b + 4:b + 8], stat[:, b:b + 4], ACT.Sqrt).then_inc(rt_ready, 1)
                    if j:
                        move(j - 1)
                for j in range(8):
                    c = hg * 8 + j
                    act.wait_ge(maxed, c + 1)
                    b = 32 + 2 * (c % 2)
                    act.activation(probs[:, c % 2, :], probs[:, c % 2, :], ACT.Exp, bias=stat[:, b:b + 1],
                                   accum_out=stat[:, b + 1:b + 2]).then_inc(prob_rdy, 1)
                    act.wait_ge(pT_ps, c + 1)
                    act.activation(pT[:, c % 2].rearrange("p a b -> p (a b)"), ps[:, 6, :], ACT.Copy).then_inc(pT_sb, 1)
            for b in range(4):
                act.wait_ge(oT_ps, b + 1)
                for f in range(2):
                    last = act.activation(oT[:, 2 * b + f, :].rearrange("p (l q r) -> p r q l", q=4, r=4),
                                          ps[:, b, f * S:(f + 1) * S].rearrange("p (r q l) -> p r q l", r=4, q=4), ACT.Copy)
                last.then_inc(oT_sb, 1)
            act.wait_ge(x_done, 4)
            rms_squares(1, probs.rearrange("p a b -> p (a b)"))
            ff_gates(FF // 256, 0, 0)
            act.wait_ge(dn_taken, 4)
            rms_squares(2, d_f.rearrange("p k s -> p (k s)")[:, 0:D])
            for j in range(5):
                act.wait_ge(mix_ps, j + 1)
                m_rows = LORA if j < 4 else P
                dst = loraT[j][0:LORA, :] if j < 4 else sgT
                f = (ACT.Tanh, ACT.Tanh, ACT.Copy, ACT.Copy, ACT.Sigmoid)[j]
                act.activation(dst, ps[0:m_rows, j % 2, 0:S], f).then_inc(mix_sb, 1)
            for c in range(12):
                act.wait_ge(rkv_ps, c + 1)
                act.activation(rkv[:, c // 4, c % 2, (c // 2 % 2) * 512:(c // 2 % 2 + 1) * 512], ps[:, 2 + c % 2, :], ACT.Copy).then_inc(rkv_sb, 1)
            act.wait_ge(pad_ok, 4)
            with act.Fori(0, NQ) as q:
                act.wait_ge(kk_ss, q + 1)
                act.activation(small[:, 8:16], small[:, 0:8], ACT.Sqrt).then_inc(kk_rt, 1)
                for d in range(2):
                    o, b = st[d], 4 * d
                    act.wait_ge(stage["za"].ps, turn(q + 1, d))
                    for n, name in enumerate(("sig", "a")):
                        act.activation(o[name].rearrange("p t n -> p (t n)"), ps[:, b + n, :], ACT.Sigmoid).then_inc(stage["za"].sb, 1)
                for d in range(2):
                    o, b = st[d], 4 * d
                    act.wait_ge(stage["cum"].ps, turn(q + 1, d))
                    for t in range(T):
                        act.activation(o["E"][:, t].rearrange("p a n -> p (a n)"), ps[:, b + 2 + t, :], ACT.Exp, scale=-DECAY).then_inc(ex_ok[d], 1)
                        act.activation(o["inv"][:, t, :], ps[:, b + 2 + t, 0:RQ], ACT.Exp, scale=DECAY).then_inc(ex_ok[d], 1)
                    act.wait_ge(stage["end"].ps, turn(q + 1, d))
                    act.activation(o["be"], ps[:, b, 0:RQ], ACT.Exp, scale=-DECAY).then_inc(ex_ok[d], 1)
                    act.activation(o["pm"], ps[:, b, RQ:RQ + 2], ACT.Exp, scale=-DECAY).then_inc(ex_ok[d], 1)
                for s in range(2):
                    k = q * 2 + (s + 1)

                    def out_of(d, name, bank, dst, width=512):
                        act.wait_ge(stage[name].ps, turn(k, d))
                        act.activation(dst, ps[:, 4 * d + bank, 0:width], ACT.Copy).then_inc(stage[name].sb, 1)

                    for d in range(2):
                        out_of(d, "tA", 0, st[d]["AR"].rearrange("p a b c -> p (a b c)"))
                        act.wait_ge(stage["tB"].ps, turn(k, d))
                        for f in range(2):
                            r = slice(f * RH, f * RH + RH)
                            act.activation(st[d]["BK"][r, f::2].rearrange("p a b c -> p a (b c)"),
                                           ps[r, 4 * d + 1, :].rearrange("p (a n) -> p a n", a=2), ACT.Copy).then_inc(stage["tB"].sb, 1)
                    for names in ((("D2", 0, "D2"), ("D2T", 1, "D2T")), (("D4", 2, "D"), ("D4T", 3, "DT")), (("D8", 1, "D2"),),
                                  (("E", 0, "D2T"), ("ET", 1, "D")), (("E2", 2, "DT"), ("E2T", 3, "Mo")), (("E4T", 0, "D2"),)):
                        for d in range(2):
                            for name, bank, dst in names:
                                out_of(d, name, bank, st[d][dst].rearrange("p a b -> p (a b)"))
                    for name, bank, n in (("z0", 1, 0), ("z1", 2, 1)):
                        for d in range(2):
                            out_of(d, name, bank, st[d]["z"][n], RQ)
                act.wait_ge(gn_ss, q + 1)
                act.activation(small[:, 32:40], small[:, 24:32], ACT.Sqrt).then_inc(gn_rt, 1)
            for b in range(4):
                act.wait_ge(oT_ps, 5 + b)
                act.activation(moT[:, 2 * b:2 * b + 2, :].rearrange("p a s -> p (a s)"), ps[:, b, :], ACT.Copy).then_inc(oT_sb, 1)
            act.wait_ge(x_done, 8)
            rms_squares(3, moT.rearrange("p k s -> p (k s)")[:, 0:D])
            act.wait_ge(lg_sb, 1)
            act.activation(logits.rearrange("p a b -> p (a b)"), logits.rearrange("p a b -> p (a b)"), ACT.Exp).then_inc(lg_ex, 1)

            def pickT_out(c, b):
                act.wait_ge(pickT_ps, c)
                act.activation(pickT[:, b].rearrange("p t n -> p (t n)"), ps[:, 4, 0:S], ACT.Copy).then_inc(pickT_sb, 1)

            def expert(n, before_last=None):
                def hidT_out(g):
                    act.wait_ge(hidT_ps, n * GE + (g + 1))
                    act.activation(hidT[:, g // 2 % 2, g % 2 * 2:g % 2 * 2 + 2, :].rearrange("p a b -> p (a b)"),
                                   ps[:, 3, g % 2 * 256:g % 2 * 256 + 256], ACT.Copy).then_inc(hidT_sb, 1)

                for g in range(GE):
                    act.wait_ge(up_ps, n * GE + (g + 1))
                    if g >= 2:
                        act.wait_ge(hide_sb, n * GE + (g - 1))
                    act.activation(sg_e[:, g % 2, :], ps[:, g % 3, 0:256], ACT.Silu).then_inc(sge_sb, 1)
                    if g:
                        hidT_out(g - 1)
                if before_last:
                    before_last()
                hidT_out(GE - 1)
                act.wait_ge(down_ps, n * (GE // 2) + GE // 2)
                act.activation(yb[:, 0:512], ps[:, 5, :], ACT.Copy).then_inc(y_sb, 1)

            pickT_out(1, 0)
            with act.Fori(0, EXPERTS // 2) as i:
                for e in range(2):
                    n = i * 2 + e
                    expert(n, lambda: pickT_out(n + 2, 1 - e))
            act.wait_ge(over_ok, 1)
            many = act.value_load(over_i[0:1, 0:1], min_val=0, max_val=OVER)
            with act.Fori(0, OVER) as j:
                with act.If(j < many):
                    pickT_out(j + (EXPERTS + 2), 0)
                    expert(j + EXPERTS)

        @block.vector
        def _(dve):
            steps = Steps(dve, dve_step)
            link = steps.link

            def attend(hg, j, c):
                h, t = j // 2, j % 2
                b = 32 + 2 * (c % 2)
                dve.wait_ge(prob_rdy, c + 1)
                link(dve.reciprocal(stat[:, b + 1:b + 2], stat[:, b + 1:b + 2]))
                dve.wait_ge(o_ps, c + 1)
                col = hg * 512 + h * HEAD
                dve.tensor_scalar(attn[:, t, col:col + HEAD], ps[:, 7, 0:HEAD], stat[:, b + 1:b + 2], None, ALU.mult).then_inc(o_sb, 1)

            def rms_rest(n, xn, gain, dst, permuted=False):
                dve.wait_ge(rms_ss, n * T + T)
                dve.tensor_scalar(stat[:, 4 * n:4 * n + 2], stat[:, 4 * n:4 * n + 2], 1.0 / D, EPS, ALU.mult, ALU.add).then_inc(rms_ms, 1)
                dve.wait_ge(rms_rt, n + 1)
                link(dve.reciprocal(stat[:, 4 * n + 2:4 * n + 4], stat[:, 4 * n + 2:4 * n + 4]))
                for t in range(T):
                    dve.tensor_scalar(xn[:, t, :], x[:, t, :], stat[:, 4 * n + 2 + t:4 * n + 3 + t], None, ALU.mult).then_inc(rms_xn, 1)
                for b in range(4):
                    dve.wait_ge(rms_tp, 4 * n + b + 1)
                    for f in range(2):
                        k = 2 * b + f
                        o, src = dst[:, k, :], ps[:, b, f * S:(f + 1) * S]
                        if permuted:
                            o = o.rearrange("p (r q l) -> p l q r", r=4, q=4)
                            src = src.rearrange("p (l q r) -> p l q r", q=4, r=4)
                        dve.tensor_scalar(o, src, vec[:, gain * KB + k:gain * KB + k + 1], None, ALU.mult).then_inc(rms_h, 1)

            def ff_products(groups, gu0, off, hid_of):
                for c in range(gu0, gu0 + 2 * groups):
                    dve.wait_ge(sg_sb, off + (c + 1))
                    n = c - gu0
                    w = hid_of + n // 4 - 1
                    if n % 4 == 0 and not (isinstance(off, int) and w < 1):
                        dve.wait_ge(dn_ps, off_dn(off, w))
                    dve.tensor_tensor(hid[:, n // 4 % 2, n % 4, :], sg[:, c % 2, :], ps[:, c % 4, S:2 * S], ALU.mult).then_inc(hid_sb, 1)

            def off_dn(off, w):
                return w if isinstance(off, int) else off[1] + w

            dve.wait_ge(in_x, 16)
            dve.wait_ge(in_small, 80)
            dve.wait_ge(in_const, 16)
            dve.memset(qkc[0:ROT, :], 1.0).then_inc(qkgain, 1)
            posf, turns = ang[:, 3, :, 0], ang[:, 0]
            link(dve.tensor_copy(posf, pos_i))
            link(dve.tensor_tensor(ang[:, 1], const[:, C_FREQ:C_FREQ + 16].unsqueeze(1).broadcast_to([P, T, 16]),
                                   posf.unsqueeze(2).broadcast_to([P, T, 16]), ALU.mult))
            whole = 1.5 * 2.0 ** 23
            link(dve.tensor_scalar(turns, ang[:, 1], 1.0 / (2.0 * math.pi), whole, ALU.mult, ALU.add))
            link(dve.tensor_scalar(turns, turns, whole, None, ALU.subtract))
            t1 = 6.28125
            t2 = float(np.float32(round((2.0 * math.pi - t1) * 2 ** 20) / 2 ** 20))
            t3 = 2.0 * math.pi - t1 - t2
            for part in (t1, t2, t3):
                link(dve.scalar_tensor_tensor(ang[:, 1], turns, -part, ang[:, 1], ALU.mult, ALU.add))
            link(dve.tensor_scalar(ang[:, 2], ang[:, 1], math.pi / 2, None, ALU.add))
            link(dve.tensor_scalar(turns, ang[:, 2], math.pi, -2.0 * math.pi, ALU.is_gt, ALU.mult))
            link(dve.tensor_tensor(ang[:, 2], ang[:, 2], turns, ALU.add))
            PI = 3.1415925
            dve.tensor_scalar(ang[:, 2], ang[:, 2], -PI, PI, ALU.max, ALU.min)
            link(dve.tensor_scalar(ang[:, 1], ang[:, 1], -PI, PI, ALU.max, ALU.min))
            dve.wait_ge(dve_step, steps.n)
            dve.memset(stat[:, 60:61], 0.0).then_inc(tables, 1)
            rms_rest(0, attn, 0, hT, permuted=True)
            dve.wait_ge(tables, 3)
            dve.tensor_copy(cs[:, 0, :, 16:32], cs[:, 0, :, 0:16]).then_inc(tables, 1)
            dve.tensor_scalar(cs[:, 1, :, 0:16], cs[:, 1, :, 16:32], -1.0, None, ALU.mult).then_inc(tables, 1)

            for hg in range(HG):
                for j in range(18):
                    c, kind, g, t = hg * 18 + j, j // 2 % 3, j // 6, j % 2
                    if kind < 2:
                        n = hg * 12 + g * 4 + j % 6
                        b = 16 + 8 * (n % 2)
                        dve.wait_ge(sq_ready, n + 1)
                        link(dve.tensor_reduce(stat[:, b:b + 4], sq[:, n % 2].rearrange("p (h d) -> p h d", h=4), AX, ALU.add))
                        dve.tensor_scalar(stat[:, b:b + 4], stat[:, b:b + 4], 1.0 / HEAD, EPS, ALU.mult, ALU.add).then_inc(ms_ready, 1)
                        dve.wait_ge(rt_ready, n + 1)
                        link(dve.reciprocal(stat[:, b + 4:b + 8], stat[:, b + 4:b + 8]))
                        if n >= 2:
                            dve.wait_ge(qkT_ps, n - 1)
                        dve.tensor_tensor(qn[:, n % 2], ps[:, c % 2, :].rearrange("p (h d) -> p h d", h=4),
                                          stat[:, b + 4:b + 8].unsqueeze(2).broadcast_to([P, 4, HEAD]), ALU.mult).then_inc(proj_taken, 1)
                    else:
                        dve.wait_ge(proj_ready, c + 1)
                        dve.tensor_copy(v[:, t, g, :], ps[:, c % 2, :]).then_inc(proj_taken, 1)

                for j in range(8):
                    h, t, c = j // 2, j % 2, hg * 8 + j
                    b = 32 + 2 * (c % 2)
                    dve.wait_ge(sc_ps, c + 1)
                    if c >= 2:
                        dve.wait_ge(pT_ps, c - 1)
                    dve.scalar_tensor_tensor(probs[:, c % 2, :], ps[:, 4 + c % 2, :], HEAD ** -0.5,
                                             amask[:, t, :], ALU.mult, ALU.add).then_inc(masked, 1)
                    dve.wait_ge(masked, c + 1)
                    link(dve.reduce_max(stat[:, b:b + 1], probs[:, c % 2, :], AX))
                    dve.tensor_scalar(stat[:, b:b + 1], stat[:, b:b + 1], -1.0, None, ALU.mult).then_inc(maxed, 1)
                    if j:
                        attend(hg, j - 1, c - 1)
                attend(hg, 7, hg * 8 + 7)

            def add_to_x(n0):
                for n in range(4):
                    h, t = n // 2, n % 2
                    dve.wait_ge(wo_ps, n0 + n + 1)
                    dve.tensor_tensor(x[:, t, h * 512:(h + 1) * 512], x[:, t, h * 512:(h + 1) * 512], ps[:, n, :], ALU.add).then_inc(x_done, 1)

            add_to_x(0)
            dve.wait_ge(x_done, 4)
            rms_rest(1, attn, 2, hT)
            ff_products(FF // 256, 0, 0, 0)
            dve.wait_ge(dn_ps, DN0)
            for t in range(T):
                for h in range(2):
                    c = slice(h * 512, (h + 1) * 512)
                    dve.tensor_tensor(x[:, t, c], x[:, t, c], ps[:, 4 + 2 * t + h, :], ALU.add).then_inc(dn_taken, 1)
            dve.wait_ge(dn_taken, 4)
            rms_rest(2, mx.rearrange("p a k s -> p a (k s)")[:, :, 0:D], 1, hR)
            dve.wait_ge(rms_h, 24)
            dve.tensor_tensor(d_f[:, :, 1:S], hR[:, :, 0:S - 1], hR[:, :, 1:S], ALU.subtract).then_inc(d_ready, 1)
            dve.tensor_scalar(d_f[:, :, 0:1], hR[:, :, 0:1], -1.0, None, ALU.mult).then_inc(d_ready, 1)
            dve.tensor_tensor(d_b[:, :, 0:S - 1], hR[:, :, 1:S], hR[:, :, 0:S - 1], ALU.subtract).then_inc(d_ready, 1)
            dve.tensor_scalar(d_b[:, :, S - 1:S], hR[:, :, S - 1:S], -1.0, None, ALU.mult).then_inc(d_ready, 1)
            dve.wait_ge(d_ready, 4)
            dve.tensor_tensor(d_c, d_f, d_b, ALU.add).then_inc(d_ready, 1)
            dve.wait_ge(d_ready, 5)
            dve.tensor_scalar(d_c, d_c, 0.5, None, ALU.mult).then_inc(d_ready, 1)
            for j in range(4):
                dve.memset(loraT[j][LORA:LORA + 1, :], 1.0).then_inc(ones_ok, 1)
            dve.wait_ge(d_ready, 6)
            for j, (mu, src) in enumerate(((4, d_f), (5, d_b), (6, d_f), (7, d_b), (3, d_c), (0, d_c), (1, d_c), (2, d_c))):
                if j == 2 or j == 3 or j == 4 or j == 5 or j == 6:
                    dve.wait_ge(mix_ps, j - 1)
                elif j == 7:
                    dve.wait_ge(rkv_ps, 4)
                for k in range(KB):
                    dve.scalar_tensor_tensor(mx[:, j % 2, k, :], src[:, k, :], vec[:, 32 + mu * KB + k:33 + mu * KB + k], hR[:, k, :],
                                             ALU.mult, ALU.add).then_inc(mix_ready, 1)
            dve.wait_ge(rkv_sb, 12)
            dve.wait_ge(rkv_ps, 12)

            dve.wait_ge(pad_ok, 4)
            dve.memset(small, 0.0).then_inc(head_done, 1)
            with dve.Fori(0, NQ) as q:
                with steps.repeated(q, NQ, LINKS):
                    qs = bass.ds(q * RQ, RQ)
                    dve.wait_ge(in_par, q * 160 + 160)
                    row = [rows[:, n, :].unsqueeze(1).broadcast_to([P, T, RQ]) for n in range(5)]
                    r_, k_, v_ = (rkv[:, n, :, qs] for n in range(3))

                    def heads(a):
                        return a.rearrange("p t (h n) -> p t h n", n=RH)

                    def per_head(n):
                        return small[:, n:n + 8].rearrange("p (t h) -> p t h", t=T)

                    def spread(n):
                        return per_head(n).unsqueeze(3).broadcast_to([P, T, 4, RH])

                    link(dve.tensor_tensor(kkn, k_, row[0], ALU.mult))
                    link(dve.tensor_tensor(w_, kkn, kkn, ALU.mult))
                    dve.tensor_reduce(per_head(0), heads(w_), AX, ALU.add).then_inc(kk_ss, 1)
                    dve.wait_ge(kk_rt, q + 1)
                    link(dve.tensor_scalar(small[:, 8:16], small[:, 8:16], 1e-12, None, ALU.max))
                    link(dve.reciprocal(small[:, 8:16], small[:, 8:16]))
                    link(dve.tensor_tensor(heads(kkn), heads(kkn), spread(8), ALU.mult))
                    for d in range(2):
                        o = st[d]
                        dve.wait_ge(stage["za"].sb, turn(q + 1, d, 2))
                        link(dve.scalar_tensor_tensor(o["kd"], o["a"], -1.0, row[1], ALU.add, ALU.mult))
                        link(dve.scalar_tensor_tensor(o["kd"], o["kd"], 1.0, k_, ALU.add, ALU.mult))
                        link(dve.tensor_tensor(o["a"], kkn, o["a"], ALU.mult))
                        dve.wait_ge(ex_ok[d], q * 6 + 6)
                        dve.tensor_tensor(o["E"][:, :, 0, :], o["E"][:, :, 0, :], r_, ALU.mult).then_inc(ops_ok[d], 1)
                        dve.scalar_tensor_tensor(o["E"][:, :, 1, :], kkn, -1.0, o["E"][:, :, 1, :], ALU.mult, ALU.mult).then_inc(ops_ok[d], 1)
                        dve.tensor_tensor(o["kt"], o["kd"], o["inv"], ALU.mult).then_inc(ops_ok[d], 1)
                        dve.tensor_tensor(o["inv"], o["a"], o["inv"], ALU.mult).then_inc(ops_ok[d], 1)
                        dve.tensor_tensor(o["ke"], o["kd"][:, d, :], o["be"], ALU.mult).then_inc(ke_ok[d], 1)
                        dve.tensor_tensor(o["be"], o["a"][:, d, :], o["be"], ALU.mult).then_inc(ke_ok[d], 1)
                    dve.wait_ge(ke_ok[0], q * 2 + 2)
                    dve.wait_ge(ke_ok[1], q * 2 + 2)
                    dve.wait_ge(ops_ok[0], q * 4 + 4)
                    dve.wait_ge(ops_ok[1], q * 4 + 4)
                    dve.tensor_copy(kkn, v_).then_inc(vq_ok, 1)
                    for s in range(2):
                        k = q * 2 + (s + 1)

                        def bank(d, n, width=512):
                            return ps[:, 4 * d + n, 0:width]

                        def ready(d, name):
                            dve.wait_ge(stage[name].ps, turn(k, d))

                        def four(a):
                            return a.rearrange("p (h n) -> p h n", h=4)

                        def over(mask):
                            return tri(mask).unsqueeze(1).broadcast_to([P, 4, P])

                        for d in range(2):
                            o = st[d]
                            ready(d, "X")
                            dve.tensor_tensor(o["D"], four(bank(d, 2)), over((L16, U16)[d]), ALU.mult).then_inc(stage["X"].sb, 1)
                            dve.tensor_tensor(o["Mo"], four(bank(d, 2)), over((LOFF, UOFF)[d]), ALU.mult).then_inc(stage["X"].sb, 1)
                        for h in range(4):
                            for d in range(2):
                                o = st[d]
                                b = ps[:, 4 * d + (3, 0, 1, 3)[h], :].rearrange("p (a n) -> p a n", a=4)
                                dve.wait_ge(stage["gm"].ps, q * 16 + (8 * s + 2 * h + d + 1))
                                incl = tri((UI, LI)[d])
                                strict = tri((US, LS)[d])
                                dve.tensor_tensor(o["DT"][:, h, :], b[:, 0], tri((U16, L16)[d]), ALU.mult)
                                dve.tensor_tensor(o["gm"][:, h, 2, :], b[:, 2], strict, ALU.mult)
                                dve.tensor_tensor(o["gm"][:, h, 1::2, :], b[:, 1::2], incl.unsqueeze(1).broadcast_to([P, 2, P]), ALU.mult).then_inc(stage["gm"].sb, 1)
                        for d in range(2):
                            o = st[d]
                            dve.wait_ge(stage["gm"].sb, q * 16 + (8 * s + d + 7))
                            dve.tensor_tensor(o["G"], o["DT"], ident.unsqueeze(1).broadcast_to([P, 4, P]), ALU.add).then_inc(g1_ok[d], 1)
                        before = g1_ok
                        for name, b in (("G2", 0), ("G3", 2), ("G4", 3)):
                            for d in range(2):
                                o = st[d]
                                ready(d, name)
                                if before is g1_ok:
                                    dve.wait_ge(g1_ok[d], k)
                                else:
                                    dve.wait_ge(stage[before].sb, turn(k, d))
                                dve.tensor_tensor(o["G"], four(bank(d, b)), o["G"], ALU.add).then_inc(stage[name].sb, 1)
                            before = name
                        for name, b, src, dst, before in (("z2", 3, 1, 2, "z1"), ("z3", 1, 2, 0, "z2"), ("u", 2, 0, 1, "z3")):
                            for d in range(2):
                                o = st[d]
                                ready(d, name)
                                dve.wait_ge(stage[before].sb, turn(k, d))
                                dve.tensor_tensor(o["z"][dst], bank(d, b, RQ), o["z"][src], ALU.add).then_inc(stage[name].sb, 1)
                        for d in range(2):
                            o = st[d]
                            t = s if d == 0 else 1 - s
                            ready(d, "y")
                            if s:
                                dve.wait_ge(stage["y"].sb, turn(q * 2 + 1, 1 - d))
                                dve.tensor_tensor(y_sum[:, t, :], bank(d, 3, RQ), y_sum[:, t, :], ALU.add).then_inc(stage["y"].sb, 1)
                            else:
                                dve.tensor_copy(y_sum[:, t, :], bank(d, 3, RQ)).then_inc(stage["y"].sb, 1)
                                dve.wait_ge(stage["st"].ps, turn(q + 1, d))
                                for h in range(4):
                                    pr, r = h // 2, slice(h % 2 * RH, h % 2 * RH + RH)
                                    dve.tensor_scalar(o["S0"][r, h, :], ps[r, 4 * d, pr * RH:(pr + 1) * RH], o["pm"][r, pr:pr + 1], None, ALU.mult).then_inc(stage["st"].sb, 1)
                    for d in range(2):
                        dve.wait_ge(stage["y"].sb, turn(q * 2 + 2, d))
                    y = y_sum
                    link(dve.tensor_reduce(per_head(16), heads(y), AX, ALU.add))
                    link(dve.tensor_scalar(small[:, 16:24], small[:, 16:24], 1.0 / RH, None, ALU.mult))
                    link(dve.tensor_tensor(heads(y), heads(y), spread(16), ALU.subtract))
                    link(dve.tensor_tensor(w_, y, y, ALU.mult))
                    link(dve.tensor_reduce(per_head(24), heads(w_), AX, ALU.add))
                    dve.tensor_scalar(small[:, 24:32], small[:, 24:32], 1.0 / RH, GN_EPS, ALU.mult, ALU.add).then_inc(gn_ss, 1)
                    link(dve.tensor_tensor(b_, st[0]["kd"], st[1]["kd"], ALU.add))
                    link(dve.tensor_tensor(b_, b_, r_, ALU.mult))
                    link(dve.tensor_tensor(b_, b_, row[2], ALU.mult))
                    link(dve.tensor_reduce(per_head(40), heads(b_), AX, ALU.add))
                    link(dve.tensor_tensor(heads(b_), heads(v_), spread(40), ALU.mult))
                    dve.wait_ge(gn_rt, q + 1)
                    link(dve.reciprocal(small[:, 32:40], small[:, 32:40]))
                    link(dve.tensor_tensor(heads(y), heads(y), spread(32), ALU.mult))
                    link(dve.tensor_tensor(y, y, row[3], ALU.mult))
                    link(dve.tensor_tensor(y, y, row[4], ALU.add))
                    link(dve.tensor_tensor(y, y, b_, ALU.add))
                    dve.wait_ge(gate_ps, q + 1)
                    dve.tensor_tensor(mixo[:, :, qs], y, ps[:, 1, :].rearrange("p (t n) -> p t n", t=T), ALU.mult).then_inc(head_done, 1)
            add_to_x(4)
            dve.wait_ge(x_done, 8)
            rms_rest(3, xn, 3, hT)
            dve.wait_ge(lg_ps, 1)
            link(dve.tensor_copy(logits, ps[:, 4, 0:2 * EXPERTS].rearrange("p (t e) -> p t e", t=T)))
            other = logits.unsqueeze(2).broadcast_to([P, T, EXPERTS, EXPERTS])
            own = logits.unsqueeze(3).broadcast_to([P, T, EXPERTS, EXPERTS])
            tie = const[:, C_TIE:C_TIE + 64].rearrange("p (a b) -> p a b", a=8)
            link(dve.tensor_tensor(cmp_a, other, own, ALU.is_gt))
            link(dve.tensor_tensor(cmp_b, other, own, ALU.is_equal))
            for t in range(T):
                link(dve.tensor_tensor(cmp_b[:, t], cmp_b[:, t], tie, ALU.mult))
            link(dve.tensor_tensor(cmp_a, cmp_a, cmp_b, ALU.add))
            link(dve.tensor_reduce(chosen, cmp_a, AX, ALU.add))
            link(dve.tensor_scalar(chosen, chosen, 1.5, None, ALU.is_lt))
            dve.memset(ones, 1.0).then_inc(chosen_ok, 1)
            dve.memset(comb, 0.0)
            dve.memset(pickT[:, 1], 0.0).then_inc(zero_ok, 1)
            dve.memset(yb[:, 0:512], 0.0).then_inc(y_sb, 1)
            dve.memset(yb[:, 512:D], 0.0).then_inc(y_sb, 1)
            link(dve.memset(place, 4.0 * S))
            top = stat[:, 40:42]
            link(dve.tensor_reduce(top, logits, AX, ALU.max))
            dve.tensor_tensor(logits, logits, top.unsqueeze(2).broadcast_to([P, T, EXPERTS]), ALU.subtract).then_inc(lg_sb, 1)
            dve.wait_ge(lg_ex, 1)
            link(dve.tensor_tensor(logits, chosen, logits, ALU.mult))
            link(dve.tensor_reduce(top, logits, AX, ALU.add))
            link(dve.reciprocal(top, top))
            link(dve.tensor_tensor(comb[:, :, 1:EXPERTS + 1], logits, top.unsqueeze(2).broadcast_to([P, T, EXPERTS]), ALU.mult))
            dve.wait_ge(place_ps, 1)
            p8 = place[:, :, 0:EXPERTS]
            link(dve.tensor_scalar(p8, chosen, -4.0 * S, 4.0 * S, ALU.mult, ALU.add))
            link(dve.tensor_tensor(p8, ps[:, 5, 0:2 * EXPERTS].rearrange("p (t e) -> p t e", t=T), p8, ALU.add))
            link(dve.tensor_scalar(place2, p8, -float(P), None, ALU.add))
            link(dve.tensor_scalar(full_e[:, 0], ps[:, 5, 2 * EXPERTS:3 * EXPERTS], P + 0.5, None, ALU.is_gt))
            link(dve.tensor_tensor(cmp_b[:, 0], tie, full_e[:, 0].unsqueeze(1).broadcast_to([P, EXPERTS, EXPERTS]), ALU.mult))
            link(dve.tensor_reduce(full_e[:, 1], cmp_b[:, 0], AX, ALU.add))
            link(dve.tensor_reduce(over_f[:, 0:1], full_e[:, 0], AX, ALU.add))
            for j in range(OVER):
                link(dve.scalar_tensor_tensor(full_e[:, 2], full_e[:, 1], float(j), full_e[:, 0], ALU.is_equal, ALU.mult))
                link(dve.tensor_tensor(full_e[:, 3], full_e[:, 2], const[:, C_ROW:C_ROW + EXPERTS], ALU.mult))
                link(dve.tensor_reduce(over_f[:, j + 1:j + 2], full_e[:, 3], AX, ALU.add))
            dve.tensor_copy(over_i, over_f).then_inc(over_ok, 1)

            def choose(c, b, where):
                if not isinstance(c, int):
                    dve.wait_ge(picked_ps, c * 2 - 2)
                for t in range(T):
                    dve.tensor_scalar(pick[:, b, t, :], const[:, C_ROW:C_ROW + P], where(t), None, ALU.is_equal).then_inc(pick_ok, 1)

            def picked_out(c, b):
                for half, bank in ((0, 7), (1, 4)):
                    dve.wait_ge(picked_ps, c * 2 + (half - 1))
                    gain = vec[:, 3 * KB + 4 * half:3 * KB + 4 * half + 4].unsqueeze(2).broadcast_to([P, 4, P])
                    dve.tensor_tensor(picked[:, b, 4 * half:4 * half + 4, :], ps[:, bank, :].rearrange("p (k n) -> p k n", k=4), gain,
                                      ALU.mult).then_inc(picked_sb, 1)

            def add_back(c, weight):
                for n in range(4):
                    t, h = n // 2, n % 2
                    cols = slice(h * 512, (h + 1) * 512)
                    dve.wait_ge(back_ps, c * 4 + (n - 3))
                    dve.scalar_tensor_tensor(x[:, t, cols], ps[:, (4, 7)[n % 2], :], weight(t), x[:, t, cols], ALU.mult, ALU.add).then_inc(back_sb, 1)

            def expert(n, at_second=None, before_last=None):
                for g in range(GE):
                    dve.wait_ge(sge_sb, n * GE + (g + 1))
                    if g >= 2:
                        dve.wait_ge(hidT_ps, n * GE + (g - 1))
                    dve.tensor_tensor(hid_e[:, g % 2, :], sg_e[:, g % 2, :], ps[:, g % 3, 256:512], ALU.mult).then_inc(hide_sb, 1)
                    if g == 1 and at_second:
                        at_second()
                if before_last:
                    before_last()
                dve.wait_ge(down_ps, n * (GE // 2) + GE // 2)
                dve.tensor_copy(yb[:, 512:D], ps[:, 6, :]).then_inc(y_sb, 1)

            choose(1, 0, lambda t: place[:, t, 0:1])
            picked_out(1, 0)
            with dve.Fori(0, EXPERTS // 2) as i:
                for e in range(2):
                    n = i * 2 + e
                    choose(n + 2, 1 - e, lambda t: place[:, t, bass.ds(n + 1, 1)])
                    expert(n, lambda: add_back(n + 1, lambda t: comb[:, t, bass.ds(n, 1)]), lambda: picked_out(n + 2, 1 - e))
            add_back(EXPERTS + 1, lambda t: comb[:, t, EXPERTS:EXPERTS + 1])
            many = dve.value_load(over_i[0:1, 0:1], min_val=0, max_val=OVER)
            with dve.Fori(0, OVER) as j:
                with dve.If(j < many):
                    e = dve.value_load(over_i[0:1, bass.ds(j + 1, 1)], min_val=0, max_val=EXPERTS - 1)
                    c = j + (EXPERTS + 2)
                    choose(c, 0, lambda t: place2[:, t, bass.ds(e, 1)])
                    picked_out(c, 0)
                    expert(j + EXPERTS)
                    add_back(c, lambda t: comb[:, t, bass.ds(e + 1, 1)])
            dve.memset(over_f, 0.0).then_inc(experts_done, 1)

        @block.gpsimd
        def _(pool):
            pool.wait_ge(tables, 5)
            pool.wait_ge(in_small, 80)
            n_step = 0

            def link(ins):
                nonlocal n_step
                n_step += 1
                ins.then_inc(pool_step, 1)
                pool.wait_ge(pool_step, n_step)

            for hg in range(HG):
                for j in range(18):
                    c, kind, g, t = hg * 18 + j, j // 2 % 3, j // 6, j % 2
                    if kind == 2:
                        continue
                    n = hg * 12 + g * 4 + j % 6
                    pool.wait_ge(proj_taken, c + 1)
                    q = qn[:, n % 2, :, 0:ROT]
                    a, b1, b2 = rope_tmp[:, 0], rope_tmp[:, 1], rope_tmp[:, 2]

                    def along(r):
                        return r.unsqueeze(1).broadcast_to([P, 4, r.shape[-1]])

                    link(pool.tensor_tensor(a, q, along(qkr[:, kind * 3 + g, :]), ALU.mult))
                    pool.tensor_tensor(b1, a, along(cs[:, 0, t, :]), ALU.mult)
                    pool.tensor_tensor(b2[:, :, 0:16], a[:, :, 16:32], along(cs[:, 1, t, 0:16]), ALU.mult)
                    link(pool.tensor_tensor(b2[:, :, 16:32], a[:, :, 0:16], along(cs[:, 1, t, 16:32]), ALU.mult))
                    pool.tensor_tensor(q, b1, b2, ALU.add).then_inc(rope_ready, 1)
            pool.wait_ge(rkv_ps, 12)
            for d in range(2):
                pool.memset(st[d]["BK"], 0.0).then_inc(pad_ok, 1)
                pool.memset(st[d]["S0"], 0.0).then_inc(pad_ok, 1)
            pool.wait_ge(head_done, NQ + 1)
            pool.dma_start(rw, router.rearrange("(k p) n -> p k n", p=P)).then_inc(in_router, 16)


LINKS = 26


def kernel(**inputs):
    import concourse.bacc as bacc
    from concourse.bass_utils import run_bass_kernel_spmd

    a = {n: np.asarray(v) for n, v in inputs.items()}

    def by_feature(v):
        return v.reshape(-1, KB, P).transpose(2, 0, 1).reshape(P, -1)

    qk = a["a_qk_norm"][0]
    given = {
        "x": a["x"][0],
        "pos": a["positions"][0].reshape(16, 4, 4).transpose(2, 1, 0).reshape(T, P).T,
        "const": constants()[0],
        "mask": constants()[1],
        "vec": by_feature(np.concatenate([a["ln_mix"], a["ln_ffn"], a["b_mu"][0]])),
        "rows": np.concatenate([a["b_kk"], a["b_ka"], a["b_rk"], a["b_lnx"][0]]),
        "qk_rows": qk[:, :, :ROT].reshape(6, ROT),
        "qk_cols": qk.reshape(6, HEAD).T,
        "wqkv": a["a_wqkv"][0], "awo": a["a_wo"][0], "wrkv": a["b_wrkv"][0], "w0": a["b_w0"][0], "w1": a["b_w1"][0],
        "w2": a["b_w2"][0], "a0": a["b_a0"][0], "a1": a["b_a1"][0], "a2": a["b_a2"][0], "g1": a["b_g1"][0],
        "g2": a["b_g2"][0], "bwo": a["b_wo"][0], "fw13": a["f_w13"][0], "fw2": a["f_w2"][0],
        "router": a["m_router"][0], "mw13": a["m_w13"][0], "mw2": a["m_w2"][0],
    }
    given = {n: np.ascontiguousarray(v) for n, v in given.items()}
    nc = bacc.Bacc("TRN2", target_bir_lowering=False, num_devices=1)
    args = [nc.dram_tensor(n, v.shape, mybir.dt.from_np(v.dtype), kind="ExternalInput").ap() for n, v in given.items()]
    out = nc.dram_tensor("out", (S, D), F32, kind="ExternalOutput").ap()
    build(nc, *args, out)
    r = run_bass_kernel_spmd(nc, [given], core_ids=[0])
    return r.results[0]["out"].reshape(1, S, D)
```

```python
import math
from contextlib import ExitStack, contextmanager

import numpy as np

import concourse.bass as bass
from concourse import mybir

F32 = mybir.dt.float32
I32 = mybir.dt.int32
ALU = mybir.AluOpType
ACT = mybir.ActivationFunctionType
AX = mybir.AxisListType.X

P = 128
D = 1024
S = 256
T = S // P
KB = D // P
EPS = 1e-6
NEG = -1e30
GROUPS = 3
HEAD = 128
ROT = 32
HG = 2
FF = 2816
FFE = 3584
EXPERTS = 8
RH = 64
RQ = 256
NQ = D // RQ
RHD = D // RH
LORA = 64
GN_EPS = 64e-5
DECAY = math.exp(-0.5)
BLK = 16

SLOT = 4096
R = 6
U_QKV = 18
U_AWO = 2
U_FF = 17
U_RKV = 6
U_BWO = 2
U_DENSE = U_QKV + U_AWO + U_FF + U_RKV + U_BWO
U_EXPERT = 21
GE = FFE // 256
OVER = 3

C_ID = 0
C_FREQ = C_ID + P
C_TRI = C_FREQ + 16
C_TIE = C_TRI + 8 * P
C_HALF = C_TIE + 64
C_ROW = C_HALF + 2
C_CEN = C_ROW + P
C_ALL = C_CEN + 4 * P
U16, UOFF, L16, LOFF, UI, US, LI, LS = range(8)


def constants():
    c = np.zeros((P, C_ALL), np.float32)
    mask = np.zeros((P, T * 512), np.float32)
    c[:, C_ID:C_ID + P] = np.eye(P)
    where = np.arange(S)
    token = (where % 16) * 16 + where // 64 + 4 * ((where // 16) % 4)
    for t in range(T):
        own = token[t * P:(t + 1) * P]
        near = np.abs(own[:, None] - token[None, :]) <= 64
        four = (own[:, None] - own[None, :]) % 4 == 0
        sixteen = (own[:, None] - own[None, :]) % 16 == 0
        mask[:, t * 512:(t + 1) * 512] = np.where(np.concatenate([near, four, sixteen], 1), 0.0, NEG)
    c[:, C_FREQ:C_FREQ + 16] = (np.float32(500000.0) ** (-np.arange(0, ROT, 2, dtype=np.float32) / np.float32(ROT)))[None]
    i = np.arange(P)
    r, q = i[:, None], i[None, :]
    same = r // BLK == q // BLK
    for n, m in enumerate([(r < q) & same, (r < q) & ~same, (r > q) & same, (r > q) & ~same, r <= q, r < q, r >= q, r > q]):
        c[:, C_TRI + n * P:C_TRI + (n + 1) * P] = m
    e = np.arange(8)
    c[:, C_TIE:C_TIE + 64] = (e[None, :] < e[:, None]).reshape(1, 64)
    c[:, C_HALF] = i < P // 2
    c[:, C_HALF + 1] = i >= P // 2
    c[:, C_ROW:C_ROW + P] = i[None, :]
    first, last = (i < P // 2)[:, None].astype(np.float32), (i >= P // 2)[:, None].astype(np.float32)
    for n, m in enumerate([(r <= q) - first, (r < q) - first, (r >= q) - last, (r > q) - last]):
        c[:, C_CEN + n * P:C_CEN + (n + 1) * P] = m
    return c, mask


class Steps:

    def __init__(self, eng, sem):
        self.eng, self.sem, self.n, self.off = eng, sem, 0, 0

    def link(self, ins):
        self.n += 1
        ins.then_inc(self.sem, 1)
        self.eng.wait_ge(self.sem, self.off + self.n)

    @contextmanager
    def repeated(self, i, times, each):
        start, self.off = self.n, i * each
        yield
        assert self.n - start == each, f"links in a turn: {self.n - start}"
        self.n, self.off = start + each * times, 0


def expert_plan(first):
    order, u = [], first
    for g in range(GE):
        order.append(("up", g, u)); u += 1
        if g >= 3 and g % 2:
            order.append(("down", (g - 3) // 2, u)); u += 1
    order.append(("down", GE // 2 - 1, u))
    return order


def ff_plan(groups, first):
    order, u = [], first
    pairs = -(-groups // 2)
    for p in range(pairs):
        for g in range(2 * p, min(2 * p + 2, groups)):
            order.append(("up", g, u)); u += 1
        if p:
            order.append(("down", p - 1, u)); u += 1
    order.append(("down", pairs - 1, u))
    return order


def build(nc, x_in, pos_in, const_in, mask_in, vec_in, rows_in, qk_rows, qk_cols, wqkv, awo, wrkv, w0, w1, w2, a0, a1, a2,
          g1, g2, bwo, fw13, fw2, router, mw13, mw2, out):
    ctx = ExitStack()
    with ctx:
        arena = ctx.enter_context(nc.sbuf_tensor("arena", [P, 53200], F32))
        ps = ctx.enter_context(nc.psum_tensor("ps", [P, 8, 512], F32))

        def sem(name):
            return ctx.enter_context(nc.semaphore(name))

        class Region:

            def __init__(self, at, end):
                self.at, self.end = at, end

            def take(self, *shape, parts=P):
                n = math.prod(shape)
                v = arena[0:parts, self.at:self.at + n]
                self.at += n
                assert self.at <= self.end, (self.at, self.end)
                if len(shape) > 1:
                    names = "abcd"[:len(shape)]
                    v = v.rearrange(f"p ({' '.join(names)}) -> p {' '.join(names)}",
                                    **{n: s for n, s in zip(names, shape)})
                return v

        fixed = Region(0, 53200)
        ring = [fixed.take(SLOT) for _ in range(R)]
        x = fixed.take(T, D)
        const = fixed.take(C_ALL)
        vec = fixed.take(96)
        qkc = fixed.take(6)
        qkr = fixed.take(6, ROT)
        pos_i = fixed.take(T).bitcast(I32)
        stat = fixed.take(64)
        minus_half = fixed.take(2)
        union = fixed.at

        ident = const[:, C_ID:C_ID + P]

        def tri(n):
            return const[:, C_TRI + n * P:C_TRI + (n + 1) * P]

        m = Region(union, 53200)
        hT = m.take(KB, S)
        qT = m.take(GROUPS, 4, S)
        kT = m.take(GROUPS, 4, S)
        v = m.take(T, GROUPS, 512)
        attn = m.take(T, D)
        oT = m.take(KB, S)
        qn = m.take(2, 4, HEAD)
        sq = m.take(2, 512)
        rope_tmp = m.take(3, 4, ROT)
        probs = m.take(3, 512)
        pT = m.take(2, 4, P)
        cs = m.take(2, T, ROT)
        ang = m.take(4, T, 16)
        amask = m.take(T, 512)
        m = Region(union, 53200)
        assert m.take(KB, S).offset == hT.offset
        hid = m.take(2, 4, S)
        sg = m.take(2, S)
        xn = m.take(T, D)
        rw = m.take(KB, EXPERTS)
        logits = m.take(T, EXPERTS)
        chosen = m.take(T, EXPERTS)
        comb = m.take(T, EXPERTS + 1)
        place = m.take(T, EXPERTS + 1)
        place2 = m.take(T, EXPERTS)
        cmp_a = m.take(T, EXPERTS, EXPERTS)
        cmp_b = m.take(T, EXPERTS, EXPERTS)
        ones = m.take(P)
        full_e = m.take(4, EXPERTS)
        over_f = m.take(4)
        over_i = m.take(4).bitcast(I32)
        pick = m.take(2, T, P)
        pickT = m.take(2, T, P)
        picked = m.take(2, KB, P)
        hid_e = m.take(2, 256)
        sg_e = m.take(2, 256)
        hidT = m.take(2, 4, P)
        yb = m.take(D)
        m = Region(union, 53200)
        rkv = m.take(3, T, D)
        loraT = [m.take(S, parts=LORA + 1) for _ in range(4)]
        sgT = m.take(S)
        after_pre = m.at
        hR = m.take(KB, S)
        d_f = m.take(KB, S)
        d_b = m.take(KB, S)
        d_c = m.take(KB, S)
        mx = m.take(2, KB, S)
        lw1 = m.take(4, KB, LORA)
        lg1 = m.take(KB, P)
        m = Region(after_pre, 53200)
        lent0 = Region(0, SLOT)
        par_l, par_g, rows = [], [], []
        for region in (m, lent0):
            par_l.append(region.take(4, RQ, parts=LORA + 1))
            par_g.append(region.take(RQ))
            rows.append(region.take(5, RQ))
        gate = lent0.take(T, RQ)
        w_ = lent0.take(T, RQ)
        b_ = lent0.take(T, RQ)
        mixo = m.take(T, D)
        kkn = m.take(T, RQ)
        vq = m.take(T, RQ)
        half_power = m.take(8)
        y_sum = m.take(T, RQ)
        small = m.take(64)
        lent = Region(3 * SLOT, R * SLOT)

        def stream(m, lent):
            o = {}
            o["E"] = lent.take(T, 2, RQ)
            o["six"] = lent.take(2, 4, P)
            o["gm"] = lent.take(4, 4, P)
            o["sig"] = m.take(T, RQ)
            o["a"] = m.take(T, RQ)
            o["inv"] = lent.take(T, RQ)
            o["kt"] = lent.take(T, RQ)
            o["kd"] = lent.take(T, RQ)
            o["be"] = m.take(RQ)
            o["ke"] = m.take(RQ)
            o["AR"] = m.take(2, 2, P)
            o["BK"] = m.take(4, 2, P)
            o["z"] = [o["sig"][:, 0, :], o["sig"][:, 1, :], o["a"][:, 0, :]]
            o["DT"] = lent.take(4, P)
            for n in ("Mo", "G", "D2T"):
                o[n] = m.take(4, P)
            o["D"], o["D2"] = o["six"][:, 0], o["six"][:, 1]
            o["S0"] = m.take(4, RH)
            o["pm"] = m.take(2)
            return o

        st = [stream(m, lent), stream(m, lent)]
        moT = rkv[:, 1].rearrange("p t (u s) -> p (t u) s", s=S)

        slot_full = [sem(f"slot_full{i}") for i in range(R)]
        in_x, in_const, in_small, out_done = sem("in_x"), sem("in_const"), sem("in_small"), sem("out_done")
        dve_step, act_step, pool_step = sem("dve_step"), sem("act_step"), sem("pool_step")
        rms_ss, rms_ms, rms_rt, rms_xn, rms_tp, rms_h = (sem("rms_" + n) for n in ("ss", "ms", "rt", "xn", "tp", "h"))
        tables, qkgain = sem("tables"), sem("qkgain")
        proj_ready, proj_taken = sem("proj_ready"), sem("proj_taken")
        sq_ready, ms_ready, rt_ready, qn_ready, rope_ready = (sem(n) for n in ("sq_ready", "ms_ready", "rt_ready", "qn_ready", "rope_ready"))
        qkT_ps, qkT_sb = sem("qkT_ps"), sem("qkT_sb")
        sc_ps, masked, maxed, prob_rdy, pT_ps, pT_sb, o_ps, o_sb = (sem(n) for n in ("sc_ps", "masked", "maxed", "prob_rdy", "pT_ps", "pT_sb", "o_ps", "o_sb"))
        oT_ps, oT_sb = sem("oT_ps"), sem("oT_sb")
        wo_ps, x_done = sem("wo_ps"), sem("x_done")
        gu_ps, sg_sb, hid_sb, dn_ps, dn_taken = (sem(n) for n in ("gu_ps", "sg_sb", "hid_sb", "dn_ps", "dn_taken"))
        lg_ps, lg_sb, lg_ex = (sem(n) for n in ("lg_ps", "lg_sb", "lg_ex"))
        chosen_ok, place_ps, over_ok, zero_ok = (sem(n) for n in ("chosen_ok", "place_ps", "over_ok", "zero_ok"))
        pick_ok, pickT_ps, pickT_sb, picked_ps, picked_sb = (sem(n) for n in ("pick_ok", "pickT_ps", "pickT_sb", "picked_ps", "picked_sb"))
        up_ps, sge_sb, hide_sb, hidT_ps, hidT_sb, down_ps, y_sb, back_ps, back_sb = (
            sem(n) for n in ("up_ps", "sge_sb", "hide_sb", "hidT_ps", "hidT_sb", "down_ps", "result_sb", "back_ps", "back_sb"))
        experts_done = sem("experts_done")
        in_lora, d_ready, mix_ready, mix_ps, mix_sb, ones_ok = (sem(n) for n in ("in_lora", "d_ready", "mix_ready", "mix_ps", "mix_sb", "ones_ok"))
        rkv_ps, rkv_sb = sem("rkv_ps"), sem("rkv_sb")
        head_done = sem("head_done")
        in_par = [sem("in_par0"), sem("in_par1")]
        gate_ps, gn_ms, gn_rt, db_ready = (sem(n) for n in ("gate_ps", "gn_ms", "gn_rt", "db_ready"))

        class Pair:

            def __init__(self, name):
                self.ps, self.sb = sem(name + "_ps"), sem(name + "_sb")

        def turn(c, d, each=1):
            return c * (2 * each) + (d - 1) * each

        STAGES = ["za", "cum", "end", "tA", "tB", "X", "gm", "D2", "D2T", "D4", "D4T", "G2", "D8", "G3", "G4",
                  "E", "ET", "E2", "E2T", "E4T", "z0", "z1", "z2", "z3", "u", "y", "st"]
        stage = {n: Pair(n) for n in STAGES}
        ops_ok = [sem(f"ops_ok{d}") for d in range(2)]
        ke_ok = [sem(f"ke_ok{d}") for d in range(2)]
        g1_ok = [sem(f"g1_ok{d}") for d in range(2)]
        ex_ok = [sem(f"ex_ok{d}") for d in range(2)]
        in_router = sem("in_router")
        gate_sb, kk_ok, kd_ok, sum_ok = sem("gate_sb"), sem("kk_done"), sem("kd_done"), sem("sum_ok")
        bonus_ok = sem("bonus_ok")
        vq_ok, pad_ok = sem("vq_ok"), sem("pad_ok")
        block = ctx.enter_context(nc.Block())

        free = {}
        for u in range(U_QKV):
            free[u] = (proj_ready, 2 * u + 2)
        u0 = U_QKV
        for n in range(U_AWO):
            free[u0 + n] = (wo_ps, 2 * n + 2)
        u0 += U_AWO
        FF0 = u0
        plan0 = ff_plan(FF // 256, FF0)
        for kind, n, u in plan0:
            free[u] = (gu_ps, 2 * n + 2) if kind == "up" else (dn_ps, n + 1)
        free[plan0[-1][2]] = (dn_ps, plan0[-1][1] + 4)
        u0 += U_FF
        RKV0 = u0
        for n in range(U_RKV):
            free[u0 + n] = (rkv_ps, 2 * n + 2)
        u0 += U_RKV
        BWO0 = u0
        for n in range(U_BWO):
            free[u0 + n] = (wo_ps, 2 * (U_AWO + n) + 2)
        MOE0 = U_DENSE
        GU0, DN0 = 2 * (FF // 256), -(-FF // 512)
        plans = [expert_plan(MOE0), expert_plan(MOE0 + U_EXPERT)]

        def arrived(eng, u, rounds=0):
            eng.wait_ge(slot_full[u % R], rounds * 32 + (u // R + 1) * 32)

        def unit(u):
            return ring[u % R]

        free_e = {}
        for e in range(2):
            for kind, n, u in plans[e]:
                free_e[u] = (up_ps, e * GE + n + 1) if kind == "up" else (down_ps, e * GE // 2 + n + 1)
        per_turn = {up_ps: 2 * GE, down_ps: GE}

        def wait_free_e(sp, u, i):
            w = u - R
            if w < MOE0 and isinstance(i, int):
                s, n = free[w]
                sp.wait_ge(s, n)
                return
            back = 0
            if w < MOE0:
                w, back = w + 2 * U_EXPERT, 1
            s, n = free_e[w]
            for t, per in per_turn.items():
                if s is t:
                    sp.wait_ge(s, i * per + (n - back * per))

        over_plan = expert_plan(0)
        over_uses = [len([v for v in range(U_EXPERT) if v % R == r]) for r in range(R)]
        uses = [len([u for u in range(MOE0 + EXPERTS * U_EXPERT) if u % R == r]) for r in range(R)]

        @block.sync
        def _(sp):
            def halves(u, dst, src):
                for a, b in zip(dst, src):
                    sp.dma_start(a, b).then_inc(slot_full[u % R], 16)

            def square(u, w):
                s = unit(u).rearrange("p (k n) -> p k n", n=512)
                w = w.rearrange("(k p) n -> p k n", p=P)
                halves(u, (s[:, 0:4], s[:, 4:8]), (w[:, 0:4], w[:, 4:8]))

            def ff_unit(kind, u, w13, wd, ff, rows=512):
                if kind == "up":
                    s = unit(u).rearrange("p (k n) -> p k n", n=512)
                    halves(u, (s[:, :, 0:256], s[:, :, 256:512]), w13)
                else:
                    n = rows // P
                    s = unit(u)[:, 0:n * D].rearrange("p (k n) -> p k n", n=D)
                    halves(u, (s[:, 0:n // 2], s[:, n // 2:n]), (wd[:, 0:n // 2], wd[:, n // 2:n]))

            def wait_free(u):
                if u >= R:
                    s, n = free[u - R]
                    sp.wait_ge(s, n)

            sp.dma_start(x, x_in.rearrange("(t p) n -> p t n", p=P)).then_inc(in_x, 16)
            sp.dma_start(const, const_in).then_inc(in_const, 16)
            sp.dma_start(amask.rearrange("p t n -> p (t n)"), mask_in).then_inc(in_small, 16)
            sp.dma_start(vec, vec_in).then_inc(in_small, 16)
            sp.dma_start(qkc, qk_cols).then_inc(in_small, 16)
            sp.dma_start(qkr, qk_rows.partition_broadcast(P)).then_inc(in_small, 16)
            sp.dma_start(pos_i, pos_in).then_inc(in_small, 16)
            for u in range(U_QKV):
                hg, g, kind = u // 9, u % 9 // 3, u % 3
                col = (kind * GROUPS + g) * D + hg * 512
                wait_free(u)
                square(u, wqkv[:, col:col + 512])
            for n in range(U_AWO):
                wait_free(U_QKV + n)
                square(U_QKV + n, awo[:, n * 512:(n + 1) * 512])
            f13 = fw13.rearrange("(k p) n -> p k n", p=P)
            for kind, n, u in plan0:
                wait_free(u)
                c = n * 256
                r0, r1 = n * 512, min(n * 512 + 512, FF)
                if kind == "up":
                    ff_unit(kind, u, (f13[:, :, c:c + 256], f13[:, :, FF + c:FF + c + 256]), None, FF)
                else:
                    ff_unit(kind, u, None, fw2[r0:r1, :].rearrange("(k p) n -> p k n", p=P), FF, r1 - r0)
            sp.wait_ge(x_done, 4)
            for j, w in enumerate((w1[0], w1[1], a1[0], a1[1])):
                sp.dma_start(lw1[:, j], w.rearrange("(k p) n -> p k n", p=P)).then_inc(in_lora, 16)
            sp.dma_start(lg1, g1.rearrange("(k p) n -> p k n", p=P)).then_inc(in_lora, 16)
            for n in range(U_RKV):
                wait_free(RKV0 + n)
                square(RKV0 + n, wrkv[n // 2, :, (n % 2) * 512:(n % 2 + 1) * 512])
            def rest_unit(u):
                if u < MOE0:
                    square(u, bwo[:, (u - BWO0) * 512:(u - BWO0 + 1) * 512])
                else:
                    expert_unit(plan_e[u - MOE0], 0)

            plan_e = [(e, *a) for e in range(2) for a in plans[e]]

            def expert_unit(item, i):
                e, kind, n, u = item
                w13 = mw13[bass.ds(i * 2 + e, 1)].rearrange("e (k p) n -> p (e k) n", p=P)
                wd = mw2[bass.ds(i * 2 + e, 1)].rearrange("e (k p) n -> p (e k) n", p=P)
                c = n * 256
                if kind == "up":
                    ff_unit(kind, u, (w13[:, :, c:c + 256], w13[:, :, FFE + c:FFE + c + 256]), None, FFE)
                else:
                    ff_unit(kind, u, None, wd[:, 4 * n:4 * n + 4, :], FFE)

            sp.wait_ge(mix_ready, 8 * KB)
            for q in range(NQ):
                if q == 1:
                    sp.wait_ge(rkv_sb, 12)
                    sp.wait_ge(rkv_ps, 12)
                elif q >= 2:
                    sp.wait_ge(head_done, q)
                c, b = q * RQ, q % 2
                for j, (w, w_bias) in enumerate(((w2[0], w0[0]), (w2[1], w0[1]), (a2[0], a0[0]), (a2[1], a0[1]))):
                    sp.dma_start(par_l[b][0:LORA, j], w[:, c:c + RQ]).then_inc(in_par[b], 16)
                    sp.dma_start(par_l[b][LORA:LORA + 1, j], w_bias[c:c + RQ].unsqueeze(0)).then_inc(in_par[b], 16)
                sp.dma_start(par_g[b], g2[:, c:c + RQ]).then_inc(in_par[b], 16)
                sp.dma_start(rows[b], rows_in[:, c:c + RQ].partition_broadcast(P)).then_inc(in_par[b], 16)
            for u in range(BWO0, BWO0 + R):
                if u % R not in (1, 2):
                    sp.wait_ge(head_done, NQ + 1)
                wait_free(u)
                rest_unit(u)
            first = BWO0 + R - MOE0
            for item in plan_e[first:]:
                wait_free_e(sp, item[3], 0)
                expert_unit(item, 0)
            with sp.Fori(1, EXPERTS // 2) as i:
                for item in plan_e:
                    wait_free_e(sp, item[3], i)
                    expert_unit(item, i)
            sp.wait_ge(over_ok, 1)
            many = sp.value_load(over_i[0:1, 0:1], min_val=0, max_val=OVER)
            with sp.Fori(0, OVER) as j:
                with sp.If(j < many):
                    e = sp.value_load(over_i[0:1, bass.ds(j + 1, 1)], min_val=0, max_val=EXPERTS - 1)
                    w13 = mw13[bass.ds(e, 1)].rearrange("e (k p) n -> p (e k) n", p=P)
                    wd = mw2[bass.ds(e, 1)].rearrange("e (k p) n -> p (e k) n", p=P)
                    sp.wait_ge(down_ps, j * (GE // 2) + EXPERTS * GE // 2)
                    freed = [(up_ps, n + 1) if kind == "up" else (down_ps, n + 1) for kind, n, _ in over_plan]
                    for kind, n, u in over_plan:
                        if u >= R:
                            s, c = freed[u - R]
                            per = GE if s is up_ps else GE // 2
                            sp.wait_ge(s, j * per + (EXPERTS * per + c))
                        c = n * 256
                        if kind == "up":
                            ff_unit(kind, u, (w13[:, :, c:c + 256], w13[:, :, FFE + c:FFE + c + 256]), None, FFE)
                        else:
                            ff_unit(kind, u, None, wd[:, 4 * n:4 * n + 4, :], FFE)
            sp.wait_ge(experts_done, 1)
            sp.dma_start(out.rearrange("(t p) n -> p t n", p=P), x).then_inc(out_done, 16)
            sp.wait_ge(out_done, 16)

        @block.tensor
        def _(pe):
            mm = pe.matmul

            def run(o, pairs, **kw):
                for n, (a, b) in enumerate(pairs):
                    last = mm(o, a, b, start=(n == 0), stop=(n == len(pairs) - 1))
                return last

            def rms_transposes(n, src):
                pe.wait_ge(rms_xn, n * T + T)
                for b in range(4):
                    for f in range(2):
                        for t in range(T):
                            c = (2 * b + f) * P
                            last = pe.transpose(ps[:, b, f * S + t * P:f * S + (t + 1) * P], src[:, t, c:c + P], ident)
                    last.then_inc(rms_tp, 1)

            def back_transposes(src, bank0, done, wait):
                pe.wait_ge(*wait)
                for b in range(4):
                    for f in range(2):
                        for t in range(T):
                            c = (2 * b + f) * P
                            last = pe.transpose(ps[:, bank0 + b, f * S + t * P:f * S + (t + 1) * P], src[:, t, c:c + P], ident)
                    last.then_inc(done, 1)

            def out_projection(n0, u0, srcT, ready):
                pe.wait_ge(*ready)
                for n in range(2):
                    arrived(pe, u0 + n)
                    w = unit(u0 + n).rearrange("p (k n) -> p k n", n=512)
                    for t in range(T):
                        run(ps[:, 2 * n + t, :], [(srcT[:, k, t * P:(t + 1) * P], w[:, k, :]) for k in range(KB)]).then_inc(wo_ps, 1)

            def ff_units(plan, src, gu0, dn0, rounds, off_gu, off_dn, taken, last_rows):
                for kind, n, u in plan:
                    arrived(pe, u, rounds)
                    if kind == "up":
                        w = unit(u).rearrange("p (k n) -> p k n", n=512)
                        for f in range(2):
                            c = gu0 + 2 * n + f
                            if isinstance(off_gu, int) and c < 4:
                                pass
                            else:
                                pe.wait_ge(hid_sb, off_gu + (c - 3))
                            for side in range(2):
                                last = run(ps[:, c % 4, side * S:(side + 1) * S],
                                           [(w[:, k, side * S + f * P:side * S + (f + 1) * P], src[:, k, :]) for k in range(KB)])
                            last.then_inc(gu_ps, 1)
                    else:
                        rows = last_rows if (kind, n) == plan[-1][:2] else 512
                        w = unit(u)[:, 0:rows * D // P].rearrange("p (k n) -> p k n", n=D)
                        blocks = rows // P
                        pe.wait_ge(hid_sb, off_gu + (gu0 + 4 * n + blocks))
                        if n == 0:
                            pe.wait_ge(*taken)
                        for t in range(T):
                            for h in range(2):
                                for k in range(blocks):
                                    last = mm(ps[:, 4 + 2 * t + h, :], hid[:, n % 2, k, t * P:(t + 1) * P],
                                              w[:, k, h * 512:(h + 1) * 512], start=(n == 0 and k == 0),
                                              stop=((kind, n) == plan[-1][:2] and k == blocks - 1), skip_group_check=True)
                                if (kind, n) == plan[-1][:2] and (t, h) != (T - 1, 1):
                                    last.then_inc(dn_ps, 1)
                        last.then_inc(dn_ps, 1)

            pe.wait_ge(in_const, 16)
            rms_transposes(0, attn)
            pe.wait_ge(rms_h, 8)
            for hg in range(HG):
                def qk_transposes(j):
                    kind = j // 2 % 3
                    if kind < 2:
                        c = hg * 12 + (j // 6) * 4 + j % 6
                        pe.wait_ge(rope_ready, c + 1)
                        if c >= 2:
                            pe.wait_ge(qkT_sb, c - 1)
                        for h in range(4):
                            last = pe.transpose(ps[:, 2 + c % 2, h * P:(h + 1) * P], qn[:, c % 2, h, :], ident)
                        last.then_inc(qkT_ps, 1)

                for j in range(18):
                    u = hg * 9 + j // 2
                    c = hg * 18 + j
                    t = j % 2
                    if t == 0:
                        arrived(pe, u)
                    if c >= 2:
                        pe.wait_ge(proj_taken, c - 1)
                    w = unit(u).rearrange("p (k n) -> p k n", n=512)
                    run(ps[:, c % 2, :], [(hT[:, k, t * P:(t + 1) * P], w[:, k, :]) for k in range(KB)]).then_inc(proj_ready, 1)
                    if j:
                        qk_transposes(j - 1)

                pe.wait_ge(qkT_sb, hg * 12 + 12)
                pe.wait_ge(proj_taken, hg * 18 + 18)

                def scores(j):
                    h, t, c = j // 2, j % 2, hg * 8 + j
                    bank = (3, 4, 5)[c % 3]
                    if c >= 3:
                        pe.wait_ge(masked, c - 2)
                    q = slice(t * P, (t + 1) * P)
                    run(ps[:, bank, 0:S], [(qT[:, 0, h, q], kT[:, 0, h, :])])
                    run(ps[:, bank, S:S + P], [(qT[:, 1, h, q], kT[:, 1, h, q])])
                    run(ps[:, bank, S + P:512], [(qT[:, 2, h, q], kT[:, 2, h, q])]).then_inc(sc_ps, 1)

                scores(0)
                scores(1)
                for j in range(8):
                    h, t, c = j // 2, j % 2, hg * 8 + j
                    pe.wait_ge(prob_rdy, c + 1)
                    if c:
                        pe.wait_ge(pT_sb, c)
                    for b in range(4):
                        last = pe.transpose(ps[:, 6, b * P:(b + 1) * P], probs[:, c % 3, b * P:(b + 1) * P], ident)
                    last.then_inc(pT_ps, 1)
                    if j < 6:
                        scores(j + 2)
                    pe.wait_ge(pT_sb, c + 1)
                    if c >= 2:
                        pe.wait_ge(o_sb, c - 1)
                    hc = slice(h * HEAD, (h + 1) * HEAD)
                    run(ps[:, (7, 2)[c % 2], 0:HEAD], [(pT[:, c % 2, 0], v[:, 0, 0, hc]), (pT[:, c % 2, 1], v[:, 1, 0, hc]),
                                           (pT[:, c % 2, 2], v[:, t, 1, hc]), (pT[:, c % 2, 3], v[:, t, 2, hc])]).then_inc(o_ps, 1)
            back_transposes(attn, 0, oT_ps, (o_sb, 16))
            out_projection(0, U_QKV, oT, (oT_sb, 4))
            rms_transposes(1, attn)
            pe.wait_ge(rms_h, 16)
            ff_units(plan0, hT, 0, 0, 0, 0, 0, (rms_h, 16), FF % 512)
            rms_transposes(2, mx.rearrange("p a k s -> p a (k s)")[:, :, 0:D])
            pe.wait_ge(in_lora, 80)
            for j in range(8):
                if j < 5:
                    m_rows = LORA if j < 4 else P
                    w = lw1[:, (0, 2, 1, 3)[j]] if j < 4 else lg1
                    if j >= 2:
                        pe.wait_ge(mix_sb, j - 1)
                    for k in range(KB):
                        pe.wait_ge(mix_ready, j * KB + k + 1)
                        last = mm(ps[0:m_rows, j % 2, 0:S], w[:, k, :], mx[:, j % 2, k, :], start=k == 0, stop=k == KB - 1)
                    last.then_inc(mix_ps, 1)
                else:
                    pe.wait_ge(mix_ready, (j + 1) * KB)
                    for n in range(2):
                        u = RKV0 + 2 * (j - 5) + n
                        arrived(pe, u)
                        w = unit(u).rearrange("p (k n) -> p k n", n=512)
                        for t in range(T):
                            c = 4 * (j - 5) + 2 * n + t
                            if c >= 2:
                                pe.wait_ge(rkv_sb, c - 1)
                            run(ps[:, 2 + c % 2, :], [(mx[:, j % 2, k, t * P:(t + 1) * P], w[:, k, :]) for k in range(KB)]).then_inc(rkv_ps, 1)

            pe.wait_ge(mix_sb, 5)
            pe.wait_ge(rkv_sb, 12)
            def head_turn(q, b2, i):
                pe.wait_ge(in_par[b2], i * 160 + 160)
                for d in range(2):
                    b = 4 * d
                    for n in range(2):
                        for t in range(T):
                            last = run(ps[:, b + n, t * RQ:(t + 1) * RQ], [(loraT[2 * n + d][:, t * P:(t + 1) * P], par_l[b2][:, 2 * n + d, :])])
                    last.then_inc(stage["za"].ps, 1)
                for d in range(2):
                    b = 4 * d
                    o = st[d]
                    pe.wait_ge(stage["za"].sb, turn(q + 1, d, 2))
                    cen = [const[:, C_CEN + (2 * d + n) * P:C_CEN + (2 * d + n + 1) * P] for n in range(2)]
                    for t in range(T):
                        for n in range(2):
                            last = run(ps[:, b + 2 + t, n * RQ:(n + 1) * RQ], [(cen[n], o["sig"][:, t, :])])
                    last.then_inc(stage["cum"].ps, 1)
                    run(ps[:, b, 0:RQ], [(tri(LS if d == 0 else US), o["sig"][:, d, :])])
                    for pr in range(2):
                        last = run(ps[:, b, RQ + pr:RQ + pr + 1], [(o["sig"][:, 1 - d, pr * P:(pr + 1) * P], const[:, C_HALF + d:C_HALF + d + 1])])
                    last.then_inc(stage["end"].ps, 1)
                for s in range(2):
                    k = q * 2 + (s + 1)

                    def need(d, name):
                        pe.wait_ge(stage[name].sb, turn(k, d))

                    def four(d, name, bank, of, by, width=P):
                        for h in range(4):
                            last = run(ps[:, 4 * d + bank, h * width:(h + 1) * width], [(of[:, h, :], by(h))])
                        last.then_inc(stage[name].ps, 1)

                    def tile(d):
                        return s if d == 0 else 1 - s

                    def operands(d):
                        o, t, b = st[d], tile(d), 4 * d
                        pe.wait_ge(ops_ok[d], q * 4 + 4)
                        if s:
                            pe.wait_ge(stage["st"].sb, turn(q + 1, d, 4))
                        for pr in range(2):
                            c = slice(pr * P, (pr + 1) * P)
                            pe.transpose(ps[:, b, (2 * pr) * P:(2 * pr + 1) * P], o["E"][:, t, 1, c], ident)
                            last = pe.transpose(ps[:, b, (2 * pr + 1) * P:(2 * pr + 2) * P], o["E"][:, t, 0, c], ident)
                        last.then_inc(stage["tA"].ps, 1)
                        for pr in range(2):
                            c = slice(pr * P, (pr + 1) * P)
                            pe.transpose(ps[:, b + 1, (2 * pr) * P:(2 * pr + 1) * P], o["inv"][:, t, c], ident)
                            last = pe.transpose(ps[:, b + 1, (2 * pr + 1) * P:(2 * pr + 2) * P], o["kt"][:, t, c], ident)
                        last.then_inc(stage["tB"].ps, 1)

                    def system(d):
                        o, b = st[d], 4 * d
                        need(d, "tA")
                        pe.wait_ge(stage["tB"].sb, turn(k, d, 2))
                        for h in range(4):
                            last = run(ps[:, b + 2, h * P:(h + 1) * P], [(o["AR"][:, h // 2, 0, :], o["BK"][:, h, 0, :])])
                        last.then_inc(stage["X"].ps, 1)

                    def pairings(h, d):
                        o, b = st[d], 4 * d
                        bank = b + (3, 0, 1, 3)[h]
                        if h == 0 and s:
                            pe.wait_ge(stage["y"].sb, turn(k - 1, d))
                        if h == 3:
                            pe.wait_ge(stage["gm"].sb, q * 16 + (8 * s + d + 1))
                        ar = o["AR"][:, h // 2].rearrange("p a b -> p (a b)")
                        run(ps[:, bank, 0:2 * P], [(o["BK"][:, h, 0, :], ar)])
                        run(ps[:, bank, 2 * P:4 * P], [(o["BK"][:, h, 1, :], ar)]).then_inc(stage["gm"].ps, 1)

                    operands(0)
                    if s == 0:
                        system(0)
                        pairings(0, 0)
                        operands(1)
                    else:
                        operands(1)
                        system(0)
                    system(1)
                    for h in range(4):
                        for d in range(2):
                            if not (s == 0 and h == 0 and d == 0):
                                pairings(h, d)
                    for d in range(2):
                        o = st[d]
                        pe.wait_ge(stage["X"].sb, turn(k, d, 2))
                        pe.wait_ge(stage["gm"].sb, q * 16 + (8 * s + d + 7))
                        four(d, "D2", 0, o["DT"], lambda h: o["D"][:, h, :])
                        four(d, "D2T", 1, o["D"], lambda h: o["DT"][:, h, :])
                    for d in range(2):
                        o = st[d]
                        need(d, "D2"); need(d, "D2T")
                        pe.wait_ge(g1_ok[d], k)
                        four(d, "D4", 2, o["D2T"], lambda h: o["D2"][:, h, :])
                        four(d, "D4T", 3, o["D2"], lambda h: o["D2T"][:, h, :])
                        four(d, "G2", 0, o["D2"], lambda h: o["G"][:, h, :])
                    for d in range(2):
                        o = st[d]
                        need(d, "D4"); need(d, "D4T")
                        four(d, "D8", 1, o["DT"], lambda h: o["D"][:, h, :])
                        need(d, "G2")
                        four(d, "G3", 2, o["D"], lambda h: o["G"][:, h, :])
                    for d in range(2):
                        o = st[d]
                        need(d, "D8"); need(d, "G3")
                        four(d, "G4", 3, o["D2"], lambda h: o["G"][:, h, :])
                    for d in range(2):
                        o = st[d]
                        need(d, "G4")
                        four(d, "E", 0, o["G"], lambda h: o["Mo"][:, h, :])
                        four(d, "ET", 1, o["Mo"], lambda h: o["G"][:, h, :])
                    for d in range(2):
                        o = st[d]
                        need(d, "E"); need(d, "ET")
                        four(d, "E2", 2, o["D"], lambda h: o["D2T"][:, h, :])
                        four(d, "E2T", 3, o["D2T"], lambda h: o["D"][:, h, :])
                    for d in range(2):
                        o = st[d]
                        need(d, "E2"); need(d, "E2T")
                        four(d, "E4T", 0, o["DT"], lambda h: o["Mo"][:, h, :])

                    def value(t, h):
                        return vq[:, t, h * RH:(h + 1) * RH]

                    pe.wait_ge(vq_ok, q + 1)
                    for d in range(2):
                        o, t = st[d], tile(d)
                        for h in range(4):
                            pairs = [(o["gm"][:, h, 2, :], value(t, h))]
                            if s:
                                pairs.append((o["AR"][:, h // 2, 0, :], o["S0"][:, h, :]))
                            last = run(ps[:, 4 * d + 1, h * RH:(h + 1) * RH], pairs)
                        last.then_inc(stage["z0"].ps, 1)
                    for name, bank, of, src, before in (("z1", 2, "G", 0, "z0"), ("z2", 3, "D", 1, "z1"),
                                                        ("z3", 1, "Mo", 2, "z2"), ("u", 2, "D2", 0, "z3")):
                        for d in range(2):
                            o = st[d]
                            need(d, before)
                            if name == "u":
                                need(d, "E4T")
                            four(d, name, bank, o[of], lambda h: o["z"][src][:, h * RH:(h + 1) * RH], RH)
                    for d in range(2):
                        o, t = st[d], tile(d)
                        need(d, "u")
                        if s and d == 0:
                            for t2 in range(T):
                                last = run(ps[:, 0, t2 * RQ:(t2 + 1) * RQ], [(sgT[:, t2 * P:(t2 + 1) * P], par_g[b2])])
                            last.then_inc(gate_ps, 1)
                        for h in range(4):
                            u = o["z"][1][:, h * RH:(h + 1) * RH]
                            pairs = [(o["gm"][:, h, 3, :], value(t, h)), (o["gm"][:, h, 1, :], u)]
                            if s:
                                pairs.append((o["AR"][:, h // 2, 1, :], o["S0"][:, h, :]))
                            last = run(ps[:, 4 * d + 3, h * RH:(h + 1) * RH], pairs)
                        last.then_inc(stage["y"].ps, 1)
                        if not s:
                            pe.wait_ge(ke_ok[d], q * 2 + 2)
                            for h in range(4):
                                pr, r = h // 2, slice(h % 2 * RH, h % 2 * RH + RH)
                                c = slice(h * RH, (h + 1) * RH)
                                last = run(ps[r, 4 * d, pr * RH:(pr + 1) * RH],
                                           [(o["ke"][:, c], value(t, h)), (o["be"][:, c], o["z"][1][:, c])])
                            last.then_inc(stage["st"].ps, 1)
                pe.wait_ge(gate_sb, q + 1)
                pe.wait_ge(stage["y"].sb, turn(q * 2 + 2, 1))
            with pe.Fori(0, NQ // 2) as i:
                for b2 in range(2):
                    head_turn(i * 2 + b2, b2, i)
            def mix_transposes(b):
                for f in range(2):
                    for t in range(T):
                        c = (2 * b + f) * P
                        last = pe.transpose(ps[:, b, f * S + t * P:f * S + (t + 1) * P], mixo[:, t, c:c + P], ident)
                last.then_inc(oT_ps, 1)

            w = [unit(BWO0 + n).rearrange("p (k n) -> p k n", n=512) for n in range(2)]
            for n in range(2):
                arrived(pe, BWO0 + n)
            for b in range(4):
                if b in (0, 3):
                    pe.wait_ge(head_done, NQ + b // 3)
                mix_transposes(b)
                for b in ((b - 1,) if b in (1, 2) else (2, 3) if b == 3 else ()):
                    pe.wait_ge(oT_sb, 5 + b)
                    for n in range(2):
                        for t in range(T):
                            for k in (2 * b, 2 * b + 1):
                                last = mm(ps[:, 4 + 2 * n + t, :], moT[:, k, t * P:(t + 1) * P], w[n][:, k, :],
                                          start=(k == 0), stop=(k == KB - 1))
                            if b == 3:
                                last.then_inc(wo_ps, 1)
            rms_transposes(3, xn)
            pe.wait_ge(rms_h, 32)
            pe.wait_ge(in_router, 16)
            for t in range(T):
                last = run(ps[:, 4, t * EXPERTS:(t + 1) * EXPERTS], [(hT[:, k, t * P:(t + 1) * P], rw[:, k, :]) for k in range(KB)])
            last.then_inc(lg_ps, 1)
            pe.wait_ge(chosen_ok, 1)
            run(ps[:, 5, 0:EXPERTS], [(tri(US), chosen[:, 0, :])])
            run(ps[:, 5, EXPERTS:2 * EXPERTS], [(tri(US), chosen[:, 1, :]), (ones, chosen[:, 0, :])])
            run(ps[:, 5, 2 * EXPERTS:3 * EXPERTS], [(ones, chosen[:, 0, :]), (ones, chosen[:, 1, :])]).then_inc(place_ps, 1)
            pe.wait_ge(zero_ok, 1)

            def gather(c, b):
                pe.wait_ge(pick_ok, c * 2)
                if not isinstance(c, int):
                    pe.wait_ge(back_sb, c * 4 - 4)
                for t in range(T):
                    last = pe.transpose(ps[:, 4, t * P:(t + 1) * P], pick[:, b, t, :], ident)
                last.then_inc(pickT_ps, 1)
                gather_half(c, b, 0)

            def gather_half(c, b, half):
                if half:
                    pe.wait_ge(pickT_sb, c)
                for k in range(4):
                    f = (4 * half + k) * P
                    last = run(ps[:, (7, 4)[half], k * P:(k + 1) * P], [(xn[:, t, f:f + P], pick[:, b, t, :]) for t in range(T)])
                last.then_inc(picked_ps, 1)

            def scatter(c, b):
                pe.wait_ge(y_sb, c * 2)
                pe.wait_ge(picked_sb, c * 2)
                for n in range(4):
                    t, h = n // 2, n % 2
                    if n >= 2:
                        pe.wait_ge(back_sb, c * 4 + (n - 5))
                    run(ps[:, (4, 7)[n % 2], :], [(pickT[:, b, t, :], yb[:, h * 512:(h + 1) * 512])]).then_inc(back_ps, 1)

            def expert(n, c, b, plan, landed, at_second=None, before_last=None):
                pe.wait_ge(picked_sb, c * 2)

                def hidden(g):
                    pe.wait_ge(hide_sb, n * GE + (g + 1))
                    if g:
                        pe.wait_ge(hidT_sb, n * GE + g)
                    for f in range(2):
                        at = g % 2 * 256 + f * P
                        last = pe.transpose(ps[:, 3, at:at + P], hid_e[:, g % 2, f * P:(f + 1) * P], ident)
                    last.then_inc(hidT_ps, 1)

                for kind, g, u in plan:
                    if kind == "down" and g == GE // 2 - 1:
                        if before_last:
                            before_last[0]()
                        hidden(GE - 1)
                        if before_last:
                            before_last[1]()
                    landed(u)
                    if kind == "up":
                        w = unit(u).rearrange("p (k n) -> p k n", n=512)
                        if g >= 3:
                            pe.wait_ge(hide_sb, n * GE + (g - 2))
                        run(ps[:, g % 3, :], [(picked[:, b, k, :], w[:, k, :]) for k in range(KB)]).then_inc(up_ps, 1)
                        if g:
                            hidden(g - 1)
                        if g == 1 and at_second:
                            at_second()
                    else:
                        w = unit(u).rearrange("p (k n) -> p k n", n=D)
                        pe.wait_ge(hidT_sb, n * GE + (2 * g + 2))
                        if g == 0:
                            pe.wait_ge(y_sb, n * 2 + 2)
                        for h in range(2):
                            for k in range(4):
                                last = mm(ps[:, 5 + h, :], hidT[:, g % 2, k, :], w[:, k, h * 512:(h + 1) * 512],
                                          start=(g == 0 and k == 0), stop=(g == GE // 2 - 1 and k == 3), skip_group_check=True)
                        last.then_inc(down_ps, 1)

            gather(1, 0)
            gather_half(1, 0, 1)
            with pe.Fori(0, EXPERTS // 2) as i:
                for e in range(2):
                    n = i * 2 + e
                    expert(n, n + 1, e, plans[e], lambda u: arrived(pe, u, i * (2 * U_EXPERT // R)),
                           lambda: scatter(n + 1, 1 - e), (lambda: gather(n + 2, 1 - e), lambda: gather_half(n + 2, 1 - e, 1)))
            scatter(EXPERTS + 1, 1)
            pe.wait_ge(over_ok, 1)
            many = pe.value_load(over_i[0:1, 0:1], min_val=0, max_val=OVER)

            with pe.Fori(0, OVER) as j:
                with pe.If(j < many):
                    def landed(u):
                        pe.wait_ge(slot_full[u % R], j * (32 * over_uses[u % R]) + 32 * (uses[u % R] + u // R + 1))

                    n = j + EXPERTS
                    gather(n + 2, 0)
                    gather_half(n + 2, 0, 1)
                    expert(n, n + 2, 0, over_plan, landed)
                    scatter(n + 2, 0)

        @block.scalar
        def _(act):
            steps = Steps(act, act_step)

            def rms_squares(n, junk, added=None):
                for t in range(T):
                    if added:
                        act.wait_ge(added[0], added[1 + t])
                    if t:
                        act.wait_ge(rms_ss, n * T + t)
                    act.activation(junk, x[:, t, :], ACT.Square, accum_out=stat[:, 4 * n + t:4 * n + t + 1]).then_inc(rms_ss, 1)

            def ff_gates(groups, gu0, off):
                for c in range(gu0, gu0 + 2 * groups):
                    act.wait_ge(gu_ps, off + (c + 1))
                    if not (isinstance(off, int) and c < 2):
                        act.wait_ge(hid_sb, off + (c - 1))
                    act.activation(sg[:, c % 2, :], ps[:, c % 4, 0:S], ACT.Silu).then_inc(sg_sb, 1)

            act.wait_ge(in_x, 16)
            rms_squares(0, probs[:, 0:2].rearrange("p a b -> p (a b)"))
            act.wait_ge(tables, 1)
            act.activation(cs[:, 1, :, 16:32], ang[:, 1], ACT.Sin).then_inc(tables, 1)
            act.activation(cs[:, 0, :, 0:16], ang[:, 2], ACT.Sin).then_inc(tables, 1)
            act.wait_ge(qkgain, 1)
            for hg in range(HG):
                def move(j):
                    kind, g, t = j // 2 % 3, j // 6, j % 2
                    if kind < 2:
                        c = hg * 12 + g * 4 + j % 6
                        act.wait_ge(qkT_ps, c + 1)
                        act.activation((qT, kT)[kind][:, g, :, t * P:(t + 1) * P],
                                       ps[:, 2 + c % 2, :].rearrange("p (h n) -> p h n", h=4), ACT.Copy,
                                       scale=qkc[:, kind * 3 + g:kind * 3 + g + 1]).then_inc(qkT_sb, 1)

                for j in range(18):
                    c = hg * 18 + j
                    if j // 2 % 3 < 2:
                        n = hg * 12 + (j // 6) * 4 + j % 6
                        act.wait_ge(proj_ready, c + 1)
                        if n >= 2:
                            act.wait_ge(ms_ready, n - 1)
                        act.activation(sq[:, n % 2, :], ps[:, c % 2, :], ACT.Square).then_inc(sq_ready, 1)
                        act.wait_ge(ms_ready, n + 1)
                        b = 16 + 8 * (n % 2)
                        act.activation(stat[:, b + 4:b + 8], stat[:, b:b + 4], ACT.Sqrt).then_inc(rt_ready, 1)
                    if j:
                        move(j - 1)
                def exponentials(c):
                    act.wait_ge(maxed, c + 1)
                    b = 32 + 2 * (c % 3)
                    act.activation(probs[:, c % 3, :], probs[:, c % 3, :], ACT.Exp, bias=stat[:, b:b + 1],
                                   accum_out=stat[:, b + 1:b + 2]).then_inc(prob_rdy, 1)

                exponentials(hg * 8)
                for j in range(8):
                    c = hg * 8 + j
                    if j < 7:
                        exponentials(c + 1)
                    act.wait_ge(pT_ps, c + 1)
                    act.activation(pT[:, c % 2].rearrange("p a b -> p (a b)"), ps[:, 6, :], ACT.Copy).then_inc(pT_sb, 1)
            for b in range(4):
                act.wait_ge(oT_ps, b + 1)
                for f in range(2):
                    last = act.activation(oT[:, 2 * b + f, :].rearrange("p (l q r) -> p r q l", q=4, r=4),
                                          ps[:, b, f * S:(f + 1) * S].rearrange("p (r q l) -> p r q l", r=4, q=4), ACT.Copy)
                last.then_inc(oT_sb, 1)
            rms_squares(1, probs[:, 0:2].rearrange("p a b -> p (a b)"), (x_done, 3, 4))
            ff_gates(FF // 256, 0, 0)
            rms_squares(2, d_f.rearrange("p k s -> p (k s)")[:, 0:D], (dn_taken, 2, 4))
            for j in range(5):
                act.wait_ge(mix_ps, j + 1)
                m_rows = LORA if j < 4 else P
                dst = loraT[(0, 2, 1, 3)[j]][0:LORA, :] if j < 4 else sgT
                f = (ACT.Tanh, ACT.Copy, ACT.Tanh, ACT.Copy, ACT.Sigmoid)[j]
                act.activation(dst, ps[0:m_rows, j % 2, 0:S], f).then_inc(mix_sb, 1)
            for c in range(12):
                act.wait_ge(rkv_ps, c + 1)
                act.activation(rkv[:, c // 4, c % 2, (c // 2 % 2) * 512:(c // 2 % 2 + 1) * 512], ps[:, 2 + c % 2, :], ACT.Copy).then_inc(rkv_sb, 1)
            act.wait_ge(pad_ok, 4)
            def head_turn(q):
                for d in range(2):
                    o, b = st[d], 4 * d
                    act.wait_ge(stage["za"].ps, turn(q + 1, d))
                    for n, name in enumerate(("sig", "a")):
                        act.activation(o[name].rearrange("p t n -> p (t n)"), ps[:, b + n, :], ACT.Sigmoid).then_inc(stage["za"].sb, 1)
                for d in range(2):
                    o, b = st[d], 4 * d
                    act.wait_ge(stage["cum"].ps, turn(q + 1, d))
                    for t in range(T):
                        act.activation(o["E"][:, t].rearrange("p a n -> p (a n)"), ps[:, b + 2 + t, :], ACT.Exp, scale=-DECAY).then_inc(ex_ok[d], 1)
                        act.activation(o["inv"][:, t, :], ps[:, b + 2 + t, 0:RQ], ACT.Exp, scale=DECAY).then_inc(ex_ok[d], 1)
                    act.wait_ge(stage["end"].ps, turn(q + 1, d))
                    act.activation(o["be"], ps[:, b, 0:RQ], ACT.Exp, scale=-DECAY).then_inc(ex_ok[d], 1)
                    act.activation(o["pm"], ps[:, b, RQ:RQ + 2], ACT.Exp, scale=-DECAY).then_inc(ex_ok[d], 1)
                for s in range(2):
                    k = q * 2 + (s + 1)

                    def out_of(d, name, bank, dst, width=512):
                        act.wait_ge(stage[name].ps, turn(k, d))
                        act.activation(dst, ps[:, 4 * d + bank, 0:width], ACT.Copy).then_inc(stage[name].sb, 1)

                    for d in range(2):
                        out_of(d, "tA", 0, st[d]["AR"].rearrange("p a b c -> p (a b c)"))
                        act.wait_ge(stage["tB"].ps, turn(k, d))
                        for f in range(2):
                            r = slice(f * RH, f * RH + RH)
                            act.activation(st[d]["BK"][r, f::2].rearrange("p a b c -> p a (b c)"),
                                           ps[r, 4 * d + 1, :].rearrange("p (a n) -> p a n", a=2), ACT.Copy).then_inc(stage["tB"].sb, 1)
                    for names in ((("D2", 0, "D2"), ("D2T", 1, "D2T")), (("D4", 2, "D"), ("D4T", 3, "DT")), (("D8", 1, "D2"),),
                                  (("E", 0, "D2T"), ("ET", 1, "D")), (("E2", 2, "DT"), ("E2T", 3, "Mo")), (("E4T", 0, "D2"),)):
                        for d in range(2):
                            for name, bank, dst in names:
                                out_of(d, name, bank, st[d][dst].rearrange("p a b -> p (a b)"))
                    for name, bank, n in (("z0", 1, 0), ("z1", 2, 1)):
                        for d in range(2):
                            out_of(d, name, bank, st[d]["z"][n], RQ)
                act.wait_ge(gate_ps, q + 1)
                act.wait_ge(head_done, q + 1)
                act.activation(gate.rearrange("p t n -> p (t n)"), ps[:, 0, :], ACT.Copy).then_inc(gate_sb, 1)

            with act.Fori(0, NQ // 2) as i:
                for b2 in range(2):
                    head_turn(i * 2 + b2)
            for b in range(4):
                act.wait_ge(oT_ps, 5 + b)
                act.activation(moT[:, 2 * b:2 * b + 2, :].rearrange("p a s -> p (a s)"), ps[:, b, :], ACT.Copy).then_inc(oT_sb, 1)
            rms_squares(3, d_b.rearrange("p k s -> p (k s)")[:, 0:D], (x_done, 7, 8))
            act.wait_ge(lg_sb, 1)
            act.activation(logits.rearrange("p a b -> p (a b)"), logits.rearrange("p a b -> p (a b)"), ACT.Exp).then_inc(lg_ex, 1)

            def pickT_out(c, b):
                act.wait_ge(pickT_ps, c)
                act.activation(pickT[:, b].rearrange("p t n -> p (t n)"), ps[:, 4, 0:S], ACT.Copy).then_inc(pickT_sb, 1)

            def expert(n, before_last=None):
                def hidT_out(g):
                    act.wait_ge(hidT_ps, n * GE + (g + 1))
                    act.activation(hidT[:, g // 2 % 2, g % 2 * 2:g % 2 * 2 + 2, :].rearrange("p a b -> p (a b)"),
                                   ps[:, 3, g % 2 * 256:g % 2 * 256 + 256], ACT.Copy).then_inc(hidT_sb, 1)

                for g in range(GE):
                    act.wait_ge(up_ps, n * GE + (g + 1))
                    if g >= 2:
                        act.wait_ge(hide_sb, n * GE + (g - 1))
                    act.activation(sg_e[:, g % 2, :], ps[:, g % 3, 0:256], ACT.Silu).then_inc(sge_sb, 1)
                    if g:
                        hidT_out(g - 1)
                if before_last:
                    before_last()
                hidT_out(GE - 1)
                act.wait_ge(down_ps, n * (GE // 2) + GE // 2)
                act.activation(yb[:, 0:512], ps[:, 5, :], ACT.Copy).then_inc(y_sb, 1)

            pickT_out(1, 0)
            with act.Fori(0, EXPERTS // 2) as i:
                for e in range(2):
                    n = i * 2 + e
                    expert(n, lambda: pickT_out(n + 2, 1 - e))
            act.wait_ge(over_ok, 1)
            many = act.value_load(over_i[0:1, 0:1], min_val=0, max_val=OVER)
            with act.Fori(0, OVER) as j:
                with act.If(j < many):
                    pickT_out(j + (EXPERTS + 2), 0)
                    expert(j + EXPERTS)

        @block.vector
        def _(dve):
            steps = Steps(dve, dve_step)
            link = steps.link

            def attend(hg, j, c):
                h, t = j // 2, j % 2
                b = 32 + 2 * (c % 3)
                dve.wait_ge(prob_rdy, c + 1)
                link(dve.reciprocal(stat[:, b + 1:b + 2], stat[:, b + 1:b + 2]))
                dve.wait_ge(o_ps, c + 1)
                col = hg * 512 + h * HEAD
                dve.tensor_scalar(attn[:, t, col:col + HEAD], ps[:, (7, 2)[c % 2], 0:HEAD], stat[:, b + 1:b + 2], None, ALU.mult).then_inc(o_sb, 1)

            def rms_rest(n, xn, gain, dst, permuted=False):
                dve.wait_ge(rms_ss, n * T + T)
                dve.tensor_scalar(stat[:, 4 * n:4 * n + 2], stat[:, 4 * n:4 * n + 2], 1.0 / D, EPS, ALU.mult, ALU.add).then_inc(rms_ms, 1)
                dve.wait_ge(rms_rt, n + 1)
                for t in range(T):
                    dve.tensor_scalar(xn[:, t, :], x[:, t, :], stat[:, 4 * n + 2 + t:4 * n + 3 + t], None, ALU.mult).then_inc(rms_xn, 1)
                for b in range(4):
                    dve.wait_ge(rms_tp, 4 * n + b + 1)
                    for f in range(2):
                        k = 2 * b + f
                        o, src = dst[:, k, :], ps[:, b, f * S:(f + 1) * S]
                        if permuted:
                            o = o.rearrange("p (r q l) -> p l q r", r=4, q=4)
                            src = src.rearrange("p (l q r) -> p l q r", q=4, r=4)
                        dve.tensor_scalar(o, src, vec[:, gain * KB + k:gain * KB + k + 1], None, ALU.mult).then_inc(rms_h, 1)

            def ff_products(groups, gu0, off, hid_of):
                for c in range(gu0, gu0 + 2 * groups):
                    dve.wait_ge(sg_sb, off + (c + 1))
                    n = c - gu0
                    w = hid_of + n // 4 - 1
                    if n % 4 == 0 and not (isinstance(off, int) and w < 1):
                        dve.wait_ge(dn_ps, off_dn(off, w))
                    dve.tensor_tensor(hid[:, n // 4 % 2, n % 4, :], sg[:, c % 2, :], ps[:, c % 4, S:2 * S], ALU.mult).then_inc(hid_sb, 1)

            def off_dn(off, w):
                return w if isinstance(off, int) else off[1] + w

            dve.wait_ge(in_x, 16)
            dve.wait_ge(in_small, 80)
            dve.wait_ge(in_const, 16)
            dve.memset(qkc[0:ROT, :], 1.0).then_inc(qkgain, 1)
            posf, turns = ang[:, 3, :, 0], ang[:, 0]
            link(dve.tensor_copy(posf, pos_i))
            link(dve.tensor_tensor(ang[:, 1], const[:, C_FREQ:C_FREQ + 16].unsqueeze(1).broadcast_to([P, T, 16]),
                                   posf.unsqueeze(2).broadcast_to([P, T, 16]), ALU.mult))
            whole = 1.5 * 2.0 ** 23
            link(dve.tensor_scalar(turns, ang[:, 1], 1.0 / (2.0 * math.pi), whole, ALU.mult, ALU.add))
            link(dve.tensor_scalar(turns, turns, whole, None, ALU.subtract))
            t1 = 6.28125
            t2 = float(np.float32(round((2.0 * math.pi - t1) * 2 ** 20) / 2 ** 20))
            t3 = 2.0 * math.pi - t1 - t2
            for part in (t1, t2, t3):
                link(dve.scalar_tensor_tensor(ang[:, 1], turns, -part, ang[:, 1], ALU.mult, ALU.add))
            link(dve.tensor_scalar(ang[:, 2], ang[:, 1], math.pi / 2, None, ALU.add))
            link(dve.tensor_scalar(turns, ang[:, 2], math.pi, -2.0 * math.pi, ALU.is_gt, ALU.mult))
            link(dve.tensor_tensor(ang[:, 2], ang[:, 2], turns, ALU.add))
            PI = 3.1415925
            dve.tensor_scalar(ang[:, 2], ang[:, 2], -PI, PI, ALU.max, ALU.min)
            link(dve.tensor_scalar(ang[:, 1], ang[:, 1], -PI, PI, ALU.max, ALU.min))
            dve.wait_ge(dve_step, steps.n)
            dve.memset(stat[:, 60:61], 0.0).then_inc(tables, 1)
            rms_rest(0, attn, 0, hT, permuted=True)
            dve.wait_ge(tables, 3)
            dve.tensor_copy(cs[:, 0, :, 16:32], cs[:, 0, :, 0:16]).then_inc(tables, 1)
            dve.tensor_scalar(cs[:, 1, :, 0:16], cs[:, 1, :, 16:32], -1.0, None, ALU.mult).then_inc(tables, 1)

            for hg in range(HG):
                for j in range(18):
                    c, kind, g, t = hg * 18 + j, j // 2 % 3, j // 6, j % 2
                    if kind < 2:
                        n = hg * 12 + g * 4 + j % 6
                        b = 16 + 8 * (n % 2)
                        dve.wait_ge(sq_ready, n + 1)
                        link(dve.tensor_reduce(stat[:, b:b + 4], sq[:, n % 2].rearrange("p (h d) -> p h d", h=4), AX, ALU.add))
                        dve.tensor_scalar(stat[:, b:b + 4], stat[:, b:b + 4], 1.0 / HEAD, EPS, ALU.mult, ALU.add).then_inc(ms_ready, 1)
                        dve.wait_ge(rt_ready, n + 1)
                        link(dve.reciprocal(stat[:, b + 4:b + 8], stat[:, b + 4:b + 8]))
                        if n >= 2:
                            dve.wait_ge(qkT_ps, n - 1)
                        dve.tensor_tensor(qn[:, n % 2], ps[:, c % 2, :].rearrange("p (h d) -> p h d", h=4),
                                          stat[:, b + 4:b + 8].unsqueeze(2).broadcast_to([P, 4, HEAD]), ALU.mult).then_inc(proj_taken, 1)
                    else:
                        dve.wait_ge(proj_ready, c + 1)
                        dve.tensor_copy(v[:, t, g, :], ps[:, c % 2, :]).then_inc(proj_taken, 1)

                for j in range(8):
                    h, t, c = j // 2, j % 2, hg * 8 + j
                    b = 32 + 2 * (c % 3)
                    dve.wait_ge(sc_ps, c + 1)
                    if c >= 3:
                        dve.wait_ge(pT_ps, c - 2)
                    dve.scalar_tensor_tensor(probs[:, c % 3, :], ps[:, (3, 4, 5)[c % 3], :], HEAD ** -0.5,
                                             amask[:, t, :], ALU.mult, ALU.add).then_inc(masked, 1)
                    dve.wait_ge(masked, c + 1)
                    link(dve.reduce_max(stat[:, b:b + 1], probs[:, c % 3, :], AX))
                    dve.tensor_scalar(stat[:, b:b + 1], stat[:, b:b + 1], -1.0, None, ALU.mult).then_inc(maxed, 1)
                    if j >= 2:
                        attend(hg, j - 2, c - 2)
                attend(hg, 6, hg * 8 + 6)
                attend(hg, 7, hg * 8 + 7)

            def add_to_x(n0, bank0):
                for n in range(4):
                    h, t = n // 2, n % 2
                    dve.wait_ge(wo_ps, n0 + n + 1)
                    dve.tensor_tensor(x[:, t, h * 512:(h + 1) * 512], x[:, t, h * 512:(h + 1) * 512], ps[:, bank0 + n, :], ALU.add).then_inc(x_done, 1)

            add_to_x(0, 0)
            dve.wait_ge(x_done, 4)
            rms_rest(1, attn, 2, hT)
            ff_products(FF // 256, 0, 0, 0)
            for t in range(T):
                for h in range(2):
                    dve.wait_ge(dn_ps, DN0 + 2 * t + h)
                    c = slice(h * 512, (h + 1) * 512)
                    dve.tensor_tensor(x[:, t, c], x[:, t, c], ps[:, 4 + 2 * t + h, :], ALU.add).then_inc(dn_taken, 1)
            dve.wait_ge(dn_taken, 4)
            rms_rest(2, mx.rearrange("p a k s -> p a (k s)")[:, :, 0:D], 1, hR)
            dve.wait_ge(rms_h, 24)
            dve.tensor_tensor(d_f[:, :, 1:S], hR[:, :, 0:S - 1], hR[:, :, 1:S], ALU.subtract).then_inc(d_ready, 1)
            dve.tensor_scalar(d_f[:, :, 0:1], hR[:, :, 0:1], -1.0, None, ALU.mult).then_inc(d_ready, 1)
            dve.wait_ge(d_ready, 2)
            for j, (mu, src) in enumerate(((4, d_f), (6, d_f), (5, d_b), (7, d_b), (3, d_c), (0, d_c), (1, d_c), (2, d_c))):
                if j == 2:
                    dve.wait_ge(db_ready, 2)
                if j == 4:
                    dve.tensor_tensor(d_c, d_f, d_b, ALU.add).then_inc(d_ready, 1)
                    dve.wait_ge(d_ready, 3)
                    dve.tensor_scalar(d_c, d_c, 0.5, None, ALU.mult).then_inc(d_ready, 1)
                    dve.wait_ge(d_ready, 4)
                if j == 2 or j == 3 or j == 4 or j == 5 or j == 6:
                    dve.wait_ge(mix_ps, j - 1)
                elif j == 7:
                    dve.wait_ge(rkv_ps, 4)
                for k in range(KB):
                    dve.scalar_tensor_tensor(mx[:, j % 2, k, :], src[:, k, :], vec[:, 32 + mu * KB + k:33 + mu * KB + k], hR[:, k, :],
                                             ALU.mult, ALU.add).then_inc(mix_ready, 1)
            dve.wait_ge(rkv_sb, 12)
            dve.wait_ge(rkv_ps, 12)

            dve.wait_ge(pad_ok, 4)

            def head_turn(q, b2, i):
                qs = bass.ds(q * RQ, RQ)
                dve.wait_ge(in_par[b2], i * 160 + 160)
                row = [rows[b2][:, n, :].unsqueeze(1).broadcast_to([P, T, RQ]) for n in range(5)]
                r_, k_, v_ = (rkv[:, n, :, qs] for n in range(3))

                dve.wait_ge(kk_ok, q + 1)
                dve.wait_ge(sum_ok, q + 1)
                for d in range(2):
                    o = st[d]
                    dve.wait_ge(stage["za"].sb, turn(q + 1, d, 2))
                    link(dve.scalar_tensor_tensor(o["kd"], o["a"], -1.0, row[1], ALU.add, ALU.mult))
                    dve.scalar_tensor_tensor(o["kd"], o["kd"], 1.0, k_, ALU.add, ALU.mult).then_inc(kd_ok, 1)
                    dve.wait_ge(kd_ok, q * 2 + (d + 1))
                    link(dve.tensor_tensor(o["a"], kkn, o["a"], ALU.mult))
                    dve.wait_ge(ex_ok[d], q * 6 + 6)
                    dve.tensor_tensor(o["E"][:, :, 0, :], o["E"][:, :, 0, :], r_, ALU.mult).then_inc(ops_ok[d], 1)
                    dve.scalar_tensor_tensor(o["E"][:, :, 1, :], kkn, -1.0, o["E"][:, :, 1, :], ALU.mult, ALU.mult).then_inc(ops_ok[d], 1)
                    dve.tensor_tensor(o["kt"], o["kd"], o["inv"], ALU.mult).then_inc(ops_ok[d], 1)
                    dve.tensor_tensor(o["inv"], o["a"], o["inv"], ALU.mult).then_inc(ops_ok[d], 1)
                for d in range(2):
                    o = st[d]
                    dve.tensor_tensor(o["ke"], o["kd"][:, d, :], o["be"], ALU.mult).then_inc(ke_ok[d], 1)
                    dve.tensor_tensor(o["be"], o["a"][:, d, :], o["be"], ALU.mult).then_inc(ke_ok[d], 1)
                for d in range(2):
                    dve.wait_ge(ke_ok[d], q * 2 + 2)
                dve.tensor_copy(vq, v_).then_inc(vq_ok, 1)
                for s in range(2):
                    k = q * 2 + (s + 1)

                    def bank(d, n, width=512):
                        return ps[:, 4 * d + n, 0:width]

                    def ready(d, name):
                        dve.wait_ge(stage[name].ps, turn(k, d))

                    def four(a):
                        return a.rearrange("p (h n) -> p h n", h=4)

                    def over(mask):
                        return tri(mask).unsqueeze(1).broadcast_to([P, 4, P])

                    for d in range(2):
                        o = st[d]
                        ready(d, "X")
                        dve.tensor_tensor(o["D"], four(bank(d, 2)), over((L16, U16)[d]), ALU.mult).then_inc(stage["X"].sb, 1)
                        dve.tensor_tensor(o["Mo"], four(bank(d, 2)), over((LOFF, UOFF)[d]), ALU.mult).then_inc(stage["X"].sb, 1)
                    for h in range(4):
                        for d in range(2):
                            o = st[d]
                            b = ps[:, 4 * d + (3, 0, 1, 3)[h], :].rearrange("p (a n) -> p a n", a=4)
                            dve.wait_ge(stage["gm"].ps, q * 16 + (8 * s + 2 * h + d + 1))
                            incl = tri((UI, LI)[d])
                            strict = tri((US, LS)[d])
                            dve.tensor_tensor(o["DT"][:, h, :], b[:, 0], tri((U16, L16)[d]), ALU.mult)
                            dve.tensor_tensor(o["gm"][:, h, 2, :], b[:, 2], strict, ALU.mult)
                            dve.tensor_tensor(o["gm"][:, h, 1::2, :], b[:, 1::2], incl.unsqueeze(1).broadcast_to([P, 2, P]), ALU.mult).then_inc(stage["gm"].sb, 1)
                    for d in range(2):
                        o = st[d]
                        dve.wait_ge(stage["gm"].sb, q * 16 + (8 * s + d + 7))
                        dve.tensor_tensor(o["G"], o["DT"], ident.unsqueeze(1).broadcast_to([P, 4, P]), ALU.add).then_inc(g1_ok[d], 1)
                    before = g1_ok
                    for name, b in (("G2", 0), ("G3", 2), ("G4", 3)):
                        for d in range(2):
                            o = st[d]
                            ready(d, name)
                            if before is g1_ok:
                                dve.wait_ge(g1_ok[d], k)
                            else:
                                dve.wait_ge(stage[before].sb, turn(k, d))
                            dve.tensor_tensor(o["G"], four(bank(d, b)), o["G"], ALU.add).then_inc(stage[name].sb, 1)
                        before = name
                    for name, b, src, dst, before in (("z2", 3, 1, 2, "z1"), ("z3", 1, 2, 0, "z2"), ("u", 2, 0, 1, "z3")):
                        for d in range(2):
                            o = st[d]
                            ready(d, name)
                            dve.wait_ge(stage[before].sb, turn(k, d))
                            dve.tensor_tensor(o["z"][dst], bank(d, b, RQ), o["z"][src], ALU.add).then_inc(stage[name].sb, 1)
                    for d in range(2):
                        o = st[d]
                        t = s if d == 0 else 1 - s
                        ready(d, "y")
                        if s:
                            dve.wait_ge(stage["y"].sb, turn(q * 2 + 1, 1 - d))
                            dve.tensor_tensor(y_sum[:, t, :], bank(d, 3, RQ), y_sum[:, t, :], ALU.add).then_inc(stage["y"].sb, 1)
                        else:
                            dve.wait_ge(head_done, q + 1)
                            dve.tensor_copy(y_sum[:, t, :], bank(d, 3, RQ)).then_inc(stage["y"].sb, 1)
                            dve.wait_ge(stage["st"].ps, turn(q + 1, d))
                            for h in range(4):
                                pr, r = h // 2, slice(h % 2 * RH, h % 2 * RH + RH)
                                dve.tensor_scalar(o["S0"][r, h, :], ps[r, 4 * d, pr * RH:(pr + 1) * RH], o["pm"][r, pr:pr + 1], None, ALU.mult).then_inc(stage["st"].sb, 1)

            with dve.Fori(0, NQ // 2) as i:
                with steps.repeated(i, NQ // 2, LINKS):
                    for b2 in range(2):
                        head_turn(i * 2 + b2, b2, i)
            q, y = NQ - 1, y_sum
            last_row = [rows[q % 2][:, n, :].unsqueeze(1).broadcast_to([P, T, RQ]) for n in range(5)]

            def heads(a):
                return a.rearrange("p t (h n) -> p t h n", n=RH)

            def per_head(n):
                return small[:, n:n + 8].rearrange("p (t h) -> p t h", t=T)

            def spread(n):
                return per_head(n).unsqueeze(3).broadcast_to([P, T, 4, RH])

            dve.wait_ge(head_done, NQ)
            dve.wait_ge(sum_ok, NQ + 1)
            dve.wait_ge(stage["y"].sb, turn(2 * NQ, 1))
            link(dve.tensor_reduce(per_head(16), heads(y), AX, ALU.add))
            link(dve.tensor_scalar(small[:, 16:24], small[:, 16:24], 1.0 / RH, None, ALU.mult))
            link(dve.tensor_tensor(heads(y), heads(y), spread(16), ALU.subtract))
            link(dve.tensor_tensor(w_, y, y, ALU.mult))
            link(dve.tensor_reduce(per_head(24), heads(w_), AX, ALU.add))
            dve.tensor_scalar(small[:, 24:32], small[:, 24:32], 1.0 / RH, GN_EPS, ALU.mult, ALU.add).then_inc(gn_ms, 1)
            dve.wait_ge(gn_rt, 1)
            link(dve.tensor_tensor(heads(y), heads(y), spread(32), ALU.mult))
            link(dve.tensor_tensor(y, y, last_row[3], ALU.mult))
            link(dve.tensor_tensor(y, y, last_row[4], ALU.add))
            link(dve.tensor_tensor(y, y, b_, ALU.add))
            dve.wait_ge(gate_sb, NQ)
            dve.tensor_tensor(mixo[:, :, q * RQ:(q + 1) * RQ], y, gate, ALU.mult).then_inc(head_done, 1)
            add_to_x(4, 4)
            dve.wait_ge(x_done, 8)
            rms_rest(3, xn, 3, hT)
            dve.wait_ge(lg_ps, 1)
            link(dve.tensor_copy(logits, ps[:, 4, 0:2 * EXPERTS].rearrange("p (t e) -> p t e", t=T)))
            other = logits.unsqueeze(2).broadcast_to([P, T, EXPERTS, EXPERTS])
            own = logits.unsqueeze(3).broadcast_to([P, T, EXPERTS, EXPERTS])
            tie = const[:, C_TIE:C_TIE + 64].rearrange("p (a b) -> p a b", a=8)
            link(dve.tensor_tensor(cmp_a, other, own, ALU.is_gt))
            link(dve.tensor_tensor(cmp_b, other, own, ALU.is_equal))
            for t in range(T):
                link(dve.tensor_tensor(cmp_b[:, t], cmp_b[:, t], tie, ALU.mult))
            link(dve.tensor_tensor(cmp_a, cmp_a, cmp_b, ALU.add))
            link(dve.tensor_reduce(chosen, cmp_a, AX, ALU.add))
            link(dve.tensor_scalar(chosen, chosen, 1.5, None, ALU.is_lt))
            dve.memset(ones, 1.0).then_inc(chosen_ok, 1)
            dve.memset(comb, 0.0)
            dve.memset(pickT[:, 1], 0.0).then_inc(zero_ok, 1)
            dve.memset(yb[:, 0:512], 0.0).then_inc(y_sb, 1)
            dve.memset(yb[:, 512:D], 0.0).then_inc(y_sb, 1)
            link(dve.memset(place, 4.0 * S))
            top = stat[:, 40:42]
            link(dve.tensor_reduce(top, logits, AX, ALU.max))
            dve.tensor_tensor(logits, logits, top.unsqueeze(2).broadcast_to([P, T, EXPERTS]), ALU.subtract).then_inc(lg_sb, 1)
            dve.wait_ge(lg_ex, 1)
            link(dve.tensor_tensor(logits, chosen, logits, ALU.mult))
            link(dve.tensor_reduce(top, logits, AX, ALU.add))
            link(dve.reciprocal(top, top))
            link(dve.tensor_tensor(comb[:, :, 1:EXPERTS + 1], logits, top.unsqueeze(2).broadcast_to([P, T, EXPERTS]), ALU.mult))
            dve.wait_ge(place_ps, 1)
            p8 = place[:, :, 0:EXPERTS]
            link(dve.tensor_scalar(p8, chosen, -4.0 * S, 4.0 * S, ALU.mult, ALU.add))
            link(dve.tensor_tensor(p8, ps[:, 5, 0:2 * EXPERTS].rearrange("p (t e) -> p t e", t=T), p8, ALU.add))
            link(dve.tensor_scalar(place2, p8, -float(P), None, ALU.add))
            link(dve.tensor_scalar(full_e[:, 0], ps[:, 5, 2 * EXPERTS:3 * EXPERTS], P + 0.5, None, ALU.is_gt))
            link(dve.tensor_tensor(cmp_b[:, 0], tie, full_e[:, 0].unsqueeze(1).broadcast_to([P, EXPERTS, EXPERTS]), ALU.mult))
            link(dve.tensor_reduce(full_e[:, 1], cmp_b[:, 0], AX, ALU.add))
            link(dve.tensor_reduce(over_f[:, 0:1], full_e[:, 0], AX, ALU.add))
            for j in range(OVER):
                link(dve.scalar_tensor_tensor(full_e[:, 2], full_e[:, 1], float(j), full_e[:, 0], ALU.is_equal, ALU.mult))
                link(dve.tensor_tensor(full_e[:, 3], full_e[:, 2], const[:, C_ROW:C_ROW + EXPERTS], ALU.mult))
                link(dve.tensor_reduce(over_f[:, j + 1:j + 2], full_e[:, 3], AX, ALU.add))
            dve.tensor_copy(over_i, over_f).then_inc(over_ok, 1)

            def choose(c, b, where):
                if not isinstance(c, int):
                    dve.wait_ge(picked_ps, c * 2 - 2)
                for t in range(T):
                    dve.tensor_scalar(pick[:, b, t, :], const[:, C_ROW:C_ROW + P], where(t), None, ALU.is_equal).then_inc(pick_ok, 1)

            def picked_out(c, b):
                for half, bank in ((0, 7), (1, 4)):
                    dve.wait_ge(picked_ps, c * 2 + (half - 1))
                    gain = vec[:, 3 * KB + 4 * half:3 * KB + 4 * half + 4].unsqueeze(2).broadcast_to([P, 4, P])
                    dve.tensor_tensor(picked[:, b, 4 * half:4 * half + 4, :], ps[:, bank, :].rearrange("p (k n) -> p k n", k=4), gain,
                                      ALU.mult).then_inc(picked_sb, 1)

            def add_back(c, weight):
                for n in range(4):
                    t, h = n // 2, n % 2
                    cols = slice(h * 512, (h + 1) * 512)
                    dve.wait_ge(back_ps, c * 4 + (n - 3))
                    dve.scalar_tensor_tensor(x[:, t, cols], ps[:, (4, 7)[n % 2], :], weight(t), x[:, t, cols], ALU.mult, ALU.add).then_inc(back_sb, 1)

            def expert(n, at_second=None, before_last=None):
                for g in range(GE):
                    dve.wait_ge(sge_sb, n * GE + (g + 1))
                    if g >= 2:
                        dve.wait_ge(hidT_ps, n * GE + (g - 1))
                    dve.tensor_tensor(hid_e[:, g % 2, :], sg_e[:, g % 2, :], ps[:, g % 3, 256:512], ALU.mult).then_inc(hide_sb, 1)
                    if g == 1 and at_second:
                        at_second()
                if before_last:
                    before_last()
                dve.wait_ge(down_ps, n * (GE // 2) + GE // 2)
                dve.tensor_copy(yb[:, 512:D], ps[:, 6, :]).then_inc(y_sb, 1)

            choose(1, 0, lambda t: place[:, t, 0:1])
            picked_out(1, 0)
            with dve.Fori(0, EXPERTS // 2) as i:
                for e in range(2):
                    n = i * 2 + e
                    choose(n + 2, 1 - e, lambda t: place[:, t, bass.ds(n + 1, 1)])
                    expert(n, lambda: add_back(n + 1, lambda t: comb[:, t, bass.ds(n, 1)]), lambda: picked_out(n + 2, 1 - e))
            add_back(EXPERTS + 1, lambda t: comb[:, t, EXPERTS:EXPERTS + 1])
            many = dve.value_load(over_i[0:1, 0:1], min_val=0, max_val=OVER)
            with dve.Fori(0, OVER) as j:
                with dve.If(j < many):
                    e = dve.value_load(over_i[0:1, bass.ds(j + 1, 1)], min_val=0, max_val=EXPERTS - 1)
                    c = j + (EXPERTS + 2)
                    choose(c, 0, lambda t: place2[:, t, bass.ds(e, 1)])
                    picked_out(c, 0)
                    expert(j + EXPERTS)
                    add_back(c, lambda t: comb[:, t, bass.ds(e + 1, 1)])
            dve.memset(over_f, 0.0).then_inc(experts_done, 1)

        @block.gpsimd
        def _(pool):
            n_step = 0

            def link(ins):
                nonlocal n_step
                n_step += 1
                ins.then_inc(pool_step, 1)
                pool.wait_ge(pool_step, n_step)

            def rms_power(n):
                pool.wait_ge(rms_ms, n + 1)
                pool.tensor_tensor(stat[:, 4 * n + 2:4 * n + 4], stat[:, 4 * n:4 * n + 2], minus_half, ALU.pow).then_inc(rms_rt, 1)

            link(pool.memset(minus_half, -0.5))
            rms_power(0)
            pool.wait_ge(tables, 5)
            pool.wait_ge(in_small, 80)
            for hg in range(HG):
                for j in range(18):
                    c, kind, g, t = hg * 18 + j, j // 2 % 3, j // 6, j % 2
                    if kind == 2:
                        continue
                    n = hg * 12 + g * 4 + j % 6
                    pool.wait_ge(proj_taken, c + 1)
                    q = qn[:, n % 2, :, 0:ROT]
                    a, b1, b2 = rope_tmp[:, 0], rope_tmp[:, 1], rope_tmp[:, 2]

                    def along(r):
                        return r.unsqueeze(1).broadcast_to([P, 4, r.shape[-1]])

                    link(pool.tensor_tensor(a, q, along(qkr[:, kind * 3 + g, :]), ALU.mult))
                    pool.tensor_tensor(b1, a, along(cs[:, 0, t, :]), ALU.mult)
                    pool.tensor_tensor(b2[:, :, 0:16], a[:, :, 16:32], along(cs[:, 1, t, 0:16]), ALU.mult)
                    link(pool.tensor_tensor(b2[:, :, 16:32], a[:, :, 0:16], along(cs[:, 1, t, 16:32]), ALU.mult))
                    pool.tensor_tensor(q, b1, b2, ALU.add).then_inc(rope_ready, 1)
            rms_power(1)
            pool.wait_ge(rms_rt, 2)
            for j in range(4):
                pool.memset(loraT[j][LORA:LORA + 1, :], 1.0).then_inc(ones_ok, 1)
                pool.wait_ge(ones_ok, j + 1)
            rms_power(2)
            pool.wait_ge(rms_h, 24)
            pool.tensor_tensor(d_b[:, :, 0:S - 1], hR[:, :, 1:S], hR[:, :, 0:S - 1], ALU.subtract).then_inc(db_ready, 1)
            pool.tensor_scalar(d_b[:, :, S - 1:S], hR[:, :, S - 1:S], -1.0, None, ALU.mult).then_inc(db_ready, 1)
            pool.wait_ge(rkv_ps, 12)
            for d in range(2):
                pool.memset(st[d]["BK"], 0.0).then_inc(pad_ok, 1)
                pool.memset(st[d]["S0"], 0.0).then_inc(pad_ok, 1)
            def heads(a):
                return a.rearrange("p t (h n) -> p t h n", n=RH)

            def per_head(n):
                return small[:, n:n + 8].rearrange("p (t h) -> p t h", t=T)

            def spread(n):
                return per_head(n).unsqueeze(3).broadcast_to([P, T, 4, RH])

            def add_up(n, src):
                v, width = heads(src), RH // 2
                while width > 1:
                    link(pool.tensor_tensor(v[:, :, :, 0:width], v[:, :, :, 0:width], v[:, :, :, width:2 * width], ALU.add))
                    width //= 2
                link(pool.tensor_tensor(per_head(n).unsqueeze(3), v[:, :, :, 0:1], v[:, :, :, 1:2], ALU.add))

            pool.memset(small, 0.0).then_inc(head_done, 1)
            pool.memset(half_power, -0.5).then_inc(sum_ok, 1)
            pool.wait_ge(sum_ok, 1)
            pool.wait_ge(rkv_sb, 12)

            def unit_kk(q):
                pool.wait_ge(in_par[q % 2], q // 2 * 160 + 160)
                if q:
                    for d in range(2):
                        pool.wait_ge(ke_ok[d], 2 * q)
                        pool.wait_ge(ops_ok[d], 4 * q)
                link(pool.tensor_tensor(kkn, rkv[:, 1, :, q * RQ:(q + 1) * RQ], rows[q % 2][:, 0, :].unsqueeze(1).broadcast_to([P, T, RQ]), ALU.mult))
                link(pool.tensor_tensor(w_, kkn, kkn, ALU.mult))
                add_up(0, w_)
                link(pool.tensor_scalar(small[:, 0:8], small[:, 0:8], 1e-24, None, ALU.max))
                link(pool.tensor_tensor(small[:, 8:16], small[:, 0:8], half_power, ALU.pow))
                pool.tensor_tensor(heads(kkn), heads(kkn), spread(8), ALU.mult).then_inc(kk_ok, 1)
                pool.wait_ge(kk_ok, q + 1)

            unit_kk(0)
            for q in range(NQ):
                row = [rows[q % 2][:, n, :].unsqueeze(1).broadcast_to([P, T, RQ]) for n in range(5)]
                qs = slice(q * RQ, (q + 1) * RQ)
                pool.wait_ge(kd_ok, 2 * q + 2)
                pool.tensor_tensor(b_, st[0]["kd"], st[1]["kd"], ALU.add).then_inc(bonus_ok, 1)
                pool.wait_ge(bonus_ok, q + 1)
                link(pool.tensor_tensor(b_, b_, rkv[:, 0, :, qs], ALU.mult))
                link(pool.tensor_tensor(b_, b_, row[2], ALU.mult))
                add_up(40, b_)
                for d in range(2):
                    pool.wait_ge(ke_ok[d], 2 * q + 2)
                pool.tensor_tensor(heads(b_), heads(rkv[:, 2, :, qs]), spread(40), ALU.mult).then_inc(sum_ok, 1)
                pool.wait_ge(sum_ok, q + 2)
                if q + 1 < NQ:
                    unit_kk(q + 1)
                else:
                    pool.wait_ge(gn_ms, 1)
                    pool.tensor_tensor(small[:, 32:40], small[:, 24:32], half_power, ALU.pow).then_inc(gn_rt, 1)
                    break
                for d in range(2):
                    pool.wait_ge(stage["y"].sb, turn(2 * q + 2, d))
                y = y_sum
                link(pool.tensor_copy(w_, y))
                add_up(16, w_)
                link(pool.tensor_scalar(small[:, 16:24], small[:, 16:24], 1.0 / RH, None, ALU.mult))
                link(pool.tensor_tensor(heads(y), heads(y), spread(16), ALU.subtract))
                link(pool.tensor_tensor(w_, y, y, ALU.mult))
                add_up(24, w_)
                link(pool.tensor_scalar(small[:, 24:32], small[:, 24:32], 1.0 / RH, GN_EPS, ALU.mult, ALU.add))
                link(pool.tensor_tensor(small[:, 32:40], small[:, 24:32], half_power, ALU.pow))
                link(pool.tensor_tensor(heads(y), heads(y), spread(32), ALU.mult))
                link(pool.tensor_tensor(y, y, row[3], ALU.mult))
                link(pool.tensor_tensor(y, y, row[4], ALU.add))
                link(pool.tensor_tensor(y, y, b_, ALU.add))
                pool.wait_ge(gate_sb, q + 1)
                pool.tensor_tensor(mixo[:, :, qs], y, gate, ALU.mult).then_inc(head_done, 1)
                pool.wait_ge(head_done, q + 2)
            pool.wait_ge(head_done, NQ + 1)
            pool.dma_start(rw, router.rearrange("(k p) n -> p k n", p=P)).then_inc(in_router, 16)
            rms_power(3)


LINKS = 8


def kernel(**inputs):
    import concourse.bacc as bacc
    from concourse.bass_utils import run_bass_kernel_spmd

    a = {n: np.asarray(v) for n, v in inputs.items()}

    def by_feature(v):
        return v.reshape(-1, KB, P).transpose(2, 0, 1).reshape(P, -1)

    qk = a["a_qk_norm"][0]
    given = {
        "x": a["x"][0],
        "pos": a["positions"][0].reshape(16, 4, 4).transpose(2, 1, 0).reshape(T, P).T,
        "const": constants()[0],
        "mask": constants()[1],
        "vec": by_feature(np.concatenate([a["ln_mix"], a["ln_ffn"], a["b_mu"][0]])),
        "rows": np.concatenate([a["b_kk"], a["b_ka"], a["b_rk"], a["b_lnx"][0]]),
        "qk_rows": qk[:, :, :ROT].reshape(6, ROT),
        "qk_cols": qk.reshape(6, HEAD).T,
        "wqkv": a["a_wqkv"][0], "awo": a["a_wo"][0], "wrkv": a["b_wrkv"][0], "w0": a["b_w0"][0], "w1": a["b_w1"][0],
        "w2": a["b_w2"][0], "a0": a["b_a0"][0], "a1": a["b_a1"][0], "a2": a["b_a2"][0], "g1": a["b_g1"][0],
        "g2": a["b_g2"][0], "bwo": a["b_wo"][0], "fw13": a["f_w13"][0], "fw2": a["f_w2"][0],
        "router": a["m_router"][0], "mw13": a["m_w13"][0], "mw2": a["m_w2"][0],
    }
    given = {n: np.ascontiguousarray(v) for n, v in given.items()}
    nc = bacc.Bacc("TRN2", target_bir_lowering=False, num_devices=1)
    args = [nc.dram_tensor(n, v.shape, mybir.dt.from_np(v.dtype), kind="ExternalInput").ap() for n, v in given.items()]
    out = nc.dram_tensor("out", (S, D), F32, kind="ExternalOutput").ap()
    build(nc, *args, out)
    r = run_bass_kernel_spmd(nc, [given], core_ids=[0])
    return r.results[0]["out"].reshape(1, S, D)
```
